# Optimizing a Trainium2 kernel written in Bass

```python
import numpy as np
import jax
import jax.numpy as jnp
from jax import lax
import jax, jax.numpy as jnp

D_MODEL = 1024
BATCH = 1
SEQ = 256
DEPTH = 2

HEAD_DIM = 64
ROT_DIM = HEAD_DIM // 4
ROPE_THETA = 500000.0
NORM_EPS = 1e-6
NEG_INF = -1e30
Q_BLOCK = 128

NSA_HEADS = 8
NSA_GROUPS = 2
NSA_HPG = NSA_HEADS // NSA_GROUPS
CMP_LEN = 32
CMP_STRIDE = 16
CMP_HIDDEN = 256
SLC_LEN = 64
SLC_TOPN = 8
WINDOW = 256
SB_HEADS = 8
GLA_HEADS = 4
GLA_DK = 64
GLA_DV = 128
GLA_RANK = 16
GLA_TAU = 16.0
GLA_CHUNK = 64
FOX_HEADS = 8

BRANCH_WIDTH = 512
N_BRANCH = 4
D_FF = 4 * D_MODEL

NSA_QW = NSA_HEADS * HEAD_DIM
NSA_KVW = NSA_GROUPS * HEAD_DIM
SB_W = SB_HEADS * HEAD_DIM
FOX_W = FOX_HEADS * HEAD_DIM
SPLITS = (NSA_QW, NSA_KVW, NSA_KVW, NSA_KVW, NSA_KVW, NSA_KVW, NSA_KVW, NSA_HEADS * 3,
          SB_W, SB_W, SB_W,
          GLA_HEADS * GLA_DK, GLA_HEADS * GLA_DK, GLA_HEADS * GLA_DV, GLA_RANK, GLA_HEADS * GLA_DV,
          FOX_W, FOX_W, FOX_W, FOX_HEADS,
          N_BRANCH * D_MODEL)
D_IN = sum(SPLITS)


def rms_norm(x, g):
    xf = x.astype(jnp.float32)
    xf = xf * lax.rsqrt(jnp.mean(xf * xf, axis=-1, keepdims=True) + NORM_EPS)
    return (xf * g.astype(jnp.float32)).astype(x.dtype)

def masked_softmax(logits, mask):
    logits = jnp.where(mask, logits.astype(jnp.float32), NEG_INF)
    return jax.nn.softmax(logits, axis=-1) * mask

def rope_partial(x, pos):
    half = ROT_DIM // 2
    inv = ROPE_THETA ** (-jnp.arange(0, ROT_DIM, 2, dtype=jnp.float32) / ROT_DIM)
    ang = pos.astype(jnp.float32)[..., None] * inv
    ang = ang.reshape(ang.shape[:2] + (1,) * (x.ndim - 3) + (half,))
    cos = jnp.cos(ang).astype(x.dtype)
    sin = jnp.sin(ang).astype(x.dtype)
    x1, x2, xp = x[..., :half], x[..., half:ROT_DIM], x[..., ROT_DIM:]
    return jnp.concatenate([x1 * cos - x2 * sin, x2 * cos + x1 * sin, xp], axis=-1)

def nsa_mixer(q, k_cmp, v_cmp, k_slc, v_slc, k_win, v_win, gate_logits, pos,
              cmp_pos_k, cmp_pos_v, cmp_wk1, cmp_wk2, cmp_wv1, cmp_wv2):
    B, S = q.shape[:2]
    G, HPG, D = NSA_GROUPS, NSA_HPG, HEAD_DIM
    scale = D ** -0.5
    q = rope_partial(q.reshape(B, S, G, HPG, D), pos)
    k_cmp, v_cmp, k_slc, v_slc, k_win, v_win = [t.reshape(B, S, G, D) for t in (k_cmp, v_cmp, k_slc, v_slc, k_win, v_win)]
    k_slc = rope_partial(k_slc, pos)
    k_win = rope_partial(k_win, pos)
    tok = np.arange(S)

    n_cmp = (S - CMP_LEN) // CMP_STRIDE + 1
    cmp_start = np.arange(n_cmp) * CMP_STRIDE
    cmp_end = cmp_start + CMP_LEN - 1
    cmp_idx = cmp_start[:, None] + np.arange(CMP_LEN)[None, :]

    def compress(t, pe, w1, w2):
        blk = t[:, cmp_idx] + pe[:, None, :]
        blk = jnp.moveaxis(blk, 3, 2).reshape(B, n_cmp, G, CMP_LEN * D)
        return jax.nn.gelu(blk @ w1) @ w2

    kc = rope_partial(compress(k_cmp, cmp_pos_k, cmp_wk1, cmp_wk2), pos[:, cmp_end])
    vc = compress(v_cmp, cmp_pos_v, cmp_wv1, cmp_wv2)
    s_cmp = jnp.einsum('bsghd,bcgd->bghsc', q, kc) * scale
    p_cmp = masked_softmax(s_cmp, cmp_end[None, :] <= tok[:, None])
    o_cmp = jnp.einsum('bghsc,bcgd->bsghd', p_cmp.astype(vc.dtype), vc)

    n_sel = S // SLC_LEN
    top_n = min(SLC_TOPN, n_sel)
    sel_start = np.arange(n_sel) * SLC_LEN
    overlap = np.clip(np.minimum(cmp_start[:, None] + CMP_LEN, sel_start[None, :] + SLC_LEN)
                      - np.maximum(cmp_start[:, None], sel_start[None, :]), 0, None) / CMP_LEN
    imp = jnp.einsum('bghsc,cj->bgsj', p_cmp, jnp.asarray(overlap, jnp.float32))
    forced = (sel_start[None, :] == 0) | (np.arange(n_sel)[None, :] == (tok // SLC_LEN)[:, None])
    imp = jnp.where(forced, jnp.inf, jnp.where(sel_start[None, :] <= tok[:, None], imp, -jnp.inf))
    _, sel = lax.top_k(imp, top_n)
    n_qb = S // Q_BLOCK

    def to_blocks(t):
        return jnp.moveaxis(t.reshape(B, n_sel, SLC_LEN, G, D), 3, 1).reshape(B, G, n_sel, SLC_LEN * D)

    ks_blk = to_blocks(k_slc)
    vs_blk = to_blocks(v_slc)
    q_blk = jnp.moveaxis(q.reshape(B, n_qb, Q_BLOCK, G, HPG, D), 1, 0)
    sel_blk = jnp.moveaxis(sel.reshape(B, G, n_qb, Q_BLOCK, top_n), 2, 0)

    def select_block(args):
        qc, ic, t_start = args
        flat = ic.reshape(B, G, Q_BLOCK * top_n, 1)
        kg = jnp.take_along_axis(ks_blk, flat, axis=2).reshape(B, G, Q_BLOCK, top_n * SLC_LEN, D)
        vg = jnp.take_along_axis(vs_blk, flat, axis=2).reshape(B, G, Q_BLOCK, top_n * SLC_LEN, D)
        key_tok = (ic[..., None] * SLC_LEN + jnp.arange(SLC_LEN)).reshape(B, G, Q_BLOCK, top_n * SLC_LEN)
        t = t_start + jnp.arange(Q_BLOCK)
        s = jnp.einsum('bqghd,bgqkd->bghqk', qc, kg) * scale
        p = masked_softmax(s, (key_tok <= t[:, None])[:, :, None])
        return jnp.einsum('bghqk,bgqkd->bqghd', p.astype(vg.dtype), vg)

    o_slc = lax.map(select_block, (q_blk, sel_blk, jnp.arange(n_qb) * Q_BLOCK))
    o_slc = jnp.moveaxis(o_slc, 0, 1).reshape(B, S, G, HPG, D)

    n_band = Q_BLOCK + WINDOW
    band_idx = np.arange(n_qb)[:, None] * Q_BLOCK + np.arange(n_band)[None, :]
    band_tok = band_idx - WINDOW
    pad = ((0, 0), (WINDOW, 0), (0, 0), (0, 0))
    kb = jnp.pad(k_win, pad)[:, band_idx]
    vb = jnp.pad(v_win, pad)[:, band_idx]
    tq = tok.reshape(n_qb, Q_BLOCK)
    win_mask = ((band_tok[:, None, :] <= tq[:, :, None]) & (band_tok[:, None, :] > tq[:, :, None] - WINDOW)
                & (band_tok[:, None, :] >= 0))
    s_win = jnp.einsum('bnqghd,bnkgd->bnghqk', q.reshape(B, n_qb, Q_BLOCK, G, HPG, D), kb) * scale
    p_win = masked_softmax(s_win, win_mask[None, :, None, None])
    o_win = jnp.einsum('bnghqk,bnkgd->bnqghd', p_win.astype(vb.dtype), vb).reshape(B, S, G, HPG, D)

    g = jax.nn.sigmoid(gate_logits.astype(jnp.float32)).reshape(B, S, G, HPG, 3).astype(q.dtype)
    o = g[..., 0:1] * o_cmp + g[..., 1:2] * o_slc + g[..., 2:3] * o_win
    return o.reshape(B, S, NSA_HEADS * D)

def stick_breaking_mixer(q, k, v):
    B, S = q.shape[:2]
    H, D = SB_HEADS, HEAD_DIM
    scale = D ** -0.5
    n_qb = S // Q_BLOCK
    kT = jnp.moveaxis(k.reshape(B, S, H, D), 1, 2)
    vT = jnp.moveaxis(v.reshape(B, S, H, D), 1, 2)
    qb = q.reshape(B, n_qb, Q_BLOCK, H, D).transpose(1, 0, 3, 2, 4)
    key_pos = jnp.arange(S)

    def block(args):
        qc, t_start = args
        z = jnp.einsum('bhqd,bhkd->bhqk', qc, kT).astype(jnp.float32) * scale
        t = t_start + jnp.arange(Q_BLOCK)
        valid = key_pos[None, :] < t[:, None]
        sp = jnp.where(valid, jax.nn.softplus(z), 0.0)
        later = lax.cumsum(sp, axis=3, reverse=True) - sp
        a = jnp.where(valid, jnp.exp(jax.nn.log_sigmoid(z) - later), 0.0)
        return jnp.einsum('bhqk,bhkd->bhqd', a.astype(vT.dtype), vT)

    o = lax.map(block, (qb, jnp.arange(n_qb) * Q_BLOCK))
    return o.transpose(1, 0, 3, 2, 4).reshape(B, S, H * D)

def gla_mixer(q, k, v, a_lr, gate, w_alpha, b_alpha, norm_g):
    B, S = q.shape[:2]
    H, DK, DV, C = GLA_HEADS, GLA_DK, GLA_DV, GLA_CHUNK
    n_ch = S // C
    log_a = jax.nn.log_sigmoid((a_lr @ w_alpha + b_alpha).astype(jnp.float32)) / GLA_TAU

    def chunks(t, f):
        return t.reshape(B, n_ch, C, H, f).transpose(1, 0, 3, 2, 4)

    qc_all = chunks(q * DK ** -0.5, DK)
    kc_all = chunks(k, DK)
    vc_all = chunks(v, DV)
    la_all = chunks(log_a, DK)
    causal = np.tril(np.ones((C, C), dtype=bool))

    def step(state, inp):
        qc, kc, vc, lac = inp
        b = jnp.cumsum(lac, axis=2)
        o_inter = jnp.einsum('bhtk,bhkv->bhtv', qc * jnp.exp(b), state)
        diff = jnp.where(causal[:, :, None], b[:, :, :, None, :] - b[:, :, None, :, :], -jnp.inf)
        att = jnp.einsum('bhtk,bhsk,bhtsk->bhts', qc, kc, jnp.exp(diff))
        o_intra = jnp.einsum('bhts,bhsv->bhtv', att, vc)
        b_last = b[:, :, -1:, :]
        state = (jnp.exp(b_last[:, :, 0])[..., None] * state
                 + jnp.einsum('bhsk,bhsv->bhkv', kc * jnp.exp(b_last - b), vc))
        return state, o_inter + o_intra

    state0 = jnp.zeros((B, H, DK, DV), jnp.float32)
    _, o = lax.scan(step, state0, (qc_all, kc_all, vc_all, la_all))
    o = o.transpose(1, 0, 3, 2, 4).reshape(B, S, H, DV)
    o = o * lax.rsqrt(jnp.mean(o * o, axis=-1, keepdims=True) + NORM_EPS) * norm_g.astype(jnp.float32)
    y = o.astype(v.dtype) * jax.nn.silu(gate).reshape(B, S, H, DV)
    return y.reshape(B, S, H * DV)

def forgetting_mixer(q, k, v, f_logit, b_f):
    B, S = q.shape[:2]
    H, D = FOX_HEADS, HEAD_DIM
    scale = D ** -0.5
    n_qb = S // Q_BLOCK
    log_f = jax.nn.log_sigmoid(f_logit.astype(jnp.float32) + b_f.astype(jnp.float32))
    cumT = jnp.moveaxis(jnp.cumsum(log_f, axis=1), 1, 2)
    kT = jnp.moveaxis(k.reshape(B, S, H, D), 1, 2)
    vT = jnp.moveaxis(v.reshape(B, S, H, D), 1, 2)
    qb = q.reshape(B, n_qb, Q_BLOCK, H, D).transpose(1, 0, 3, 2, 4)
    cb = cumT.reshape(B, H, n_qb, Q_BLOCK).transpose(2, 0, 1, 3)
    key_pos = jnp.arange(S)

    def block(args):
        qc, ct, t_start = args
        s = jnp.einsum('bhqd,bhkd->bhqk', qc, kT).astype(jnp.float32) * scale
        s = s + ct[..., None] - cumT[:, :, None, :]
        t = t_start + jnp.arange(Q_BLOCK)
        p = masked_softmax(s, key_pos[None, :] <= t[:, None])
        return jnp.einsum('bhqk,bhkd->bhqd', p.astype(vT.dtype), vT)

    o = lax.map(block, (qb, cb, jnp.arange(n_qb) * Q_BLOCK))
    return o.transpose(1, 0, 3, 2, 4).reshape(B, S, H * D)

def hybrid_layer(x, positions, norm_mix, w_in, b_gate, cmp_pos_k, cmp_pos_v, cmp_wk1, cmp_wk2,
                 cmp_wv1, cmp_wv2, gla_w_alpha, gla_b_alpha, gla_norm, fox_b_f, w_branch, w_out,
                 norm_ff, w_ff1, w_ff2):
    B, S, _ = x.shape
    h = rms_norm(x, norm_mix)
    proj = h @ w_in
    offsets = np.cumsum(SPLITS)[:-1].tolist()
    (nsa_q, nsa_kc, nsa_vc, nsa_ks, nsa_vs, nsa_kw, nsa_vw, nsa_g,
     sb_q, sb_k, sb_v,
     gla_q, gla_k, gla_v, gla_a, gla_g,
     fox_q, fox_k, fox_v, fox_f,
     gate_logits) = jnp.split(proj, offsets, axis=-1)

    y_nsa = nsa_mixer(nsa_q, nsa_kc, nsa_vc, nsa_ks, nsa_vs, nsa_kw, nsa_vw, nsa_g, positions,
                      cmp_pos_k, cmp_pos_v, cmp_wk1, cmp_wk2, cmp_wv1, cmp_wv2)
    y_sb = stick_breaking_mixer(sb_q, sb_k, sb_v)
    y_gla = gla_mixer(gla_q.reshape(B, S, GLA_HEADS, GLA_DK), gla_k.reshape(B, S, GLA_HEADS, GLA_DK),
                      gla_v.reshape(B, S, GLA_HEADS, GLA_DV), gla_a, gla_g, gla_w_alpha, gla_b_alpha, gla_norm)
    y_fox = forgetting_mixer(fox_q, fox_k, fox_v, fox_f, fox_b_f)

    ys = jnp.stack([y_nsa, y_sb, y_gla, y_fox], axis=2)
    branch = jnp.einsum('bsnc,ncd->bsnd', ys, w_branch)
    gates = jax.nn.sigmoid((gate_logits + b_gate).astype(jnp.float32)).astype(x.dtype)
    mixed = jnp.sum(gates.reshape(B, S, N_BRANCH, D_MODEL) * branch, axis=2)
    x = x + mixed @ w_out
    h2 = rms_norm(x, norm_ff)
    return x + jnp.square(jax.nn.relu(h2 @ w_ff1)) @ w_ff2

def first_inputs(seed: int = 0) -> dict:
    key = jax.random.key(seed)
    ks = jax.random.split(key, 21)
    L = DEPTH

    def nrm(k, shape, scale):
        return jax.random.normal(k, shape, jnp.float32) * scale

    x = nrm(ks[0], (BATCH, SEQ, D_MODEL), 1.0)
    offset = jax.random.randint(ks[1], (BATCH, 1), 0, 4096, dtype=jnp.int32)
    positions = jnp.arange(SEQ, dtype=jnp.int32)[None, :] + offset
    return {
        'x': x,
        'positions': positions,
        'norm_mix': 1.0 + nrm(ks[2], (L, D_MODEL), 0.02),
        'w_in': nrm(ks[3], (L, D_MODEL, D_IN), D_MODEL ** -0.5),
        'b_gate': nrm(ks[4], (L, N_BRANCH * D_MODEL), 0.02),
        'nsa_cmp_pos_k': nrm(ks[5], (L, CMP_LEN, HEAD_DIM), 0.1),
        'nsa_cmp_pos_v': nrm(ks[6], (L, CMP_LEN, HEAD_DIM), 0.1),
        'nsa_cmp_wk1': nrm(ks[7], (L, CMP_LEN * HEAD_DIM, CMP_HIDDEN), (CMP_LEN * HEAD_DIM) ** -0.5),
        'nsa_cmp_wk2': nrm(ks[8], (L, CMP_HIDDEN, HEAD_DIM), CMP_HIDDEN ** -0.5),
        'nsa_cmp_wv1': nrm(ks[9], (L, CMP_LEN * HEAD_DIM, CMP_HIDDEN), (CMP_LEN * HEAD_DIM) ** -0.5),
        'nsa_cmp_wv2': nrm(ks[10], (L, CMP_HIDDEN, HEAD_DIM), CMP_HIDDEN ** -0.5),
        'gla_w_alpha': nrm(ks[11], (L, GLA_RANK, GLA_HEADS * GLA_DK), GLA_RANK ** -0.5),
        'gla_b_alpha': nrm(ks[12], (L, GLA_HEADS * GLA_DK), 0.1),
        'gla_norm': 1.0 + nrm(ks[13], (L, GLA_DV), 0.02),
        'fox_b_f': 2.0 + nrm(ks[14], (L, FOX_HEADS), 0.1),
        'w_branch': nrm(ks[15], (L, N_BRANCH, BRANCH_WIDTH, D_MODEL), BRANCH_WIDTH ** -0.5),
        'w_out': nrm(ks[16], (L, D_MODEL, D_MODEL), D_MODEL ** -0.5),
        'norm_ff': 1.0 + nrm(ks[17], (L, D_MODEL), 0.02),
        'w_ff1': nrm(ks[18], (L, D_MODEL, D_FF), D_MODEL ** -0.5),
        'w_ff2': nrm(ks[19], (L, D_FF, D_MODEL), D_FF ** -0.5),
        'norm_final': 1.0 + nrm(ks[20], (D_MODEL,), 0.02),
    }

def first_block(x, positions, norm_mix, w_in, b_gate, nsa_cmp_pos_k, nsa_cmp_pos_v, nsa_cmp_wk1,
              nsa_cmp_wk2, nsa_cmp_wv1, nsa_cmp_wv2, gla_w_alpha, gla_b_alpha, gla_norm, fox_b_f,
              w_branch, w_out, norm_ff, w_ff1, w_ff2, norm_final):
    for l in range(DEPTH):
        x = hybrid_layer(x, positions, norm_mix[l], w_in[l], b_gate[l], nsa_cmp_pos_k[l], nsa_cmp_pos_v[l],
                         nsa_cmp_wk1[l], nsa_cmp_wk2[l], nsa_cmp_wv1[l], nsa_cmp_wv2[l], gla_w_alpha[l],
                         gla_b_alpha[l], gla_norm[l], fox_b_f[l], w_branch[l], w_out[l], norm_ff[l],
                         w_ff1[l], w_ff2[l])
    return rms_norm(x, norm_final)


GRID_W = 64
CTX_LEN = 256
N_MIXERS = 2
GQA_HEADS = 16
GQA_KV_HEADS = 4
GQA_GROUP = GQA_HEADS // GQA_KV_HEADS
GQA_HEAD_DIM = D_MODEL // GQA_HEADS
MLA_HEADS = 16
MLA_Q_RANK = (3 * D_MODEL) // 8
MLA_KV_RANK = D_MODEL // 4
MLA_NOPE_DIM = 64
MLA_ROPE_DIM = 32
MLA_V_DIM = 64
FFN_HIDDEN = 4 * D_MODEL
ROPE_THETA_2 = 10000.0
DEEPNORM_ALPHA = (2.0 * DEPTH) ** 0.25
DEEPNORM_BETA = (8.0 * DEPTH) ** -0.25


def layer_norm(x, g, b):
    xf = x.astype(jnp.float32)
    mu = jnp.mean(xf, axis=-1, keepdims=True)
    var = jnp.mean(jnp.square(xf - mu), axis=-1, keepdims=True)
    return ((xf - mu) * lax.rsqrt(var + NORM_EPS) * g.astype(jnp.float32) + b.astype(jnp.float32)).astype(x.dtype)

def rms_norm_2(x, g):
    xf = x.astype(jnp.float32)
    ms = jnp.mean(jnp.square(xf), axis=-1, keepdims=True)
    return (xf * lax.rsqrt(ms + NORM_EPS) * g.astype(jnp.float32)).astype(x.dtype)

def grid_rope_tables(n_tok, rot_dim):
    rows = n_tok // GRID_W
    row = jnp.broadcast_to(jnp.arange(rows, dtype=jnp.float32)[:, None], (rows, GRID_W)).reshape(-1)
    col = jnp.broadcast_to(jnp.arange(GRID_W, dtype=jnp.float32)[None, :], (rows, GRID_W)).reshape(-1)
    axis_dim = rot_dim // 2
    inv_freq = ROPE_THETA_2 ** (-jnp.arange(0, axis_dim, 2, dtype=jnp.float32) / axis_dim)
    ang_row = row[:, None] * inv_freq[None, :]
    ang_col = col[:, None] * inv_freq[None, :]
    return (jnp.cos(ang_row), jnp.sin(ang_row), jnp.cos(ang_col), jnp.sin(ang_col))

def rotate_axis(x, cos, sin):
    x1, x2 = jnp.split(x, 2, axis=-1)
    c = cos[:, None, :]
    s = sin[:, None, :]
    return jnp.concatenate([x1 * c - x2 * s, x2 * c + x1 * s], axis=-1)

def apply_grid_rope(x, tables):
    cr, sr, cc, sc = tables
    half = x.shape[-1] // 2
    xf = x.astype(jnp.float32)
    out = jnp.concatenate([rotate_axis(xf[..., :half], cr, sr), rotate_axis(xf[..., half:], cc, sc)], axis=-1)
    return out.astype(x.dtype)

def block_attention(q, k, v):
    b, sq, kvh, g, dk = q.shape
    nb = sq // Q_BLOCK
    scale = dk ** -0.5
    qb = jnp.moveaxis(q.reshape(b, nb, Q_BLOCK, kvh, g, dk), 1, 0)

    def one_block(qi):
        s = jnp.einsum('bqhgd,bkhd->bhgqk', qi, k, preferred_element_type=jnp.float32) * scale
        p = jax.nn.softmax(s, axis=-1).astype(v.dtype)
        return jnp.einsum('bhgqk,bkhe->bqhge', p, v)

    o = lax.map(one_block, qb)
    return jnp.moveaxis(o, 0, 1).reshape(b, sq, kvh * g * v.shape[-1])

def gqa_mixer(h_lat, h_ctx, w_qkv, q_norm, k_norm, w_o, rope, need_ctx):
    def project(h, rotate):
        b, n, _ = h.shape
        q, k, v = jnp.split(h @ w_qkv, [GQA_HEADS * GQA_HEAD_DIM, (GQA_HEADS + GQA_KV_HEADS) * GQA_HEAD_DIM], axis=-1)
        q = rms_norm_2(q.reshape(b, n, GQA_HEADS, GQA_HEAD_DIM), q_norm)
        k = rms_norm_2(k.reshape(b, n, GQA_KV_HEADS, GQA_HEAD_DIM), k_norm)
        v = v.reshape(b, n, GQA_KV_HEADS, GQA_HEAD_DIM)
        if rotate:
            q = apply_grid_rope(q, rope)
            k = apply_grid_rope(k, rope)
        return q.reshape(b, n, GQA_KV_HEADS, GQA_GROUP, GQA_HEAD_DIM), k, v

    q_lat, k_lat, v_lat = project(h_lat, True)
    q_ctx, k_ctx, v_ctx = project(h_ctx, False)
    k_all = jnp.concatenate([k_ctx, k_lat], axis=1)
    v_all = jnp.concatenate([v_ctx, v_lat], axis=1)
    y_lat = block_attention(q_lat, k_all, v_all) @ w_o
    y_ctx = block_attention(q_ctx, k_ctx, v_ctx) @ w_o if need_ctx else None
    return y_lat, y_ctx

def mla_mixer(h_lat, h_ctx, w_in, q_norm, kv_norm, w_uq, w_ukv, w_o, rope, need_ctx):
    def project(h, rotate):
        b, n, _ = h.shape
        cq, ckv, k_pe = jnp.split(h @ w_in, [MLA_Q_RANK, MLA_Q_RANK + MLA_KV_RANK], axis=-1)
        q = (rms_norm_2(cq, q_norm) @ w_uq).reshape(b, n, MLA_HEADS, MLA_NOPE_DIM + MLA_ROPE_DIM)
        q_nope, q_pe = jnp.split(q, [MLA_NOPE_DIM], axis=-1)
        kv = (rms_norm_2(ckv, kv_norm) @ w_ukv).reshape(b, n, MLA_HEADS, MLA_NOPE_DIM + MLA_V_DIM)
        k_nope, v = jnp.split(kv, [MLA_NOPE_DIM], axis=-1)
        k_pe = k_pe[:, :, None, :]
        if rotate:
            q_pe = apply_grid_rope(q_pe, rope)
            k_pe = apply_grid_rope(k_pe, rope)
        q = jnp.concatenate([q_nope, q_pe], axis=-1)[:, :, :, None, :]
        k = jnp.concatenate([k_nope, jnp.broadcast_to(k_pe, (b, n, MLA_HEADS, MLA_ROPE_DIM))], axis=-1)
        return q, k, v

    q_lat, k_lat, v_lat = project(h_lat, True)
    q_ctx, k_ctx, v_ctx = project(h_ctx, False)
    k_all = jnp.concatenate([k_ctx, k_lat], axis=1)
    v_all = jnp.concatenate([v_ctx, v_lat], axis=1)
    y_lat = block_attention(q_lat, k_all, v_all) @ w_o
    y_ctx = block_attention(q_ctx, k_ctx, v_ctx) @ w_o if need_ctx else None
    return y_lat, y_ctx

def sq_relu_mlp(h, w1, w2):
    return jnp.square(jax.nn.relu(h @ w1)) @ w2

def second_inputs(seed: int = 0) -> dict:
    key = jax.random.key(seed)
    ks = jax.random.split(key, 20)
    d = D_MODEL
    n_a = (DEPTH + N_MIXERS - 1) // N_MIXERS
    n_b = DEPTH // N_MIXERS

    def w(k, shape, fan_in, gain=1.0):
        return jax.random.normal(k, shape, jnp.float32) * (gain * fan_in ** -0.5)

    def gain_vec(k, shape):
        return 1.0 + 0.02 * jax.random.normal(k, shape, jnp.float32)

    qkv_cols = (GQA_HEADS + 2 * GQA_KV_HEADS) * GQA_HEAD_DIM
    mla_in_cols = MLA_Q_RANK + MLA_KV_RANK + MLA_ROPE_DIM
    return {
        "x": jax.random.normal(ks[0], (BATCH, SEQ, d), jnp.float32),
        "c": jax.random.normal(ks[1], (BATCH, d), jnp.float32),
        "ctx": jax.random.normal(ks[2], (BATCH, CTX_LEN, d), jnp.float32),
        "c_ctx": jax.random.normal(ks[3], (d,), jnp.float32),
        "w_ada": w(ks[4], (DEPTH, d, 6 * d), d),
        "b_ada": 0.02 * jax.random.normal(ks[5], (DEPTH, 6 * d), jnp.float32),
        "ln_g": gain_vec(ks[6], (DEPTH, 2, d)),
        "ln_b": 0.02 * jax.random.normal(ks[7], (DEPTH, 2, d), jnp.float32),
        "mlp_w1": w(ks[8], (DEPTH, d, FFN_HIDDEN), d),
        "mlp_w2": w(ks[9], (DEPTH, FFN_HIDDEN, d), FFN_HIDDEN, DEEPNORM_BETA),
        "gqa_w_qkv": w(ks[10], (n_a, d, qkv_cols), d),
        "gqa_q_norm": gain_vec(ks[11], (n_a, GQA_HEAD_DIM)),
        "gqa_k_norm": gain_vec(ks[12], (n_a, GQA_HEAD_DIM)),
        "gqa_w_o": w(ks[13], (n_a, GQA_HEADS * GQA_HEAD_DIM, d), GQA_HEADS * GQA_HEAD_DIM, DEEPNORM_BETA),
        "mla_w_in": w(ks[14], (n_b, d, mla_in_cols), d),
        "mla_q_norm": gain_vec(ks[15], (n_b, MLA_Q_RANK)),
        "mla_kv_norm": gain_vec(ks[16], (n_b, MLA_KV_RANK)),
        "mla_w_uq": w(ks[17], (n_b, MLA_Q_RANK, MLA_HEADS * (MLA_NOPE_DIM + MLA_ROPE_DIM)), MLA_Q_RANK),
        "mla_w_ukv": w(ks[18], (n_b, MLA_KV_RANK, MLA_HEADS * (MLA_NOPE_DIM + MLA_V_DIM)), MLA_KV_RANK),
        "mla_w_o": w(ks[19], (n_b, MLA_HEADS * MLA_V_DIM, d), MLA_HEADS * MLA_V_DIM, DEEPNORM_BETA),
    }

def second_block(x, c, ctx, c_ctx, w_ada, b_ada, ln_g, ln_b, mlp_w1, mlp_w2,
              gqa_w_qkv, gqa_q_norm, gqa_k_norm, gqa_w_o,
              mla_w_in, mla_q_norm, mla_kv_norm, mla_w_uq, mla_w_ukv, mla_w_o):
    n_tok = x.shape[1]
    rope_gqa = grid_rope_tables(n_tok, GQA_HEAD_DIM)
    rope_mla = grid_rope_tables(n_tok, MLA_ROPE_DIM)
    alpha = DEEPNORM_ALPHA
    silu_c = jax.nn.silu(c)
    silu_cc = jax.nn.silu(c_ctx)
    xc = ctx
    for i in range(DEPTH):
        need_ctx = i < DEPTH - 1
        mod_lat = (silu_c @ w_ada[i] + b_ada[i])[:, None, :]
        mod_ctx = silu_cc @ w_ada[i] + b_ada[i]
        sh_a, sc_a, g_a, sh_m, sc_m, g_m = jnp.split(mod_lat, 6, axis=-1)
        csh_a, csc_a, cg_a, csh_m, csc_m, cg_m = jnp.split(mod_ctx, 6, axis=-1)

        h_lat = x * (1.0 + sc_a) + sh_a
        h_ctx = xc * (1.0 + csc_a) + csh_a
        j = i // N_MIXERS
        if i % N_MIXERS == 0:
            y_lat, y_ctx = gqa_mixer(h_lat, h_ctx, gqa_w_qkv[j], gqa_q_norm[j], gqa_k_norm[j],
                                     gqa_w_o[j], rope_gqa, need_ctx)
        else:
            y_lat, y_ctx = mla_mixer(h_lat, h_ctx, mla_w_in[j], mla_q_norm[j], mla_kv_norm[j],
                                     mla_w_uq[j], mla_w_ukv[j], mla_w_o[j], rope_mla, need_ctx)

        x = layer_norm(alpha * x + g_a * y_lat, ln_g[i, 0], ln_b[i, 0])
        x = layer_norm(alpha * x + g_m * sq_relu_mlp(x * (1.0 + sc_m) + sh_m, mlp_w1[i], mlp_w2[i]),
                       ln_g[i, 1], ln_b[i, 1])
        if need_ctx:
            xc = layer_norm(alpha * xc + cg_a * y_ctx, ln_g[i, 0], ln_b[i, 0])
            xc = layer_norm(alpha * xc + cg_m * sq_relu_mlp(xc * (1.0 + csc_m) + csh_m, mlp_w1[i], mlp_w2[i]),
                            ln_g[i, 1], ln_b[i, 1])
    return x


def setup_inputs(seed=0):
    out = dict(first_inputs(seed))
    for name, value in second_inputs(seed + 1).items():
        if name != "x":
            out[name + "_2"] = value
    return out


def reference(
    x, positions, norm_mix, w_in, b_gate, nsa_cmp_pos_k, nsa_cmp_pos_v, nsa_cmp_wk1,
    nsa_cmp_wk2, nsa_cmp_wv1, nsa_cmp_wv2, gla_w_alpha, gla_b_alpha, gla_norm, fox_b_f,
    w_branch, w_out, norm_ff, w_ff1, w_ff2, norm_final, c_2, ctx_2, c_ctx_2, w_ada_2, b_ada_2,
    ln_g_2, ln_b_2, mlp_w1_2, mlp_w2_2, gqa_w_qkv_2, gqa_q_norm_2, gqa_k_norm_2, gqa_w_o_2,
    mla_w_in_2, mla_q_norm_2, mla_kv_norm_2, mla_w_uq_2, mla_w_ukv_2, mla_w_o_2,
):
    x = first_block(
        x, positions, norm_mix, w_in, b_gate, nsa_cmp_pos_k, nsa_cmp_pos_v, nsa_cmp_wk1,
        nsa_cmp_wk2, nsa_cmp_wv1, nsa_cmp_wv2, gla_w_alpha, gla_b_alpha, gla_norm, fox_b_f,
        w_branch, w_out, norm_ff, w_ff1, w_ff2, norm_final,
    )
    return second_block(
        x, c_2, ctx_2, c_ctx_2, w_ada_2, b_ada_2, ln_g_2, ln_b_2, mlp_w1_2, mlp_w2_2,
        gqa_w_qkv_2, gqa_q_norm_2, gqa_k_norm_2, gqa_w_o_2, mla_w_in_2, mla_q_norm_2,
        mla_kv_norm_2, mla_w_uq_2, mla_w_ukv_2, mla_w_o_2,
    )


_drawn_inputs = setup_inputs


def setup_inputs(seed=0):
    import zlib

    import numpy as np

    out = dict(_drawn_inputs(seed))
    spreads = {}
    factors = {'b_gate': 8.0,
     'nsa_cmp_pos_k': 8.0,
     'nsa_cmp_pos_v': 2.741,
     'gla_b_alpha': 3.336,
     'gla_norm': 6.631,
     'fox_b_f': 2.712,
     'norm_final': 2.959,
     'ctx_2': 3.538,
     'gqa_q_norm_2': 8.0,
     'gqa_k_norm_2': 8.0,
     'mla_q_norm_2': 8.0,
     'mla_kv_norm_2': 8.0}
    for name, (base, spread) in spreads.items():
        noise = np.random.default_rng([zlib.crc32(name.encode()), seed]).standard_normal(out[name].shape)
        drawn = base * np.exp(spread * noise) if base else spread * noise
        out[name] = jnp.asarray(drawn.astype(out[name].dtype))
    for name, factor in factors.items():
        out[name] = (out[name] * factor).astype(out[name].dtype)
    return out
```

```python
from contextlib import ExitStack

import numpy as np

import concourse.bass as bass
from concourse import mybir

F32, BF16, I32, U16 = mybir.dt.float32, mybir.dt.bfloat16, mybir.dt.int32, mybir.dt.uint16
ACT = mybir.ActivationFunctionType
ALU = mybir.AluOpType
AX = mybir.AxisListType

P = 128
D, S, DEPTH = 1024, 256, 2
KD = D // P
TT = S // P
HD = 64
HALF_HEADS = 4
N_CMP, CMP_LEN, CMP_STRIDE, CMP_HID = 15, 32, 16, 256
N_GATE = 24
GLA_H, GLA_DV, GLA_RANK, GLA_TAU = 4, 128, 16, 16.0
FFK = 4 * D // P
EPS = 1e-6
NEG = -1e30
GELU_C = 0.7978845608028654
ROT_HALF, ROPE_THETA = 8, 500000.0
GRID_W, GRID_THETA = 64, 10000.0
HEADS, KV_HEADS = 16, 4
Q_RANK, KV_RANK, PE_DIM = 384, 256, 32
MLA_QK = HD + PE_DIM
ALPHA = (2.0 * DEPTH) ** 0.25
MOD_PARTS = 6
MODC = MOD_PARTS * KD

ROW_ADA, ROW_QN, ROW_KN, ROW_MQN, ROW_MKN, ROW_C, N_ROWS2 = 0, 96, 97, 98, 101, 103, 119

Q0, KC0, KS0 = 0, 512, 768
SBQ0, SBK0, SBV0 = 1304, 1816, 2328
GLQ0, GLV0, GLA0, GLG0 = 2840, 3352, 3864, 3880
FXQ0, FXK0, FXV0, GATE0 = 4392, 4904, 5416, 5936

ROW_MIX, ROW_FF, ROW_GATE, ROW_GLB, ROW_GLN, ROW_PEK, ROW_PEV, N_ROWS = 0, 8, 16, 48, 50, 51, 67, 83

LEVELS = [128, 0, 64, 32, 16, 8, 4, 2, 1]
SLOT = 528 * KD
N_SLOTS = 4
MAGIC = 1.5 * 2.0 ** 23
TWO_PI_PARTS = (6.28125, 0.0019340515136718750, 1.2556659146019e-06)


def constants():
    i = np.arange(P)
    row, col = i[:, None], i[None, :]
    rot = np.zeros((P, P), np.float32)
    for half in (0, HD):
        for d in range(ROT_HALF):
            rot[half + ROT_HALF + d, half + d] = -1.0
            rot[half + d, half + ROT_HALF + d] = 1.0
    levels = [(row == col)]
    for h in LEVELS[2:]:
        s, t = row, col
        levels.append((s // (2 * h) == t // (2 * h)) & (s % (2 * h) < h) & (t % (2 * h) >= h))
    inv = (ROPE_THETA ** (-np.arange(0, 2 * ROT_HALF, 2) / (2 * ROT_HALF))).astype(np.float32)
    inv_col = np.zeros((P, 1), np.float32)
    for half in (0, HD):
        for d in range(2 * ROT_HALF):
            inv_col[half + d, 0] = inv[d % ROT_HALF]
    end = np.arange(N_CMP) * CMP_STRIDE + CMP_LEN - 1
    seen = np.stack([end[None, :] <= (tt * P + i)[:, None] for tt in range(TT)], 1).reshape(P, -1)
    f32 = {
        "ident": np.eye(P),
        "neg_from": -1.0 * (row >= col),
        "neg_upto": -1.0 * (row <= col),
        "neg_ones": -np.ones((P, P)),
        "rot": rot,
        "inv_freq": inv_col,
        "one": np.ones((P, 1)), "eps": np.full((P, 1), EPS),
        "cmp_seen": seen, "cmp_bias": np.where(seen, 0.0, NEG),
        "head_sel": np.repeat(np.eye(P)[:, :8], P, axis=1),
        "ones": np.ones((P, S)),
        "head_mean": np.kron(np.eye(2), np.ones((HD, HD))) / HD,
    }
    bf16 = {
        "ident": np.eye(P),
        "causal": np.where(col > row, NEG, 0.0),
        "strict": np.where(row >= col, NEG, 0.0),
        "levels": np.stack(levels, 1).reshape(P, -1),
    }
    return f32, bf16


def grid_tables(rot_dim, start, period):
    axis, half = rot_dim // 2, rot_dim // 4
    swap, angle = np.zeros((P, P), np.float32), np.zeros((P, S), np.float32)
    inv = (GRID_THETA ** (-np.arange(0, axis, 2, dtype=np.float32) / np.float32(axis))).astype(np.float32)
    tok = np.arange(S)
    for base in range(start, P, period):
        for a, place in enumerate((tok // GRID_W, tok % GRID_W)):
            for j in range(half):
                lo = base + a * axis + j
                hi = lo + half
                swap[hi, lo], swap[lo, hi] = -1.0, 1.0
                angle[lo] = angle[hi] = place.astype(np.float32) * inv[j]
    return np.concatenate([swap, np.cos(angle), np.sin(angle)], 1).astype(np.float32)


def packed(tables, dtype):
    at, parts, n = {}, [], 0
    for name, a in tables.items():
        at[name] = (n, a.shape[1])
        parts.append(np.asarray(a, np.float32))
        n += a.shape[1]
    return at, np.concatenate(parts, 1).astype(dtype)


class Banks:

    def __init__(self, sem, label, banks, uses):
        assert len(set(uses)) == len(uses), label
        self.order = {name: i for i, name in enumerate(uses)}
        self.banks, self.filled, self.n = banks, 0, len(banks)
        self.full = sem(label + "_full")
        self.free_sems = [sem(f"{label}_free{b}") for b in range(self.n)]

    def bank(self, name):
        return self.banks[self.order[name] % self.n]

    def claim(self, pe, name):
        i = self.order[name]
        assert i == self.filled, (name, i, self.filled)
        self.filled += 1
        if i >= self.n:
            pe.wait_ge(self.free_sems[i % self.n], i // self.n)
        return self.bank(name)

    def arrived(self, eng, name):
        eng.wait_ge(self.full, self.order[name] + 1)
        return self.bank(name)

    def taken(self, eng, *names):
        for name in names:
            i = self.order[name]
            eng.wait_ge(self.free_sems[i % self.n], i // self.n + 1)

    def free(self, name):
        return self.free_sems[self.order[name] % self.n]


class Weights:

    def __init__(self, sem, label, ring, tiles):
        self.tiles, self.ring = tiles, ring
        self.order = {tile[0]: i for i, tile in enumerate(tiles)}
        self.loaded = [sem(f"{label}_loaded{s}") for s in range(N_SLOTS)]
        count, self.ready = [0] * N_SLOTS, []
        for i, (_, _, _, sources, _) in enumerate(tiles):
            count[i % N_SLOTS] += 16 * len(sources)
            self.ready.append(count[i % N_SLOTS])

    def slot(self, i):
        _, k, n, _, _ = self.tiles[i]
        return self.ring[:, i % N_SLOTS, 0:k * n].rearrange("p (k n) -> p k n", k=k)

    def load(self, sp):
        for i, (_, _, _, sources, _) in enumerate(self.tiles):
            if i >= N_SLOTS:
                sp.wait_ge(*self.tiles[i - N_SLOTS][4])
            for part, src in sources:
                sp.dma_start(self.slot(i)[part], src).then_inc(self.loaded[i % N_SLOTS], 16)

    def arrived(self, pe, name):
        i = self.order[name]
        pe.wait_ge(self.loaded[i % N_SLOTS], self.ready[i])
        return self.slot(i)


class Chain:

    def __init__(self, eng, sem):
        self.eng, self.sem, self.n = eng, sem, 0

    def __call__(self, ins):
        self.n += 1
        ins.then_inc(self.sem, 1)
        self.eng.wait_ge(self.sem, self.n)


class Carver:

    def __init__(self, whole, at=0):
        self.whole, self.at = whole, at

    def take(self, *dims):
        n = int(np.prod(dims))
        part = self.whole[:, self.at:self.at + n]
        self.at += n
        assert self.at <= self.whole.shape[1], ("SBUF work space", self.at)
        if len(dims) == 1:
            return part
        names = "abcde"[:len(dims)]
        spec = f"p ({' '.join(names)}) -> p {' '.join(names)}"
        return part.rearrange(spec, **{c: d for c, d in zip(names, dims)})


def first_layer(nc, l, T, dram, sem, chip):
    x, consts, masks = chip["x"], chip["consts"], chip["masks"]
    cos, sin, silu_c = chip["cos"], chip["sin"], chip["silu_c"]
    work = Carver(chip["work"])

    rows, cols = work.take(P), work.take(N_ROWS)
    wk2, wv2 = work.take(2, HD), work.take(2, HD)
    w_alpha, fox_b = work.take(GLA_H * HD), work.take(8)
    hT = work.take(KD, S)
    nsaT = work.take(6, S)
    hid_c = work.take(2, 2, 2 * N_CMP)
    gelu_t, gelu_e = work.take(2, 2 * N_CMP), work.take(2, 2 * N_CMP)
    kcT, kc_sin = work.take(N_CMP), work.take(N_CMP)
    vc = work.take(2, HD)
    vs, vw = work.take(TT, P), work.take(TT, P)
    g_nsa = work.take(TT, N_GATE)
    p_cmp = work.take(2, 4, TT, N_CMP)
    stat_cmp = work.take(2, 4, TT)
    sb_qk = work.take(KD, S)
    sbq, sbk = sb_qk[:, 0:4, :], sb_qk[:, 4:8, :]
    sbv = work.take(TT, 512)
    gle = work.take(TT, 512)
    gla_b = work.take(2, S)
    att = work.take(2, 3, 2, P)
    fxq, fxk = work.take(4, S), work.take(4, S)
    fxv = work.take(TT, 512)
    log_f, fox_t = work.take(TT, 8), work.take(TT, 8)
    fox_row = work.take(S)
    gates = work.take(4 * KD, S)
    yT = work.take(4 * 4, S)
    prob, probT = work.take(2, 3 * P), work.take(2, 3 * P)
    sb_at = work.at
    sb_u, sb_p = work.take(2, 3 * P), work.take(2, 3 * P)
    neg_max, total = work.take(2, TT), work.take(2, TT)
    stat, rstd = work.take(TT), work.take(TT)
    gl_stat, gl_rstd = work.take(TT, GLA_H), work.take(TT, GLA_H)
    early = Carver(gates.rearrange("p a b -> p (a b)"))
    glq, glk = early.take(2, S), early.take(2, S)
    glv, glg = early.take(TT, 512), early.take(TT, 512)
    gla_t, glaT = early.take(2, S), early.take(S)
    lv_d, lv_q, lv_k = early.take(2, 512), early.take(2, 512), early.take(2, 512)
    flat_y = yT.rearrange("p a b -> p (a b)")
    xn = flat_y[:, 0:TT * D].rearrange("p (t d) -> p t d", t=TT)
    sq = flat_y[:, TT * D:TT * D + D]
    pcT = [yT[:, 4:8, :], yT[:, 12:16, :]]
    blk = Carver(chip["work"], sb_at).take(2, CMP_LEN // 2, 2, N_CMP)
    mix_t = fxv
    hidden = gates
    mixedT = sb_qk

    K = lambda name: consts[:, T["f32"][name][0]:sum(T["f32"][name])]
    M = lambda name: masks[:, T["bf16"][name][0]:sum(T["bf16"][name])]
    ident, one, eps = K("ident"), K("one"), K("eps")
    head_sel = K("head_sel").rearrange("p (h t) -> p h t", h=8)
    level_mask = M("levels").bitcast(U16).rearrange("p (n t) -> p n t", n=len(LEVELS) - 1)

    jobs = []
    for c in range(HALF_HEADS):
        for g in range(2):
            jobs += [("slc", c, g), ("win", c, g)]
    jobs += [("fox", h // 2, h % 2) for h in range(8)]
    jobs += [("sb", h // 2, h % 2) for h in range(8)]
    NJ = len(jobs)

    ada_steps = [i for i in range(4 * KD) if i % 8 in (1, 4, 6)]
    step_fills, step_tiles = [], []
    for i in range(4 * KD):
        if i % 4 == 0:
            step_tiles.append(("gate", i // 4))
        step_fills.append(f"g{i}")
        if i in ada_steps:
            step_fills.append(f"ada{ada_steps.index(i)}")
            step_tiles.append(("ada", ada_steps.index(i)))

    LV = [f"lv{n}_{par}" for n in range(len(LEVELS)) for par in range(2)]
    proj_uses = (["params"] + [f"xT{c}" for c in range(4)]
                 + ["q0", "q1", "kc", "vc", "vs", "kskw", "vwg", "rope0", "rope1", "rope2"]
                 + ["hk", "hv", "kc2", "rope_kc", "vc2"]
                 + ["gq", "gk", "ga", "gg0", "gg1", "la", "gv0", "gv1"]
                 + ["sq0", "sq1", "sk0", "sk1", "sv0", "sv1", "fq0", "fq1", "fk0", "fk1",
                    "fv0", "fv1", "ff", "fc", "gyT0", "gyT1"]
                 + step_fills
                 + [f"br{n}_{f}" for n in range(4) for f in range(KD // 2)]
                 + [f"wo{h}{t}" for h in range(2) for t in range(TT)]
                 + [f"yT{c}" for c in range(4)]
                 + [f"up{i}" for i in range(FFK // 2)])
    PROJ = Banks(sem, "proj", chip["psum"][0:2], proj_uses)
    SC = Banks(sem, "score", chip["psum"][2:4], ["cmp0", "cmp1"] + [f"s{j}" for j in range(NJ)] + ["down0", "down1"])
    PT = Banks(sem, "turn", chip["psum"][4:6],
               LV + [f"pc{g}{i}" for g in range(2) for i in range(2)]
               + [f"p{j}" for j in range(NJ) if jobs[j][0] != "sb"])
    OT = Banks(sem, "out", chip["psum"][6:8],
               ["go0", "go1"] + [f"o_{k}{c}" for k in ("nsa", "fox", "sb") for c in range(HALF_HEADS)]
               + ["down2", "down3"])

    def done(name):
        return PROJ.full, PROJ.order[name] + 1

    w_in = dram["w_in"][bass.ds(l, 1)].rearrange("l (k p) n -> p (l k) n", p=P)
    whole = (slice(None), slice(None), slice(None))

    def in_tile(name, c0, n, last):
        return name, KD, n, [(whole, w_in[:, :, c0:c0 + n])], done(last)

    down_used = sem("down_used")
    branch = dram["w_branch"][bass.ds(l, 1)].rearrange("l n c d -> (l n) c d")

    def branch_tile(n):
        if n == 0:
            src = branch[0].rearrange("(g c d) m -> g d c m", g=2, d=HD)
            parts = [((slice(g * HD, g * HD + HD), slice(None), slice(None)), src[g]) for g in range(2)]
        else:
            parts = [(whole, branch[n].rearrange("(c p) m -> p c m", p=P))]
        return f"branch{n}", 4, D, parts, done(f"br{n}_{KD // 2 - 1}")

    def layer_of(name):
        return dram[name][bass.ds(l, 1)]

    wk1 = layer_of("nsa_cmp_wk1").rearrange("l (k p) n -> p (l k) n", p=P)
    wv1 = layer_of("nsa_cmp_wv1").rearrange("l (k p) n -> p (l k) n", p=P)
    w_out = layer_of("w_out").rearrange("l (k p) n -> p (l k) n", p=P)
    w_ff1 = layer_of("w_ff1").rearrange("l (k p) n -> p (l k) n", p=P)
    w_ff2 = layer_of("w_ff2").rearrange("l (k p) n -> p (l k) n", p=P)
    def blocks(name, c0, order, last):
        parts = [((slice(None), slice(None), slice(i * HD, (i + 1) * HD)),
                  w_in[:, :, c0 + b * HD:c0 + (b + 1) * HD]) for i, b in enumerate(order)]
        return name, KD, 512, parts, done(last)

    q_tile = blocks("q", Q0, [0, 4, 1, 5, 2, 6, 3, 7], "q1")
    cmp_tile = blocks("cmp", KC0, [0, 0, 1, 1, 2, 2, 3, 3], "vc")
    tiles = [q_tile, cmp_tile, in_tile("kvs", KS0, 256, "kskw"), in_tile("kwg", KS0 + 256, 280, "vwg"),
             ("wk1", 16, CMP_HID, [(whole, wk1)], done("hk")), ("wv1", 16, CMP_HID, [(whole, wv1)], done("hv")),
             in_tile("glqk", GLQ0, 512, "gk"), in_tile("glag", GLA0, 528, "gg1"), in_tile("glv", GLV0, 512, "gv1"),
             in_tile("sbq", SBQ0, 512, "sq1"), in_tile("sbk", SBK0, 512, "sk1"), in_tile("sbv", SBV0, 512, "sv1"),
             in_tile("fxq", FXQ0, 512, "fq1"), in_tile("fxk", FXK0, 512, "fk1"), in_tile("fxv", FXV0, 520, "ff")]
    w_ada = layer_of("w_ada_2").rearrange("l (k p) n -> p (l k) n", p=P)
    for kind, i in step_tiles:
        if kind == "gate":
            tiles.append(in_tile(f"gate{i}", GATE0 + 512 * i, 512, f"g{4 * i + 3}"))
        else:
            tiles.append((f"ada{i}", KD, 512, [(whole, w_ada[:, :, 512 * i:512 * i + 512])], done(f"ada{i}")))
    tiles += [branch_tile(n) for n in range(4)]
    tiles += [(f"out{h}", KD, 512, [(whole, w_out[:, :, 512 * h:512 * h + 512])], done(f"wo{h}1")) for h in range(2)]
    tiles += [(f"up{i}", KD, 512, [(whole, w_ff1[:, :, 512 * i:512 * i + 512])], done(f"up{2 * i + 1}")) for i in range(8)]
    tiles += [(f"down{i}", 4, D, [(whole, w_ff2[:, 4 * i:4 * i + 4, :])], (down_used, i + 1)) for i in range(8)]
    W = Weights(sem, "w", chip["ring"], tiles)

    rows_in = sem("rows_in")
    small_in = sem("small_in")
    rstd_ready = sem("rstd_ready")
    xn_ready = sem("xn_ready")
    gelu_x2 = sem("gelu_x2")
    gelu_in = sem("gelu_in")
    gelu_exp = sem("gelu_exp")
    roped = sem("roped")
    gate_ready = sem("gate_ready")
    cmp_in = sem("cmp_in")
    cmp_exp = sem("cmp_exp")
    cmp_ready = sem("cmp_ready")
    gl_gate = sem("gl_gate")
    la_log = sem("la_log")
    lv_diff = sem("lv_diff")
    lv_exp = sem("lv_exp")
    lv_ready = sem("lv_ready")
    gl_scale = sem("gl_scale")
    fox_log = sem("fox_log")
    fox_ready = sem("fox_ready")
    max_ready = sem("max_ready")
    prob_ready = sem("prob_ready")
    sb_log = sem("sb_log")
    sb_soft = sem("sb_soft")
    sb_later = sem("sb_later")
    mix_gate = sem("mix_gate")
    mixed_ready = sem("mixed_ready")
    hidden_ready = sem("hidden_ready")
    act_self, dve_self = sem("act_self"), sem("dve_self")

    with nc.Block() as block:

        @block.sync
        def _(sp):
            W.load(sp)

        @block.tensor
        def _(pe):
            def mm(out, lhsT, rhs, start, stop):
                return nc.tensor.matmul(out, lhsT, rhs, start=start, stop=stop)

            def turn(out, src):
                return nc.tensor.transpose(out, src, ident[0:src.shape[0], 0:src.shape[0]])

            def gemm_T(out, w, cols):
                for k in range(KD):
                    last = mm(out, w[:, k, cols], hT[:, k, :], k == 0, k == KD - 1)
                return last

            def gemm(out, w, cols, t):
                for k in range(KD):
                    last = mm(out, hT[:, k, t * P:t * P + P], w[:, k, cols], k == 0, k == KD - 1)
                return last

            def turn_x(name, ready):
                pe.wait_ge(xn_ready, ready)
                for c in range(4):
                    ps = PROJ.claim(pe, f"{name}{c}")
                    for k in range(2):
                        for t in range(TT):
                            last = turn(ps[:, (2 * k + t) * P:(2 * k + t + 1) * P],
                                        xn[:, t, (2 * c + k) * P:(2 * c + k + 1) * P])
                    last.then_inc(PROJ.full, 1)

            def pairs(names, w, c0):
                for i, name in enumerate(names):
                    ps = PROJ.claim(pe, name)
                    for k in range(2):
                        at = c0 + (2 * i + k) * P
                        last = gemm_T(ps[:, k * S:(k + 1) * S], w, slice(at, at + P))
                    last.then_inc(PROJ.full, 1)

            pe.wait_ge(rows_in, 7 * 16)
            turn(PROJ.claim(pe, "params")[:, 0:N_ROWS], rows[0:N_ROWS, :]).then_inc(PROJ.full, 1)
            turn_x("xT", TT)

            w = W.arrived(pe, "q")
            PROJ.taken(pe, "xT2", "xT3")
            for i in range(2):
                ps = PROJ.claim(pe, f"q{i}")
                for k in range(2):
                    c = 2 * i + k
                    last = gemm_T(ps[:, k * S:(k + 1) * S], w, slice(c * P, (c + 1) * P))
                last.then_inc(PROJ.full, 1)
            w = W.arrived(pe, "cmp")
            for i, name in enumerate(("kc", "vc")):
                ps = PROJ.claim(pe, name)
                for g in range(2):
                    last = gemm_T(ps[:, g * S:(g + 1) * S], w, slice((2 * i + g) * P, (2 * i + g + 1) * P))
                last.then_inc(PROJ.full, 1)
            w = W.arrived(pe, "kvs")
            ps = PROJ.claim(pe, "vs")
            for t in range(TT):
                last = gemm(ps[:, t * P:(t + 1) * P], w, slice(P, 2 * P), t)
            last.then_inc(PROJ.full, 1)
            ps = PROJ.claim(pe, "kskw")
            gemm_T(ps[:, 0:S], w, slice(0, P))
            w = W.arrived(pe, "kwg")
            gemm_T(ps[:, S:2 * S], w, slice(0, P)).then_inc(PROJ.full, 1)
            ps = PROJ.claim(pe, "vwg")
            for t in range(TT):
                last = gemm(ps[:, t * 152:(t + 1) * 152], w, slice(P, 280), t)
            last.then_inc(PROJ.full, 1)

            for i in range(3):
                ps = PROJ.claim(pe, f"rope{i}")
                PROJ.taken(pe, ("q0", "q1", "kskw")[i])
                mm(ps[:, :], K("rot"), nsaT[:, 2 * i:2 * i + 2, :], True, True).then_inc(PROJ.full, 1)

            for i, name in enumerate(("hk", "hv")):
                w = W.arrived(pe, ("wk1", "wv1")[i])
                ps = PROJ.claim(pe, name)
                PROJ.taken(pe, ("kc", "vc")[i])
                for m in range(2):
                    for r in range(16):
                        last = mm(ps[:, m * 2 * N_CMP:(m + 1) * 2 * N_CMP], w[:, r, m * P:(m + 1) * P],
                                  blk[:, i, r, :, :], r == 0, r == 15)
                last.then_inc(PROJ.full, 1)
            ps = PROJ.claim(pe, "kc2")
            pe.wait_ge(small_in, 4 * 16)
            PROJ.taken(pe, "hk")
            for g in range(2):
                for m in range(2):
                    last = mm(ps[g * HD:(g + 1) * HD, 0:N_CMP], wk2[:, m, :],
                              hid_c[:, 0, m, g * N_CMP:(g + 1) * N_CMP], m == 0, m == 1)
            last.then_inc(PROJ.full, 1)
            ps = PROJ.claim(pe, "rope_kc")
            PROJ.taken(pe, "kc2")
            mm(ps[:, 0:N_CMP], K("rot"), kcT, True, True).then_inc(PROJ.full, 1)
            ps = PROJ.claim(pe, "vc2")
            PROJ.taken(pe, "hv")
            for g in range(2):
                for m in range(2):
                    last = mm(ps[0:N_CMP, g * HD:(g + 1) * HD], hid_c[:, 1, m, g * N_CMP:(g + 1) * N_CMP],
                              wv2[:, m, :], m == 0, m == 1)
            last.then_inc(PROJ.full, 1)

            pairs(["gq"], W.arrived(pe, "glqk"), 0)
            pairs(["gk"], W.arrived(pe, "glqk"), S)
            w = W.arrived(pe, "glag")
            gemm_T(PROJ.claim(pe, "ga")[0:GLA_RANK, 0:S], w, slice(0, GLA_RANK)).then_inc(PROJ.full, 1)
            for t in range(TT):
                gemm(PROJ.claim(pe, f"gg{t}")[:, :], w, slice(GLA_RANK, 528), t).then_inc(PROJ.full, 1)
            ps = PROJ.claim(pe, "la")
            PROJ.taken(pe, "ga")
            for c in range(2):
                last = mm(ps[:, c * S:(c + 1) * S], w_alpha[0:GLA_RANK, c * P:(c + 1) * P], glaT[0:GLA_RANK, :], True, True)
            last.then_inc(PROJ.full, 1)
            w = W.arrived(pe, "glv")
            for t in range(TT):
                gemm(PROJ.claim(pe, f"gv{t}")[:, :], w, slice(0, 512), t).then_inc(PROJ.full, 1)

            pe.wait_ge(roped, 4)
            for g in range(2):
                ps = SC.claim(pe, f"cmp{g}")
                for c in range(4):
                    for t in range(TT):
                        at = (c * TT + t) * N_CMP
                        last = mm(ps[:, at:at + N_CMP], nsaT[g * HD:(g + 1) * HD, c, t * P:(t + 1) * P],
                                  kcT[g * HD:(g + 1) * HD, :], True, True)
                last.then_inc(SC.full, 1)

            def level(n):
                if LEVELS[n] == 0:
                    PROJ.taken(pe, "gq", "gk")
                else:
                    pe.wait_ge(lv_ready, n + (n == 0))
                at = max(n - 1, 0) % 2
                q = glq if LEVELS[n] == 0 else lv_q[:, at].rearrange("p (c s) -> p c s", c=2)
                k = glk if LEVELS[n] == 0 else lv_k[:, at].rearrange("p (c s) -> p c s", c=2)
                for par in range(2):
                    ps = PT.claim(pe, f"lv{n}_{par}")
                    r = slice(par * HD, (par + 1) * HD)
                    for c in range(2):
                        for t in ([1] if LEVELS[n] == P else range(TT)):
                            at = c * P if LEVELS[n] == P else (t * 2 + c) * P
                            s = 0 if LEVELS[n] == P else t
                            last = mm(ps[:, at:at + P], k[r, c, s * P:(s + 1) * P], q[r, c, t * P:(t + 1) * P], True, True)
                    last.then_inc(PT.full, 1)

            w = W.arrived(pe, "sbq")
            for i in range(2):
                ps = PROJ.claim(pe, f"sq{i}")
                for k in range(2):
                    last = gemm_T(ps[:, k * S:(k + 1) * S], w, slice((2 * i + k) * P, (2 * i + k + 1) * P))
                last.then_inc(PROJ.full, 1)
                level(i)
            w = W.arrived(pe, "sbk")
            for i in range(2):
                ps = PROJ.claim(pe, f"sk{i}")
                for k in range(2):
                    last = gemm_T(ps[:, k * S:(k + 1) * S], w, slice((2 * i + k) * P, (2 * i + k + 1) * P))
                last.then_inc(PROJ.full, 1)
                level(2 + i)
            w = W.arrived(pe, "sbv")
            for t in range(TT):
                gemm(PROJ.claim(pe, f"sv{t}")[:, :], w, slice(0, 512), t).then_inc(PROJ.full, 1)
                level(4 + t)
            w = W.arrived(pe, "fxq")
            for i in range(2):
                ps = PROJ.claim(pe, f"fq{i}")
                for k in range(2):
                    last = gemm_T(ps[:, k * S:(k + 1) * S], w, slice((2 * i + k) * P, (2 * i + k + 1) * P))
                last.then_inc(PROJ.full, 1)
                level(6 + i)
            w = W.arrived(pe, "fxk")
            for i in range(2):
                ps = PROJ.claim(pe, f"fk{i}")
                for k in range(2):
                    last = gemm_T(ps[:, k * S:(k + 1) * S], w, slice((2 * i + k) * P, (2 * i + k + 1) * P))
                last.then_inc(PROJ.full, 1)
                if i == 0:
                    level(8)
            w = W.arrived(pe, "fxv")
            for t in range(TT):
                gemm(PROJ.claim(pe, f"fv{t}")[:, :], w, slice(0, 512), t).then_inc(PROJ.full, 1)
            ps = PROJ.claim(pe, "ff")
            for t in range(TT):
                last = gemm(ps[:, t * 8:(t + 1) * 8], w, slice(512, 520), t)
            last.then_inc(PROJ.full, 1)

            PT.taken(pe, "lv8_0", "lv8_1")
            PROJ.taken(pe, "gv0", "gv1")
            for t in range(TT):
                ps = OT.claim(pe, f"go{t}")
                for h in range(GLA_H):
                    dv = slice(h * GLA_DV, (h + 1) * GLA_DV)
                    last = mm(ps[:, dv], att[:, h % 2, t, h // 2, :], glv[:, t, dv], True, t == 0)
                    if t == 1:
                        last = mm(ps[:, dv], att[:, h % 2, 2, h // 2, :], glv[:, 0, dv], False, True)
                last.then_inc(OT.full, 1)

            for g in range(2):
                pe.wait_ge(cmp_ready, g + 1)
                for i in range(2):
                    ps = PT.claim(pe, f"pc{g}{i}")
                    for c in range(2):
                        for t in range(TT):
                            at = (c * TT + t) * P
                            last = turn(ps[0:N_CMP, at:at + P], p_cmp[:, g, 2 * i + c, t, :])
                    last.then_inc(PT.full, 1)

            ps = PROJ.claim(pe, "fc")
            pe.wait_ge(fox_ready, 1)
            upto = consts[:, T["f32"]["neg_upto"][0]:T["f32"]["neg_upto"][0] + S]
            mm(ps[0:8, 0:S], log_f[:, 0, :], upto, True, False)
            mm(ps[0:8, P:S], log_f[:, 1, :], upto[:, 0:P], False, True).then_inc(PROJ.full, 1)

            for t in range(TT):
                ps = PROJ.claim(pe, f"gyT{t}")
                OT.taken(pe, f"go{t}")
                for h in range(GLA_H):
                    last = turn(ps[:, h * P:(h + 1) * P], gle[:, t, h * GLA_DV:(h + 1) * GLA_DV])
                last.then_inc(PROJ.full, 1)

            def scores(j):
                kind, c, par = jobs[j]
                r = slice(par * HD, (par + 1) * HD)
                ps = SC.claim(pe, f"s{j}")
                if kind == "sb":
                    mm(ps[:, 0:S], sbk[r, c, 0:P], sbq[r, c, :], True, False)
                    mm(ps[:, S:S + P], sbk[r, c, P:S], sbq[r, c, P:S], False, False)
                    mm(ps[:, 0:P], M("ident"), M("strict"), False, False)
                    mm(ps[:, S:S + P], M("ident"), M("strict"), False, True).then_inc(SC.full, 1)
                    return
                for t in range(TT):
                    n = (t + 1) * P
                    at = t * P
                    if kind == "fox":
                        mm(ps[:, at:at + n], fxq[r, c, t * P:(t + 1) * P], fxk[r, c, 0:n], True, False)
                        mm(ps[:, at:at + n], head_sel[0:8, 2 * c + par, :], fox_row[0:8, 0:n], False, False)
                    else:
                        mm(ps[:, at:at + n], nsaT[r, c, t * P:(t + 1) * P], nsaT[r, 4 + (kind == "win"), 0:n], True, False)
                    last = mm(ps[:, at + n - P:at + n], M("ident"), M("causal"), False, True)
                last.then_inc(SC.full, 1)

            def turned(j):
                kind, c, par = jobs[j]
                if kind == "sb":
                    ps = SC.bank(f"s{j}")
                    pe.wait_ge(sb_soft, j - 23)
                    sp_ = sb_p[:, j % 2]
                    add = lambda out, neg, rhs: nc.tensor.matmul(out, K(neg), rhs, start=False, stop=True, skip_group_check=True)
                    add(ps[:, 0:S], "neg_from", sp_[:, 0:S])
                    add(ps[:, P:S], "neg_ones", sp_[:, S:S + P])
                    add(ps[:, S:S + P], "neg_from", sp_[:, S:S + P]).then_inc(sb_later, 1)
                    return
                ps = PT.claim(pe, f"p{j}")
                pe.wait_ge(prob_ready, j + 1)
                p = prob[:, j % 2]
                turn(ps[:, 0:P], p[:, 0:P])
                turn(ps[:, P:2 * P], p[:, P:2 * P])
                turn(ps[:, 2 * P:3 * P], p[:, 2 * P:3 * P]).then_inc(PT.full, 1)

            def output(j):
                kind, c, par = jobs[j]
                r = slice(par * HD, (par + 1) * HD)
                group = "nsa" if kind in ("slc", "win") else kind
                name = f"o_{group}{c}"
                first, last_of = (kind != "win"), (kind != "slc")
                ps = OT.claim(pe, name) if first and par == 0 else OT.bank(name)
                if kind == "slc":
                    PT.taken(pe, f"pc{par}{c // 2}")
                    mm(ps[r, 0:S], vc[0:N_CMP, par, :], pcT[par][0:N_CMP, c, :], True, False)
                if kind == "sb":
                    SC.taken(pe, f"s{j}")
                    p, v = probT[:, j % 2], sbv[:, :, (2 * c + par) * HD:(2 * c + par + 1) * HD]
                else:
                    PT.taken(pe, f"p{j}")
                    p = probT[:, j % 2]
                    v = {"slc": vs, "win": vw}[kind][:, :, r] if kind != "fox" else \
                        fxv[:, :, (2 * c + par) * HD:(2 * c + par + 1) * HD]
                mm(ps[r, 0:S], v[:, 0, :], p[:, 0:S], kind in ("sb", "fox"), False)
                last = mm(ps[r, P:S], v[:, 1, :], p[:, S:S + P], False, last_of)
                if par == 1 and last_of:
                    last.then_inc(OT.full, 1)

            PROJ.taken(pe, "vs", "vwg", "vc2")
            for i in range(NJ + 2):
                if i < 4 * KD:
                    w = W.arrived(pe, f"gate{i // 4}")
                    gemm_T(PROJ.claim(pe, f"g{i}")[:, 0:S], w, slice(i % 4 * P, (i % 4 + 1) * P)).then_inc(PROJ.full, 1)
                if i in ada_steps:
                    n = ada_steps.index(i)
                    w = W.arrived(pe, f"ada{n}")
                    ps = PROJ.claim(pe, f"ada{n}")
                    for c in range(4):
                        for k in range(KD):
                            last = mm(ps[:, 2 * c:2 * c + 2], w[:, k, c * P:(c + 1) * P], silu_c[:, k, :], k == 0, k == KD - 1)
                    last.then_inc(PROJ.full, 1)
                if i == 15:
                    PROJ.taken(pe, "fc", "fv0", "fv1", "fk0", "fk1")
                if i < NJ:
                    scores(i)
                if 1 <= i <= NJ:
                    turned(i - 1)
                if i >= 2:
                    output(i - 2)

            for n in range(4):
                w = W.arrived(pe, f"branch{n}")
                if n == 0:
                    PROJ.taken(pe, "gyT0", "gyT1")
                    OT.taken(pe, "o_sb2", "o_sb3")
                for f in range(KD // 2):
                    ps = PROJ.claim(pe, f"br{n}_{f}")
                    for k in range(2):
                        for c in range(4):
                            last = mm(ps[:, k * S:(k + 1) * S], w[:, c, (2 * f + k) * P:(2 * f + k + 1) * P],
                                      yT[:, 4 * n + c, :], c == 0, c == 3)
                    last.then_inc(PROJ.full, 1)
            pe.wait_ge(mixed_ready, 3 * KD // 2)
            for h in range(2):
                w = W.arrived(pe, f"out{h}")
                for t in range(TT):
                    ps = PROJ.claim(pe, f"wo{h}{t}")
                    for k in range(KD):
                        last = mm(ps[:, :], mixedT[:, k, t * P:(t + 1) * P], w[:, k, :], k == 0, k == KD - 1)
                    last.then_inc(PROJ.full, 1)

            turn_x("yT", 2 * TT)
            PROJ.taken(pe, "yT2", "yT3")
            for i in range(8):
                pairs([f"up{2 * i}", f"up{2 * i + 1}"], W.arrived(pe, f"up{i}"), 0)
            downs = [SC.claim(pe, "down0"), SC.claim(pe, "down1"), OT.claim(pe, "down2"), OT.claim(pe, "down3")]
            for i in range(8):
                w = W.arrived(pe, f"down{i}")
                pe.wait_ge(hidden_ready, 2 * i + 2)
                for k in range(4):
                    c = 4 * i + k
                    for t in range(TT):
                        for h in range(2):
                            last = mm(downs[2 * t + h][:, :], hidden[:, c, t * P:(t + 1) * P],
                                      w[:, k, 512 * h:512 * h + 512], c == 0, c == FFK - 1)
                            if c == FFK - 1:
                                last.then_inc((SC, OT)[t].full, 1)
                if i < 7:
                    last.then_inc(down_used, 1)

        @block.scalar
        def _(act):
            link = Chain(act, act_self)

            def f(out, in_, func, **kw):
                return nc.scalar.activation(out, in_, func, **kw)

            def copy(out, in_, **kw):
                return f(out, in_, ACT.Copy, **kw)

            def take(name, out, in_=slice(None), **kw):
                ps = PROJ.arrived(act, name)
                copy(out, ps[:, in_], **kw).then_inc(PROJ.free(name), 1)

            def row_scale():
                for t in range(TT):
                    link(f(sq, x[:, t, :], ACT.Square, accum_out=stat[:, t:t + 1]))
                link(f(stat, stat, ACT.Ln, scale=1.0 / D, bias=eps))
                f(rstd, stat, ACT.Exp, scale=-0.5).then_inc(rstd_ready, 1)

            def take_hT(name, row):
                for c in range(4):
                    ps = PROJ.arrived(act, f"{name}{c}")
                    copy(hT[:, 2 * c, :], ps[:, 0:S], scale=cols[:, row + 2 * c:row + 2 * c + 1])
                    copy(hT[:, 2 * c + 1, :], ps[:, S:2 * S], scale=cols[:, row + 2 * c + 1:row + 2 * c + 2])\
                        .then_inc(PROJ.free(f"{name}{c}"), 1)

            def log1p_exp_neg_abs(out, in_):
                link(f(out, in_, ACT.Abs))
                link(f(out, out, ACT.Exp, scale=-1.0))
                return f(out, out, ACT.Ln, bias=one)

            def level_exp(k):
                act.wait_ge(lv_diff, k + 1)
                link(f(lv_d[:, k % 2], lv_d[:, k % 2], ACT.Abs))
                f(lv_d[:, k % 2], lv_d[:, k % 2], ACT.Exp, scale=-1.0 / GLA_TAU).then_inc(lv_exp, 1)

            def row_load(at, n, src):
                act.dma_start(rows[at:at + n, :], src).then_inc(rows_in, 16)

            row_load(ROW_MIX, KD, layer_of("norm_mix").rearrange("l (r p) -> (l r) p", p=P))
            row_load(ROW_FF, KD, layer_of("norm_ff").rearrange("l (r p) -> (l r) p", p=P))
            row_load(ROW_GATE, 4 * KD, layer_of("b_gate").rearrange("l (r p) -> (l r) p", p=P))
            row_load(ROW_GLB, 2, layer_of("gla_b_alpha").rearrange("l (r p) -> (l r) p", p=P))
            row_load(ROW_GLN, 1, layer_of("gla_norm"))
            row_load(ROW_PEK, 16, layer_of("nsa_cmp_pos_k").rearrange("l (r a) d -> (l r) (a d)", a=2))
            row_load(ROW_PEV, 16, layer_of("nsa_cmp_pos_v").rearrange("l (r a) d -> (l r) (a d)", a=2))
            act.dma_start(wk2, layer_of("nsa_cmp_wk2").rearrange("l (k p) n -> p (l k) n", p=P)).then_inc(small_in, 16)
            act.dma_start(wv2, layer_of("nsa_cmp_wv2").rearrange("l (k p) n -> p (l k) n", p=P)).then_inc(small_in, 16)
            act.dma_start(w_alpha[0:GLA_RANK, :], layer_of("gla_w_alpha").rearrange("l r n -> (l r) n")).then_inc(small_in, 16)
            act.dma_start(fox_b, layer_of("fox_b_f").partition_broadcast(P).rearrange("p l h -> p (l h)")).then_inc(small_in, 16)

            row_scale()
            ps = PROJ.arrived(act, "params")
            copy(cols[:, 0:ROW_GATE], ps[:, 0:ROW_GATE])
            copy(cols[:, ROW_GATE:ROW_GLB], ps[:, ROW_GATE:ROW_GLB], scale=-1.0)
            link(copy(cols[:, ROW_GLB:N_ROWS], ps[:, ROW_GLB:N_ROWS]))
            copy(kc_sin, ps[:, 0:N_CMP]).then_inc(PROJ.free("params"), 1)
            take_hT("xT", ROW_MIX)

            for i in range(2):
                take(f"q{i}", nsaT[:, 2 * i:2 * i + 2, :].rearrange("p a b -> p (a b)"), scale=HD ** -0.5)
            take("vs", vs.rearrange("p a b -> p (a b)"), slice(0, S))
            take("kskw", nsaT[:, 4:6, :].rearrange("p a b -> p (a b)"))
            ps = PROJ.arrived(act, "vwg")[:, 0:TT * 152].rearrange("p (t n) -> p t n", t=TT)
            copy(vw, ps[:, :, 0:P])
            f(g_nsa, ps[:, :, P:152], ACT.Exp, scale=-1.0).then_inc(PROJ.free("vwg"), 1)
            for i, name in enumerate(("hk", "hv")):
                ps = PROJ.arrived(act, name)[:, 0:4 * N_CMP].rearrange("p (m n) -> p m n", m=2)
                f(gelu_t, ps, ACT.Square).then_inc(gelu_x2, 1)
                act.wait_ge(gelu_in, i + 1)
                f(gelu_e, gelu_t, ACT.Exp, scale=-2.0 * GELU_C).then_inc(gelu_exp, 1)
                PROJ.taken(act, name)
            take("kc2", kcT, slice(0, N_CMP))
            ps = PROJ.arrived(act, "vc2")
            copy(vc[0:N_CMP], ps[0:N_CMP, 0:P].rearrange("p (g d) -> p g d", g=2)).then_inc(PROJ.free("vc2"), 1)

            take("gq", glq.rearrange("p a b -> p (a b)"), scale=HD ** -0.5)
            take("gk", glk.rearrange("p a b -> p (a b)"))
            ps = PROJ.arrived(act, "ga")
            copy(glaT[0:GLA_RANK, :], ps[0:GLA_RANK, 0:S]).then_inc(PROJ.free("ga"), 1)
            for t in range(TT):
                ps = PROJ.arrived(act, f"gg{t}")
                copy(glg[:, t, :], ps[:, :])
                f(gle[:, t, :], ps[:, :], ACT.Exp, scale=-1.0).then_inc(PROJ.free(f"gg{t}"), 1)
            ps = PROJ.arrived(act, "la")
            for c in range(2):
                link(f(gla_t[:, c, :], ps[:, c * S:(c + 1) * S], ACT.Abs, bias=cols[:, ROW_GLB + c:ROW_GLB + c + 1]))
            link(f(gla_t, gla_t, ACT.Exp, scale=-1.0))
            f(gla_t, gla_t, ACT.Ln, bias=one).then_inc(la_log, 1)
            for t in range(TT):
                take(f"gv{t}", glv[:, t, :])

            for g in range(2):
                act.wait_ge(cmp_in, g + 1)
                f(p_cmp[:, g], p_cmp[:, g], ACT.Exp).then_inc(cmp_exp, 1)

            level_exp(0)
            level_exp(1)
            for i, (name, out, kw) in enumerate((
                    ("sq0", sbq[:, 0:2, :], {"scale": HD ** -0.5}), ("sq1", sbq[:, 2:4, :], {"scale": HD ** -0.5}),
                    ("sk0", sbk[:, 0:2, :], {}), ("sk1", sbk[:, 2:4, :], {}),
                    ("sv0", sbv[:, 0:1, :], {}), ("sv1", sbv[:, 1:2, :], {}),
                    ("fq0", fxq[:, 0:2, :], {"scale": HD ** -0.5}), ("fq1", fxq[:, 2:4, :], {"scale": HD ** -0.5}),
                    ("fk0", fxk[:, 0:2, :], {}), ("fk1", fxk[:, 2:4, :], {}),
                    ("fv0", fxv[:, 0:1, :], {}), ("fv1", fxv[:, 1:2, :], {}))):
                take(name, out.rearrange("p a b -> p (a b)"), **kw)
                if 2 <= i + 1 <= len(LEVELS) - 2:
                    level_exp(i + 1)
            PROJ.taken(act, "ff")
            log1p_exp_neg_abs(log_f, fox_t).then_inc(fox_log, 1)

            for t in range(TT):
                ps = OT.arrived(act, f"go{t}")
                for h in range(GLA_H):
                    link(f(gla_t[:, 0, 0:P], ps[:, h * P:(h + 1) * P], ACT.Square, accum_out=gl_stat[:, t, h:h + 1]))
                link(f(gl_stat[:, t], gl_stat[:, t], ACT.Ln, scale=1.0 / GLA_DV, bias=eps))
                f(gl_rstd[:, t], gl_stat[:, t], ACT.Exp, scale=-0.5).then_inc(gl_scale, 1)

            for g in range(2):
                for i in range(2):
                    ps = PT.arrived(act, f"pc{g}{i}")
                    copy(pcT[g][0:N_CMP, 2 * i:2 * i + 2, :], ps[0:N_CMP, :].rearrange("p (c s) -> p c s", c=2))\
                        .then_inc(PT.free(f"pc{g}{i}"), 1)
            ps = PROJ.arrived(act, "fc")
            copy(fox_row[0:8, :], ps[0:8, 0:S]).then_inc(PROJ.free("fc"), 1)
            for t in range(TT):
                ps = PROJ.arrived(act, f"gyT{t}")
                copy(yT[:, 8:12, t * P:(t + 1) * P], ps[:, :].rearrange("p (h s) -> p h s", h=GLA_H),
                     scale=cols[:, ROW_GLN:ROW_GLN + 1]).then_inc(PROJ.free(f"gyT{t}"), 1)

            for i in range(NJ + 2):
                if i < 4 * KD:
                    ps = PROJ.arrived(act, f"g{i}")
                    f(gates[:, i, :], ps[:, 0:S], ACT.Exp, scale=-1.0, bias=cols[:, ROW_GATE + i:ROW_GATE + i + 1])\
                        .then_inc(PROJ.free(f"g{i}"), 1)
                if i in ada_steps:
                    n = ada_steps.index(i)
                    ps = PROJ.arrived(act, f"ada{n}")
                    copy(chip["mod"][:, bass.ds(l * (2 * MODC) + 8 * n, 8)], ps[:, 0:8]).then_inc(PROJ.free(f"ada{n}"), 1)
                if i < NJ and jobs[i][0] == "sb":
                    ps = SC.arrived(act, f"s{i}")
                    log1p_exp_neg_abs(sb_u[:, i % 2], ps[:, 0:3 * P]).then_inc(sb_log, 1)
                elif i < NJ:
                    act.wait_ge(max_ready, i + 1)
                    ps = SC.arrived(act, f"s{i}")
                    f(prob[:, i % 2, 0:P], ps[:, 0:P], ACT.Exp, bias=neg_max[:, i % 2, 0:1],
                      accum_out=total[:, i % 2, 0:1])
                    f(prob[:, i % 2, P:3 * P], ps[:, P:3 * P], ACT.Exp, bias=neg_max[:, i % 2, 1:2],
                      accum_out=total[:, i % 2, 1:2]).then_inc(SC.free(f"s{i}"), 1)
                if 1 <= i <= NJ and jobs[i - 1][0] == "sb":
                    act.wait_ge(sb_later, i - 24)
                    ps = SC.arrived(act, f"s{i - 1}")
                    f(probT[:, (i - 1) % 2], ps[:, 0:3 * P], ACT.Exp).then_inc(SC.free(f"s{i - 1}"), 1)
                elif 1 <= i <= NJ:
                    ps = PT.arrived(act, f"p{i - 1}")
                    copy(probT[:, (i - 1) % 2], ps[:, 0:3 * P]).then_inc(PT.free(f"p{i - 1}"), 1)
                if i >= 2:
                    kind, c, par = jobs[i - 2]
                    if kind != "slc" and par == 1:
                        group, at = {"win": ("nsa", 0), "sb": ("sb", 4), "fox": ("fox", 12)}[kind]
                        ps = OT.arrived(act, f"o_{group}{c}")
                        copy(yT[:, at + c, :], ps[:, 0:S]).then_inc(OT.free(f"o_{group}{c}"), 1)

            PROJ.taken(act, "wo10", "wo11")
            row_scale()
            take_hT("yT", ROW_FF)
            for i in range(FFK // 2):
                ps = PROJ.arrived(act, f"up{i}")
                f(hidden[:, 2 * i:2 * i + 2, :].rearrange("p a b -> p (a b)"), ps[:, :], ACT.Relu)\
                    .then_inc(PROJ.free(f"up{i}"), 1)

        @block.vector
        def _(dve):
            link = Chain(dve, dve_self)
            vec = nc.vector

            def norm(count):
                dve.wait_ge(rstd_ready, count)
                for t in range(TT):
                    vec.tensor_scalar(xn[:, t, :], x[:, t, :], rstd[:, t:t + 1], None, ALU.mult).then_inc(xn_ready, 1)

            def sigmoid(e):
                link(vec.tensor_scalar_add(e, e, 1.0))
                link(vec.reciprocal(e, e))

            norm(1)
            link(vec.memset(att[:, :, 0:2].rearrange("p a b c d -> p a (b c d)"), 0.0))

            for i, name in enumerate(("kc", "vc")):
                if i == 0:
                    PROJ.taken(dve, "params")
                ps = PROJ.arrived(dve, name)
                row = (ROW_PEK, ROW_PEV)[i]
                for g in range(2):
                    tok = ps[:, g * S:(g + 1) * S].rearrange("p (n b r) -> p r b n", n=16, r=2)
                    for r in range(2):
                        h = slice(r * HD, (r + 1) * HD)
                        for a in range(2):
                            last = vec.tensor_tensor(blk[h, i, 8 * a:8 * a + 8, g, :], tok[h, r, :, a:a + N_CMP],
                                                     cols[h, row + 8 * a:row + 8 * a + 8].unsqueeze(2).to_broadcast([HD, 8, N_CMP]),
                                                     ALU.add)
                last.then_inc(PROJ.free(name), 1)

            cos2 = cos.unsqueeze(1).to_broadcast([P, 2, S])
            sin2 = sin.unsqueeze(1).to_broadcast([P, 2, S])
            for i in range(3):
                ps = PROJ.arrived(dve, f"rope{i}")
                part = nsaT[:, 2 * i:2 * i + 2, :]
                turn = mix_t[:, 0, :].rearrange("p (a b) -> p a b", a=2)
                vec.tensor_tensor(turn, ps[:, :].rearrange("p (a b) -> p a b", a=2), sin2, ALU.mult)\
                    .then_inc(PROJ.free(f"rope{i}"), 1)
                link(vec.tensor_tensor(part, part, cos2, ALU.mult))
                PROJ.taken(dve, f"rope{i}")
                vec.tensor_tensor(part, part, turn, ALU.add).then_inc(roped, 1)
                dve.wait_ge(roped, i + 1)

            for i, name in enumerate(("hk", "hv")):
                ps = PROJ.arrived(dve, name)[:, 0:4 * N_CMP].rearrange("p (m n) -> p m n", m=2)
                dve.wait_ge(gelu_x2, i + 1)
                link(vec.tensor_scalar(gelu_t, gelu_t, 0.044715, 1.0, ALU.mult, ALU.add))
                vec.tensor_tensor(gelu_t, gelu_t, ps, ALU.mult).then_inc(gelu_in, 1)
                dve.wait_ge(gelu_exp, i + 1)
                sigmoid(gelu_e)
                vec.tensor_tensor(hid_c[:, i], gelu_e, ps, ALU.mult).then_inc(PROJ.free(name), 1)
            last_tok = CMP_LEN - 1
            ps = PROJ.arrived(dve, "rope_kc")
            vec.tensor_tensor(kc_sin, ps[:, 0:N_CMP], sin[:, last_tok:S:CMP_STRIDE], ALU.mult).then_inc(PROJ.free("rope_kc"), 1)
            link(vec.tensor_tensor(kcT, kcT, cos[:, last_tok:S:CMP_STRIDE], ALU.mult))
            PROJ.taken(dve, "rope_kc")
            vec.tensor_tensor(kcT, kcT, kc_sin, ALU.add).then_inc(roped, 1)
            PROJ.taken(dve, "vwg")
            sigmoid(g_nsa)
            nsa_gate = g_nsa.rearrange("p t (h k) -> p k h t", k=3)

            for t in range(TT):
                PROJ.taken(dve, f"gg{t}")
                sigmoid(gle[:, t, :])
                link(vec.tensor_tensor(gle[:, t, :], gle[:, t, :], glg[:, t, :], ALU.mult))
            dve.wait_ge(la_log, 1)
            ps = PROJ.arrived(dve, "la")
            vec.tensor_scalar(gla_b[:, 0, :], ps[:, 0:S], cols[:, ROW_GLB:ROW_GLB + 1], 0.0, ALU.add, ALU.min)
            vec.tensor_scalar(gla_b[:, 1, :], ps[:, S:2 * S], cols[:, ROW_GLB + 1:ROW_GLB + 2], 0.0, ALU.add, ALU.min)\
                .then_inc(PROJ.free("la"), 1)
            PROJ.taken(dve, "la")
            link(vec.tensor_tensor(gla_t, gla_b, gla_t, ALU.subtract))
            for c in range(2):
                link(vec.tensor_tensor_scan(gla_b[:, c, :], K("ones"), gla_t[:, c, :], 0.0, ALU.mult, ALU.add))

            bias = K("cmp_bias").rearrange("p (t n) -> p t n", t=TT).unsqueeze(1).to_broadcast([P, 4, TT, N_CMP])
            seen = K("cmp_seen").rearrange("p (t n) -> p t n", t=TT).unsqueeze(1).to_broadcast([P, 4, TT, N_CMP])
            for g in range(2):
                ps = SC.arrived(dve, f"cmp{g}")
                pc, st = p_cmp[:, g], stat_cmp[:, g]
                wide = st.unsqueeze(3).to_broadcast([P, 4, TT, N_CMP])
                vec.tensor_tensor(pc, ps[:, 0:4 * TT * N_CMP].rearrange("p (c t n) -> p c t n", c=4, t=TT), bias, ALU.add)\
                    .then_inc(SC.free(f"cmp{g}"), 1)
                SC.taken(dve, f"cmp{g}")
                link(vec.tensor_reduce(st, pc, axis=AX.X, op=ALU.max))
                vec.tensor_tensor(pc, pc, wide, ALU.subtract).then_inc(cmp_in, 1)
                dve.wait_ge(cmp_exp, g + 1)
                link(vec.tensor_tensor(pc, pc, seen, ALU.mult))
                link(vec.tensor_reduce(st, pc, axis=AX.X, op=ALU.add))
                link(vec.tensor_scalar_max(st, st, 1e-30))
                link(vec.reciprocal(st, st))
                link(vec.tensor_tensor(st, st, nsa_gate[:, 0, 4 * g:4 * g + 4, :], ALU.mult))
                vec.tensor_tensor(pc, pc, wide, ALU.mult).then_inc(cmp_ready, 1)

            prepared = [0]

            def prepare(n):
                h, k = LEVELS[n], prepared[0]
                prepared[0] += 1
                b = gla_b.rearrange("p c s -> p (c s)").rearrange("p (n j) -> p n j", j=2 * h)
                d = lv_d[:, k % 2]
                vec.tensor_tensor(d.rearrange("p (n j) -> p n j", j=2 * h), b,
                                  b[:, :, h - 1:h].to_broadcast([P, 512 // (2 * h), 2 * h]), ALU.subtract).then_inc(lv_diff, 1)
                dve.wait_ge(lv_exp, k + 1)
                vec.tensor_tensor(lv_q[:, k % 2], glq.rearrange("p c s -> p (c s)"), d, ALU.mult)
                vec.tensor_tensor(lv_k[:, k % 2], glk.rearrange("p c s -> p (c s)"), d, ALU.mult).then_inc(lv_ready, 1)

            def merge(n):
                for par in range(2):
                    name = f"lv{n}_{par}"
                    ps = PT.arrived(dve, name)
                    if LEVELS[n] == P:
                        vec.tensor_copy(att[:, par, 2].rearrange("p c t -> p (c t)"), ps[:, 0:2 * P])\
                            .then_inc(PT.free(name), 1)
                    else:
                        vec.copy_predicated(att[:, par, 0:2].rearrange("p b c t -> p (b c) t"),
                                            level_mask[:, n - 1:n, :].to_broadcast([P, 4, P]),
                                            ps[:, :].rearrange("p (a t) -> p a t", a=4)).then_inc(PT.free(name), 1)
                PT.taken(dve, f"lv{n}_0", f"lv{n}_1")

            PROJ.taken(dve, "gq", "gk")
            prepare(0)
            prepare(2)
            merge(0)
            merge(1)
            for n in range(3, len(LEVELS)):
                prepare(n)
                merge(n - 1)
            merge(len(LEVELS) - 1)

            dve.wait_ge(small_in, 4 * 16)
            ps = PROJ.arrived(dve, "ff")
            vec.tensor_tensor(fox_t, ps[:, 0:TT * 8].rearrange("p (t h) -> p t h", t=TT),
                              fox_b.unsqueeze(1).to_broadcast([P, TT, 8]), ALU.add).then_inc(PROJ.free("ff"), 1)
            dve.wait_ge(fox_log, 1)
            vec.scalar_tensor_tensor(log_f, fox_t, 0.0, log_f, ALU.min, ALU.subtract).then_inc(fox_ready, 1)

            for t in range(TT):
                dve.wait_ge(gl_scale, t + 1)
                ps = OT.arrived(dve, f"go{t}")
                for h in range(GLA_H):
                    dv = slice(h * GLA_DV, (h + 1) * GLA_DV)
                    last = vec.scalar_tensor_tensor(gle[:, t, dv], ps[:, dv], gl_rstd[:, t, h:h + 1], gle[:, t, dv],
                                                    ALU.mult, ALU.mult)
                last.then_inc(OT.free(f"go{t}"), 1)

            for i in range(NJ):
                kind, c, par = jobs[i]
                if kind != "sb":
                    ps = SC.arrived(dve, f"s{i}")
                    vec.tensor_reduce(neg_max[:, i % 2, 0:1], ps[:, 0:P], axis=AX.X, op=ALU.max, negate=True)
                    vec.tensor_reduce(neg_max[:, i % 2, 1:2], ps[:, P:3 * P], axis=AX.X, op=ALU.max, negate=True)\
                        .then_inc(max_ready, 1)
                PROJ.taken(dve, f"g{i}")
                sigmoid(gates[:, i, :])
                if kind == "sb":
                    dve.wait_ge(sb_log, i - 23)
                    ps = SC.arrived(dve, f"s{i}")
                    vec.scalar_tensor_tensor(sb_p[:, i % 2], ps[:, 0:3 * P], 0.0, sb_u[:, i % 2], ALU.max, ALU.add)\
                        .then_inc(sb_soft, 1)
                    continue
                SC.taken(dve, f"s{i}")
                link(vec.reciprocal(total[:, i % 2], total[:, i % 2]))
                if kind != "fox":
                    branch_of = 1 if kind == "slc" else 2
                    link(vec.tensor_tensor(total[:, i % 2], total[:, i % 2], nsa_gate[:, branch_of, 4 * par + c, :], ALU.mult))
                vec.tensor_scalar(prob[:, i % 2, 0:P], prob[:, i % 2, 0:P], total[:, i % 2, 0:1], None, ALU.mult)
                vec.tensor_scalar(prob[:, i % 2, P:3 * P], prob[:, i % 2, P:3 * P], total[:, i % 2, 1:2], None, ALU.mult)\
                    .then_inc(prob_ready, 1)

            for n in range(4):
                for fc in range(KD // 2):
                    name = f"br{n}_{fc}"
                    ps = PROJ.arrived(dve, name)[:, :].rearrange("p (a b) -> p a b", a=2)
                    gate = gates[:, n * KD + 2 * fc:n * KD + 2 * fc + 2, :]
                    mixed = mixedT[:, 2 * fc:2 * fc + 2, :]
                    if n == 0:
                        vec.tensor_tensor(mixed, ps, gate, ALU.mult).then_inc(PROJ.free(name), 1)
                        continue
                    part = mix_t[:, fc % 2, :].rearrange("p (a b) -> p a b", a=2)
                    vec.tensor_tensor(part, ps, gate, ALU.mult).then_inc(PROJ.free(name), 1)
                    PROJ.taken(dve, name)
                    vec.tensor_tensor(mixed, mixed, part, ALU.add).then_inc(mixed_ready, 1)
                if n > 0:
                    dve.wait_ge(mixed_ready, 4 * n)
            for h in range(2):
                for t in range(TT):
                    ps = PROJ.arrived(dve, f"wo{h}{t}")
                    part = x[:, t, 512 * h:512 * h + 512]
                    vec.tensor_tensor(part, part, ps[:, :], ALU.add).then_inc(PROJ.free(f"wo{h}{t}"), 1)
            norm(2)
            for i in range(FFK // 2):
                PROJ.taken(dve, f"up{i}")
                part = hidden[:, 2 * i:2 * i + 2, :]
                vec.tensor_tensor(part, part, part, ALU.mult).then_inc(hidden_ready, 1)
            for t in range(TT):
                for h in range(2):
                    name = f"down{2 * t + h}"
                    bank = (SC, OT)[t]
                    ps = bank.arrived(dve, name)
                    part = x[:, t, 512 * h:512 * h + 512]
                    vec.tensor_tensor(part, part, ps[:, :], ALU.add).then_inc(bank.free(name), 1)


def prologue(nc, T, dram, sem, chip):
    x, consts, masks, cos, sin = (chip[n] for n in ("x", "consts", "masks", "cos", "sin"))
    work = Carver(chip["work"])
    pos, rows = work.take(S), work.take(P)
    cols, silu_c = chip["cols2"], chip["silu_c"]
    silu_t = work.take(2, KD)
    ident = consts[:, T["f32"]["ident"][0]:sum(T["f32"]["ident"])]
    angle, turns, part = work.take(S), work.take(S), work.take(S)
    tables_in, x_in = sem("tables_in"), sem("x_in")
    sin_arg, cos_arg = sem("sin_arg"), sem("cos_arg")
    sin_cos = sem("sin_cos")
    rows_in = sem("rows2_in")
    cols_full = sem("cols2_full")
    silu_exp = sem("silu_exp")
    pro_self, silu_done = sem("pro_self"), sem("silu_done")

    with nc.Block() as block:

        @block.sync
        def _(sp):
            sp.dma_start(pos.bitcast(I32), dram["positions"].partition_broadcast(P).rearrange("p b s -> p (b s)"))\
                .then_inc(tables_in, 16)
            sp.dma_start(consts[:, :], dram["f32_tables"]).then_inc(tables_in, 16)
            sp.dma_start(masks[:, :], dram["bf16_tables"]).then_inc(tables_in, 16)
            sp.dma_start(x, dram["x"].rearrange("b (t p) d -> p (b t) d", p=P)).then_inc(x_in, 16)
            sp.wait_ge(x_in, 16)

        @block.tensor
        def _(pe):
            pe.wait_ge(tables_in, 3 * 16)
            pe.wait_ge(rows_in, 9 * 16)
            nc.tensor.transpose(chip["psum"][0][:, 0:N_ROWS2], rows[0:N_ROWS2, :], ident[0:N_ROWS2, 0:N_ROWS2])\
                .then_inc(cols_full, 1)

        @block.vector
        def _(dve):
            link = Chain(dve, pro_self)
            vec = nc.vector
            inv = consts[:, T["f32"]["inv_freq"][0]:T["f32"]["inv_freq"][0] + 1]
            dve.wait_ge(tables_in, 3 * 16)
            link(vec.tensor_copy(angle, pos.bitcast(I32)))
            link(vec.tensor_scalar(angle, angle, inv, None, ALU.mult))
            link(vec.tensor_scalar(turns, angle, float(1 / (2 * np.pi)), None, ALU.mult))
            link(vec.tensor_scalar(turns, turns, MAGIC, None, ALU.add))
            link(vec.tensor_scalar(turns, turns, -MAGIC, None, ALU.add))
            for c in TWO_PI_PARTS:
                link(vec.scalar_tensor_tensor(angle, turns, -c, angle, ALU.mult, ALU.add))
            limit = 3.1415925
            vec.tensor_scalar(part, angle, limit, -limit, ALU.min, ALU.max).then_inc(sin_arg, 1)
            link(vec.tensor_scalar(angle, angle, float(np.pi / 2), None, ALU.add))
            link(vec.tensor_scalar(turns, angle, float(np.pi), float(-2 * np.pi), ALU.is_gt, ALU.mult))
            link(vec.tensor_tensor(angle, angle, turns, ALU.add))
            vec.tensor_scalar(angle, angle, limit, -limit, ALU.min, ALU.max).then_inc(cos_arg, 1)
            dve.wait_ge(silu_exp, 1)
            link(vec.tensor_scalar_add(silu_t, silu_t, 1.0))
            link(vec.reciprocal(silu_t, silu_t))
            vec.tensor_tensor(silu_c.rearrange("p k s -> p s k"), silu_t,
                              cols[:, ROW_C:N_ROWS2].rearrange("p (s k) -> p s k", s=2), ALU.mult)

        @block.scalar
        def _(act):
            def row_load(at, n, src, c0=0, width=P):
                act.dma_start(rows[at:at + n, c0:c0 + width], src).then_inc(rows_in, 16)

            row_load(ROW_ADA, 2 * MODC, dram["b_ada_2"].rearrange("l (r p) -> (l r) p", p=P))
            for half in range(2):
                row_load(ROW_QN, 1, dram["gqa_q_norm_2"], half * HD, HD)
                row_load(ROW_KN, 1, dram["gqa_k_norm_2"], half * HD, HD)
            row_load(ROW_MQN, 3, dram["mla_q_norm_2"].rearrange("l (r p) -> (l r) p", p=P))
            row_load(ROW_MKN, 2, dram["mla_kv_norm_2"].rearrange("l (r p) -> (l r) p", p=P))
            c_rows = dram["c_2"].rearrange("b (r p) -> (b r) p", p=P)
            row_load(ROW_C, KD, c_rows)
            act.dma_start(rows[ROW_C + KD:N_ROWS2, :], dram["c_ctx_2"].rearrange("(r p) -> r p", p=P)).then_inc(rows_in, 16)
            act.wait_ge(cols_full, 1)
            ps = chip["psum"][0]
            nc.scalar.activation(cols, ps[:, 0:N_ROWS2], ACT.Copy)
            nc.scalar.activation(silu_t, ps[:, ROW_C:N_ROWS2].rearrange("p (s k) -> p s k", s=2), ACT.Exp, scale=-1.0)\
                .then_inc(silu_exp, 1)
            act.wait_ge(sin_arg, 1)
            nc.scalar.activation(sin, part, ACT.Sin)
            act.wait_ge(cos_arg, 1)
            nc.scalar.activation(cos, angle, ACT.Sin)


def second_block(nc, T, dram, out, sem, chip):
    x, consts, mod, cols2 = chip["x"], chip["consts"], chip["mod"], chip["cols2"]
    work = Carver(chip["work"])

    xc = work.take(TT, D)
    hT = work.take(KD, 2 * S)
    gate_rows = work.take(2, D)
    ln_rows = work.take(2, D)
    grid = work.take(P + 2 * S)
    z = work.take(2, 512)
    ln_stats, ln_mv, ln_rs = work.take(4, 2, 6), work.take(4, 2), work.take(4)
    neg_max, total = work.take(6, 2), work.take(6, 2)
    nf_stat = work.take(TT)
    late = work.at
    gate_src = z.rearrange("p a b -> p (a b)").rearrange("p (k j) -> p k j", k=KD)
    grid_swap, grid_cos, grid_sin = grid[:, 0:P], grid[:, P:P + S], grid[:, P + S:P + 2 * S]
    g = Carver(chip["work"], late)
    g_qT = g.take(KD, 2 * S)
    g_kT = g.take(KV_HEADS, 2 * S)
    g_k = g.take(2, 2 * S)
    g_v = g.take(4, KV_HEADS * HD)
    g_prob, g_turn = g.take(6, 512), g.take(2, 6, S)
    g_yT = g.take(KD, 2 * S)
    g_sq, g_rs, g_rot = g_prob[:, 0:2], g_prob[:, 2:4], g_prob[:, 4, 0:S]
    hidden0 = Carver(chip["work"], late).take(FFK, 2 * S)
    nf_row, nf_junk = (g_yT.rearrange("p a b -> p (a b)")[:, n * D:(n + 1) * D] for n in range(2))
    m = Carver(chip["work"], late)
    m_kT = m.take(HEADS, 2 * S)
    m_qT = m.take(HEADS, S)
    m_v = m.take(4, HEADS * HD)
    m_cq, m_ckv = m.take(3, S), m.take(2, 2 * S)
    early = Carver(hT.rearrange("p a b -> p (a b)"))
    m_prob, m_turn = early.take(4, 512), early.take(2, 4, S)
    m_yT = xc.rearrange("p a b -> p (a b)").rearrange("p (c s) -> p c s", c=KD)
    flat_xc = xc.rearrange("p a b -> p (a b)")
    m_sqkv = flat_xc[:, 0:4 * S].rearrange("p (c s) -> p c s", c=2)
    m_sqq = flat_xc[:, 4 * S:7 * S].rearrange("p (c s) -> p c s", c=3)
    m_rskv, m_rsq = z[:, 0], z[:, 1, 0:S]
    m_kpe, m_rot = gate_rows[:, 1, 0:512], gate_rows[:, 1, 512:1024]
    hidden1 = Carver(chip["work"], late).take(FFK, S)

    tok = [x[:, 0, :], x[:, 1, :], xc[:, 0, :], xc[:, 1, :]]
    K = lambda name: consts[:, T["f32"][name][0]:sum(T["f32"][name])]
    ident, eps = K("ident"), K("eps")

    def mod_col(i, part, k, s):
        at = ((i * MOD_PARTS + part) * KD + k) * 2 + s
        return mod[:, at:at + 1]

    NT = [4, 2]
    UNITS = [3, 2]
    NORMED = 10
    XT_ORDER = [(2, 3, 0, 1), (0, 1, 2, 3)]
    UP_PER = [1, 2]
    GM_AT = [2, 5]

    def gate_fills(i, kind, s):
        return [f"{i}{kind}{s}{h}" for h in range(2)]

    proj, score, turned, outs = [], [], [], []
    for i in range(DEPTH):
        streams = NT[i] // TT
        proj += [f"{i}xT{t}{h}" for t in XT_ORDER[i] for h in range(2)]
        if i == 0:
            proj += ["0v0"] + gate_fills(0, "ga", 0) + ["0v1"] + gate_fills(0, "ga", 1)
            proj += [f"0a{n}" for n in range(NORMED)]
            score += [f"0ms{n}" for n in range(NORMED)]
            turned += [f"0rt{n}" for n in range(NORMED)]
        else:
            proj += ["1ckv0"] + gate_fills(1, "ga", 0) + ["1ckv1", "1kpe", "1cq0", "1cq1"]
            proj += [f"1kn{j}" for j in range(8)] + [f"1v{j}" for j in range(8)] + [f"1qf{j}" for j in range(8)]
            score += ["1mskv", "1msq"]
            turned += ["1rtk"] + [f"1rt{j}" for j in range(8)]
        units = [(h, u) for h in range(HEADS) for u in range(UNITS[i])]
        score += [f"{i}s{h}_{u}" for h, u in units]
        turned += [f"{i}t{h}_{u}" for h, u in units]
        outs += [f"{i}o{h}" for h in range(HEADS)] + [f"{i}wo{t}{h}" for t in range(NT[i]) for h in range(2)]
        proj += [f"{i}hT{t}{h}" for t in range(NT[i]) for h in range(2)]
        for n in range(FFK // UP_PER[i]):
            proj.append(f"{i}up{n}")
            for s in range(streams):
                if n == GM_AT[s]:
                    proj += gate_fills(i, "gm", s)
        score += [f"{i}down0{t}" for t in range(2)]
        outs += [f"{i}down0{t}" for t in range(2, NT[i])]
        turned += [f"{i}down1{t}" for t in range(2)]
        proj += [f"{i}down1{t}" for t in range(2, NT[i])]
    PROJ = Banks(sem, "proj2", chip["psum"][0:2], proj)
    SC = Banks(sem, "score2", chip["psum"][2:4], score)
    PT = Banks(sem, "turn2", chip["psum"][4:6], turned)
    OT = Banks(sem, "out2", chip["psum"][6:8], outs)

    def down_banks(h, t):
        return ((SC, OT), (PT, PROJ))[h][t // 2]

    whole = (slice(None), slice(None), slice(None))
    down_used = sem("down_used2")

    def chunked(a):
        return a.rearrange("(k p) n -> p k n", p=P)

    def done(bank, name):
        return bank.full, bank.order[name] + 1

    w_qkv, w_in = chunked(dram["gqa_w_qkv_2"][0]), chunked(dram["mla_w_in_2"][0])
    w_uq = chunked(dram["mla_w_uq_2"][0])
    w_ukv = dram["mla_w_ukv_2"][0].rearrange("(k p) (h e d) -> k e p h d", p=P, e=2, d=HD)
    qw, kvw = HEADS * HD, 2 * KV_HEADS * HD
    uq_half = HEADS * MLA_QK // 2
    tiles = [("0kv", KD, kvw, [(whole, w_qkv[:, :, qw:qw + kvw])], done(PROJ, "0a1"))]
    tiles += [(f"0q{j}", KD, 512, [(whole, w_qkv[:, :, 512 * j:512 * j + 512])], done(PROJ, f"0a{4 * j + 5}"))
              for j in range(2)]
    for i in range(DEPTH):
        if i == 1:
            tiles += [("1ckv", KD, KV_RANK + PE_DIM, [(whole, w_in[:, :, Q_RANK:])], done(PROJ, "1kpe")),
                      ("1cq", KD, Q_RANK, [(whole, w_in[:, :, 0:Q_RANK])], done(PROJ, "1cq1")),
                      ("1ukv", 4, HEADS * HD, [((slice(None), 2 * e + k, slice(None)), w_ukv[k, e])
                                               for e in range(2) for k in range(2)], done(PROJ, "1v7"))]
            tiles += [(f"1uq{j}", 3, uq_half, [(whole, w_uq[:, :, uq_half * j:uq_half * (j + 1)])],
                       done(PROJ, f"1qf{4 * j + 3}")) for j in range(2)]
        w_o = chunked(dram[("gqa_w_o_2", "mla_w_o_2")[i]][0])
        w1, w2 = chunked(dram["mlp_w1_2"][i]), chunked(dram["mlp_w2_2"][i])
        last = NT[i] - 1
        tiles += [(f"{i}wo{h}", KD, 512, [(whole, w_o[:, :, 512 * h:512 * h + 512])], done(OT, f"{i}wo{last}{h}"))
                  for h in range(2)]
        tiles += [(f"{i}up{j}", KD, 512, [(whole, w1[:, :, 512 * j:512 * j + 512])],
                   done(PROJ, f"{i}up{(4 * j + 3) // UP_PER[i]}")) for j in range(8)]
        tiles += [(f"{i}down{h}{j}", KD, 512, [(whole, w2[:, KD * j:KD * j + KD, 512 * h:512 * h + 512])],
                   (down_used, 6 * i + 3 * h + j + 1) if j < 3 else done(down_banks(h, last), f"{i}down{h}{last}"))
                  for h in range(2) for j in range(4)]
    W = Weights(sem, "w2", chip["ring"], tiles)

    first_in = sem("first_in")
    grid_in = sem("grid_in")
    ln_in = sem("ln_in")
    out_in = sem("out_done")
    nf_scale = sem("nf_scale")
    x_first = sem("x_first")
    mod_ready = sem("mod_ready")
    gate_wide = sem("gate_wide")
    rs_ready = sem("rs_ready")
    normed = sem("normed")
    roped = sem("roped2")
    k_copied = sem("k_copied")
    max_ready = sem("max_ready2")
    prob_ready = sem("prob_ready2")
    var_ready = sem("var_ready")
    ln_scale = sem("ln_scale")
    x_ready = sem("x_ready")
    hidden_ready = sem("hidden_ready2")
    kpe_ready = sem("kpe_ready")
    kpe_zero = sem("kpe_zero")
    act_self, dve_self = sem("act_self2"), sem("dve_self2")

    ln_order = [(i, j, t) for i in range(DEPTH) for j in range(2) for t in range(NT[i])]
    ln_count = {key: n + 1 for n, key in enumerate(ln_order)}
    gate_order = [(i, kind, s) for i in range(DEPTH) for kind in ("ga", "gm") for s in range(NT[i] // TT)]
    gate_count = {key: n + 1 for n, key in enumerate(gate_order)}
    unit_base = [0, HEADS * UNITS[0]]
    up_base = [0, FFK]

    def unit(i, h, u):
        return unit_base[i] + h * UNITS[i] + u

    def buffers(i):
        return ((g_prob, g_turn, g_yT, hidden0, 2 * S), (m_prob, m_turn, m_yT, hidden1, S))[i]

    def x_arrived(eng, i, t):
        if i == 1:
            eng.wait_ge(x_ready, ln_count[0, 1, t])
        elif t < TT:
            eng.wait_ge(x_first, t + 1)
        else:
            eng.wait_ge(first_in, 5 * 16)

    with nc.Block() as block:

        @block.sync
        def _(sp):
            W.load(sp)
            for t in range(TT):
                sp.wait_ge(x_ready, ln_count[1, 1, t])
                sp.dma_start(out.rearrange("b (t p) d -> p (b t) d", p=P)[:, t, :], x[:, t, :]).then_inc(out_in, 16)
            sp.wait_ge(out_in, TT * 16)

        @block.tensor
        def _(pe):
            def mm(o, lhsT, rhs, start, stop):
                return nc.tensor.matmul(o, lhsT, rhs, start=start, stop=stop)

            def turn(o, src):
                return nc.tensor.transpose(o, src, ident)

            def turn_tile(names, t):
                for h, name in enumerate(names):
                    ps = PROJ.claim(pe, name)
                    for k in range(4):
                        last = turn(ps[:, k * P:k * P + P], tok[t][:, (4 * h + k) * P:(4 * h + k + 1) * P])
                    last.then_inc(PROJ.full, 1)

            def turn_gate(i, kind, s):
                pe.wait_ge(gate_wide, gate_count[i, kind, s])
                for h, name in enumerate(gate_fills(i, kind, s)):
                    ps = PROJ.claim(pe, name)
                    for k in range(4):
                        last = turn(ps[:, k * P:k * P + P], gate_src[:, 4 * h + k, :])
                    last.then_inc(PROJ.full, 1)

            def gemm_T(o, w, cols, n=2 * S, chunks=KD, src=None):
                src = hT if src is None else src
                for k in range(chunks):
                    last = mm(o, w[:, k, cols], src[:, k, 0:n], k == 0, k == chunks - 1)
                return last

            def gqa_project():
                w = W.arrived(pe, "0kv")
                kw = KV_HEADS * HD
                for j in range(2):
                    ps = PROJ.claim(pe, f"0v{j}")
                    for b in range(2):
                        for k in range(KD):
                            t = 2 * j + b
                            last = mm(ps[:, b * kw:(b + 1) * kw], hT[:, k, t * P:t * P + P], w[:, k, kw:2 * kw],
                                      k == 0, k == KD - 1)
                    last.then_inc(PROJ.full, 1)
                    turn_gate(0, "ga", j)
                for n in range(NORMED + 2):
                    if n < NORMED:
                        if n >= 2 and n % 4 == 2:
                            w = W.arrived(pe, f"0q{n // 4}")
                        c = n if n < 2 else (n - 2) % 4
                        gemm_T(PROJ.claim(pe, f"0a{n}")[:, :], w, slice(c * P, c * P + P)).then_inc(PROJ.full, 1)
                    if 1 <= n <= NORMED:
                        PROJ.taken(pe, f"0a{n - 1}")
                        mm(SC.claim(pe, f"0ms{n - 1}")[:, :], K("head_mean"), g_sq[:, (n - 1) % 2], True, True)\
                            .then_inc(SC.full, 1)
                    if n >= 2:
                        pe.wait_ge(normed, n - 1)
                        raw = g_k[:, n - 2] if n < 4 else g_qT[:, n - 4]
                        mm(PT.claim(pe, f"0rt{n - 2}")[:, 0:S], grid_swap, raw[:, 0:S], True, True).then_inc(PT.full, 1)

            def mla_project():
                w = W.arrived(pe, "1ckv")
                for j in range(2):
                    gemm_T(PROJ.claim(pe, f"1ckv{j}")[:, :], w, slice(j * P, j * P + P)).then_inc(PROJ.full, 1)
                    if j == 0:
                        turn_gate(1, "ga", 0)
                gemm_T(PROJ.claim(pe, "1kpe")[HD:MLA_QK, :], w, slice(KV_RANK, KV_RANK + PE_DIM)).then_inc(PROJ.full, 1)
                w = W.arrived(pe, "1cq")
                for j in range(2):
                    ps = PROJ.claim(pe, f"1cq{j}")
                    for b in range(2 - j):
                        c = 2 * j + b
                        last = gemm_T(ps[:, b * S:b * S + S], w, slice(c * P, c * P + P), S)
                    last.then_inc(PROJ.full, 1)
                PROJ.taken(pe, "1ckv0", "1ckv1")
                ps = SC.claim(pe, "1mskv")
                for c in range(2):
                    last = mm(ps[:, :], K("ones")[:, 0:P], m_sqkv[:, c, :], c == 0, c == 1)
                last.then_inc(SC.full, 1)
                PROJ.taken(pe, "1cq0", "1cq1")
                ps = SC.claim(pe, "1msq")
                for c in range(3):
                    last = mm(ps[:, 0:S], K("ones")[:, 0:P], m_sqq[:, c, :], c == 0, c == 2)
                last.then_inc(SC.full, 1)
                PROJ.taken(pe, "1kpe")
                pe.wait_ge(kpe_zero, 1)
                pe.wait_ge(grid_in, 16)
                mm(PT.claim(pe, "1rtk")[0:MLA_QK, 0:S], grid_swap[0:MLA_QK, 0:MLA_QK], m_kpe[0:MLA_QK, 0:S], True, True)\
                    .then_inc(PT.full, 1)
                w = W.arrived(pe, "1ukv")
                pe.wait_ge(normed, NORMED + 1)
                for j in range(8):
                    gemm_T(PROJ.claim(pe, f"1kn{j}")[:, :], w[:, 0:2], slice(j * P, j * P + P), chunks=2, src=m_ckv)\
                        .then_inc(PROJ.full, 1)
                for j in range(8):
                    ps = PROJ.claim(pe, f"1v{j}")
                    for c in range(2):
                        last = mm(ps[:, :], m_ckv[:, c, (j // 2) * P:(j // 2 + 1) * P],
                                  w[:, 2 + c, 512 * (j % 2):512 * (j % 2) + 512], c == 0, c == 1)
                    last.then_inc(PROJ.full, 1)
                pe.wait_ge(normed, NORMED + 2)
                for j in range(9):
                    if j < 8:
                        if j % 4 == 0:
                            w = W.arrived(pe, f"1uq{j // 4}")
                        ps = PROJ.claim(pe, f"1qf{j}")
                        for b in range(2):
                            at = (2 * j + b) % 8 * MLA_QK
                            last = gemm_T(ps[0:MLA_QK, b * S:b * S + S], w, slice(at, at + MLA_QK), S, 3, m_cq)
                        last.then_inc(PROJ.full, 1)
                    if j >= 1:
                        PROJ.taken(pe, f"1qf{j - 1}")
                        mm(PT.claim(pe, f"1rt{j - 1}")[0:MLA_QK, :], grid_swap[0:MLA_QK, 0:MLA_QK],
                           m_qT[0:MLA_QK, 2 * j - 2:2 * j, :].rearrange("p a b -> p (a b)"), True, True).then_inc(PT.full, 1)

            def operands(i, h):
                if i == 0:
                    rows, kv = slice(h % 2 * HD, h % 2 * HD + HD), h // (HEADS // KV_HEADS)
                    return g_qT[rows, h // 2, :], g_kT[rows, kv, :], g_v[:, :, kv * HD:kv * HD + HD]
                return m_qT[0:MLA_QK, h, :], m_kT[0:MLA_QK, h, :], m_v[:, :, h * HD:h * HD + HD]

            def attention(i):
                prob, turned_p = buffers(i)[0:2]
                U = UNITS[i]
                for h in range(HEADS + 2):
                    for u in range(U):
                        if h < HEADS:
                            q, k, _ = operands(i, h)
                            if u == 0:
                                pe.wait_ge(roped, (3 if i == 0 else NORMED + 1) + h // 2)
                            ps = SC.claim(pe, f"{i}s{h}_{u}")
                            if u < 2:
                                last = mm(ps[:, :], q[:, u * P:u * P + P], k, True, True)
                            else:
                                for t in range(TT):
                                    last = mm(ps[:, t * S:t * S + S], q[:, S + t * P:S + t * P + P], k[:, S:2 * S], True, True)
                            last.then_inc(SC.full, 1)
                        if 1 <= h <= HEADS:
                            n = unit(i, h - 1, u)
                            src = prob[:, ((h - 1) * U + u) % (2 * U)]
                            pe.wait_ge(prob_ready, n + 1)
                            ps = PT.claim(pe, f"{i}t{h - 1}_{u}")
                            for b in range(4):
                                at = b if u < 2 else b % 2 * 2 + b // 2
                                last = turn(ps[:, b * P:b * P + P], src[:, at * P:at * P + P])
                            last.then_inc(PT.full, 1)
                    if h >= 2:
                        v = operands(i, h - 2)[2]
                        half = slice((h - 2) % 2 * HD, (h - 2) % 2 * HD + HD)
                        PT.taken(pe, *[f"{i}t{h - 2}_{u}" for u in range(U)])
                        ps = OT.claim(pe, f"{i}o{h - 2}")
                        keys = turned_p[:, (h - 2) % 2]
                        for b in range(4):
                            last = mm(ps[half, 0:S], v[:, b, :], keys[:, b, :], b == 0, b == 3)
                        if U == 3:
                            for b in range(2):
                                last = mm(ps[half, S:2 * S], v[:, 2 + b, :], keys[:, 4 + b, :], b == 0, b == 1)
                        last.then_inc(OT.full, 1)

            for i in range(DEPTH):
                yT, hidden, n_tok = buffers(i)[2:]
                for t in XT_ORDER[i]:
                    x_arrived(pe, i, t)
                    turn_tile([f"{i}xT{t}{h}" for h in range(2)], t)
                PROJ.taken(pe, *[f"{i}xT{t}{h}" for t in XT_ORDER[i] for h in range(2)])
                if i == 0:
                    gqa_project()
                    pe.wait_ge(k_copied, 8)
                else:
                    mla_project()
                    pe.wait_ge(k_copied, 12)
                attention(i)

                OT.taken(pe, f"{i}o{HEADS - 2}", f"{i}o{HEADS - 1}")
                w = [W.arrived(pe, f"{i}wo{h}") for h in range(2)]
                for t in range(NT[i] + 1):
                    if t < NT[i]:
                        for h in range(2):
                            ps = OT.claim(pe, f"{i}wo{t}{h}")
                            for c in range(KD):
                                last = mm(ps[:, :], yT[:, c, t * P:t * P + P], w[h][:, c, :], c == 0, c == KD - 1)
                            last.then_inc(OT.full, 1)
                    if t >= 1:
                        pe.wait_ge(x_ready, ln_count[i, 0, t - 1])
                        turn_tile([f"{i}hT{t - 1}{h}" for h in range(2)], t - 1)

                PROJ.taken(pe, *[f"{i}hT{t}{h}" for t in range(NT[i]) for h in range(2)])
                per = UP_PER[i]
                for n in range(FFK // per):
                    if n * per % 4 == 0:
                        w = W.arrived(pe, f"{i}up{n * per // 4}")
                    ps = PROJ.claim(pe, f"{i}up{n}")
                    for b in range(per):
                        at = (n * per + b) % 4 * P
                        last = gemm_T(ps[:, b * n_tok:(b + 1) * n_tok], w, slice(at, at + P), n_tok)
                    last.then_inc(PROJ.full, 1)
                    for s in range(NT[i] // TT):
                        if n == GM_AT[s]:
                            turn_gate(i, "gm", s)
                for h in range(2):
                    for j in range(4):
                        w = W.arrived(pe, f"{i}down{h}{j}")
                        for t in range(NT[i]):
                            banks, name = down_banks(h, t), f"{i}down{h}{t}"
                            ps = banks.claim(pe, name) if j == 0 else banks.bank(name)
                            for k in range(KD):
                                c = KD * j + k
                                if t == 0:
                                    pe.wait_ge(hidden_ready, up_base[i] + c // per + 1)
                                last = mm(ps[:, :], hidden[:, c, t * P:t * P + P], w[:, k, :], c == 0, c == FFK - 1)
                            if j == 3:
                                last.then_inc(banks.full, 1)
                        if j < 3:
                            last.then_inc(down_used, 1)

        @block.scalar
        def _(act):
            f = nc.scalar.activation
            link = Chain(act, act_self)

            def copy(o, src, **kw):
                return f(o, src, ACT.Copy, **kw)

            def modulate(i, name, t, part):
                ps = PROJ.arrived(act, name)
                for k in range(4):
                    last = f(hT[:, k, t * P:t * P + P], ps[:, k * P:k * P + P], ACT.Identity,
                             scale=mod_col(i, part + 1, k, t // TT), bias=mod_col(i, part, k, t // TT))
                last.then_inc(PROJ.free(name), 1)

            def take_gate(i, kind, s):
                for h, name in enumerate(gate_fills(i, kind, s)):
                    ps = PROJ.arrived(act, name)
                    copy(gate_rows[:, s, 512 * h:512 * h + 512], ps[:, :]).then_inc(PROJ.free(name), 1)

            def scale_of(banks, name, part, o, mean):
                ps = banks.arrived(act, name)
                f(o, ps[:, 0:o.shape[1]], ACT.Ln, scale=mean, bias=eps).then_inc(banks.free(name), 1)
                banks.taken(act, name)
                f(o, o, ACT.Exp, scale=-0.5).then_inc(rs_ready, 1)

            def gqa_project():
                for j in range(2):
                    ps = PROJ.arrived(act, f"0v{j}")
                    copy(g_v[:, 2 * j:2 * j + 2, :].rearrange("p a b -> p (a b)"), ps[:, :]).then_inc(PROJ.free(f"0v{j}"), 1)
                    take_gate(0, "ga", j)
                for n in range(NORMED + 1):
                    if n < NORMED:
                        ps = PROJ.arrived(act, f"0a{n}")
                        copy(g_k[:, n] if n < 2 else g_qT[:, n - 2], ps[:, :])
                        f(g_sq[:, n % 2], ps[:, :], ACT.Square).then_inc(PROJ.free(f"0a{n}"), 1)
                    if n >= 1:
                        if n >= 3:
                            act.wait_ge(normed, n - 2)
                        scale_of(SC, f"0ms{n - 1}", None, g_rs[:, (n - 1) % 2], 1.0)

            def mla_project():
                for j in range(2):
                    ps = PROJ.arrived(act, f"1ckv{j}")
                    copy(m_ckv[:, j, :], ps[:, :])
                    f(m_sqkv[:, j, :], ps[:, :], ACT.Square).then_inc(PROJ.free(f"1ckv{j}"), 1)
                    if j == 0:
                        take_gate(1, "ga", 0)
                ps = PROJ.arrived(act, "1kpe")
                copy(m_kpe[HD:MLA_QK, :], ps[HD:MLA_QK, :]).then_inc(PROJ.free("1kpe"), 1)
                for j in range(2):
                    ps = PROJ.arrived(act, f"1cq{j}")
                    n = (2 - j) * S
                    copy(m_cq[:, 2 * j:2 * j + 2 - j, :].rearrange("p a b -> p (a b)"), ps[:, 0:n])
                    f(m_sqq[:, 2 * j:2 * j + 2 - j, :].rearrange("p a b -> p (a b)"), ps[:, 0:n], ACT.Square)\
                        .then_inc(PROJ.free(f"1cq{j}"), 1)
                scale_of(SC, "1mskv", None, m_rskv, 1.0 / KV_RANK)
                scale_of(SC, "1msq", None, m_rsq, 1.0 / Q_RANK)
                for j in range(0, 8, 2):
                    ps = PROJ.arrived(act, f"1kn{j}")
                    copy(m_kT[0:HD, 2 * j, :], ps[0:HD, :])
                    copy(m_kT[0:HD, 2 * j + 1, :], ps[HD:P, :]).then_inc(PROJ.free(f"1kn{j}"), 1)
                for j in range(0, 8, 2):
                    ps = PROJ.arrived(act, f"1v{j}")
                    copy(m_v[:, j // 2, 0:512], ps[:, :]).then_inc(PROJ.free(f"1v{j}"), 1)
                for j in range(8):
                    ps = PROJ.arrived(act, f"1qf{j}")
                    copy(m_qT[0:MLA_QK, 2 * j:2 * j + 2, :].rearrange("p a b -> p (a b)"), ps[0:MLA_QK, :],
                         scale=MLA_QK ** -0.5).then_inc(PROJ.free(f"1qf{j}"), 1)

            def attention(i):
                prob, turned_p, yT = buffers(i)[0:3]
                U = UNITS[i]
                for h in range(HEADS + 2):
                    for u in range(U):
                        if h < HEADS:
                            n = unit(i, h, u)
                            slot = (h * U + u) % (2 * U)
                            act.wait_ge(max_ready, n + 1)
                            ps = SC.arrived(act, f"{i}s{h}_{u}")
                            for t in range(1 if u < 2 else TT):
                                part = slice(0, 512) if u < 2 else slice(t * S, t * S + S)
                                last = f(prob[:, slot, part], ps[:, part], ACT.Exp, bias=neg_max[:, slot, t:t + 1],
                                         accum_out=total[:, slot, t:t + 1])
                            last.then_inc(SC.free(f"{i}s{h}_{u}"), 1)
                        if 1 <= h <= HEADS:
                            name = f"{i}t{h - 1}_{u}"
                            ps = PT.arrived(act, name)
                            keys = turned_p[:, (h - 1) % 2]
                            if u < 2:
                                o, src = keys[:, 0:4, u * P:u * P + P], ps[:, :].rearrange("p (b t) -> p b t", b=4)
                            else:
                                o, src = keys[:, 4:6, :].rearrange("p a b -> p (a b)"), ps[:, :]
                            copy(o, src).then_inc(PT.free(name), 1)
                    if h >= 2:
                        half = slice((h - 2) % 2 * HD, (h - 2) % 2 * HD + HD)
                        ps = OT.arrived(act, f"{i}o{h - 2}")
                        n = yT.shape[2]
                        copy(yT[half, (h - 2) // 2, :], ps[half, 0:n]).then_inc(OT.free(f"{i}o{h - 2}"), 1)

            def ln_rstd(i, j, t):
                act.wait_ge(var_ready, ln_count[i, j, t])
                link(f(ln_rs[:, t:t + 1], ln_mv[:, t, 1:2], ACT.Ln, bias=eps))
                f(ln_rs[:, t:t + 1], ln_rs[:, t:t + 1], ACT.Exp, scale=-0.5).then_inc(ln_scale, 1)

            act.dma_start(nf_row, dram["norm_final"].partition_broadcast(P)).then_inc(first_in, 16)
            act.dma_start(xc, dram["ctx_2"].rearrange("b (t p) d -> p (b t) d", p=P)).then_inc(first_in, 16)
            act.dma_start(grid, dram["grid_gqa"]).then_inc(first_in, 16)
            for n, name in enumerate(("ln_g_2", "ln_b_2")):
                act.dma_start(ln_rows[:, n, :], dram[name][0, 0].partition_broadcast(P)).then_inc(first_in, 16)
            for t in range(TT):
                link(f(nf_junk, x[:, t, :], ACT.Square, accum_out=nf_stat[:, t:t + 1]))
            link(f(nf_stat, nf_stat, ACT.Ln, scale=1.0 / D, bias=eps))
            f(nf_stat, nf_stat, ACT.Exp, scale=-0.5).then_inc(nf_scale, 1)
            act.wait_ge(mod_ready, 1)
            for i in range(DEPTH):
                hidden, n_tok = buffers(i)[3:]
                for t in XT_ORDER[i]:
                    modulate(i, f"{i}xT{t}0", t, 0)
                (gqa_project, mla_project)[i]()
                attention(i)
                for t in range(NT[i] + 1):
                    if t < NT[i]:
                        ln_rstd(i, 0, t)
                    if t >= 1:
                        modulate(i, f"{i}hT{t - 1}0", t - 1, 3)
                per = UP_PER[i]
                for n in range(FFK // per):
                    ps = PROJ.arrived(act, f"{i}up{n}")
                    f(hidden[:, n * per:(n + 1) * per, :].rearrange("p a b -> p (a b)"), ps[:, :], ACT.Relu)\
                        .then_inc(PROJ.free(f"{i}up{n}"), 1)
                    for s in range(NT[i] // TT):
                        if n == GM_AT[s]:
                            take_gate(i, "gm", s)
                for t in range(NT[i]):
                    ln_rstd(i, 1, t)

        @block.vector
        def _(dve):
            link = Chain(dve, dve_self)
            vec = nc.vector

            def widen(i, kind, s):
                part = {"ga": 2, "gm": 5}[kind]
                at = (i * MOD_PARTS + part) * KD * 2
                src = mod[:, at:at + 2 * KD].rearrange("p (k s) -> p k s", s=2)[:, :, s:s + 1]
                if gate_count[i, kind, s] > 1:
                    i0, kind0, s0 = gate_order[gate_count[i, kind, s] - 2]
                    PROJ.taken(dve, *gate_fills(i0, kind0, s0))
                vec.tensor_copy(gate_src, src.to_broadcast([P, KD, P])).then_inc(gate_wide, 1)
                dve.wait_ge(gate_wide, gate_count[i, kind, s])

            def modulate(i, name, t, part):
                ps = PROJ.arrived(dve, name)
                for k in range(4):
                    last = vec.tensor_scalar(hT[:, 4 + k, t * P:t * P + P], ps[:, k * P:k * P + P],
                                             mod_col(i, part + 1, 4 + k, t // TT), mod_col(i, part, 4 + k, t // TT),
                                             ALU.mult, ALU.add)
                last.then_inc(PROJ.free(name), 1)

            def residual(t, h, banks, name):
                ps = banks.arrived(dve, name)
                half = slice(512 * h, 512 * h + 512)
                vec.tensor_tensor(z[:, h, :], ps[:, :], gate_rows[:, t // TT, half], ALU.mult).then_inc(banks.free(name), 1)
                banks.taken(dve, name)
                link(vec.scalar_tensor_tensor(tok[t][:, half], tok[t][:, half], ALPHA, z[:, h, :], ALU.mult, ALU.add))

            def layer_norm(i, j, t):
                n, xt = ln_count[i, j, t], tok[t]
                for h in range(2):
                    link(vec.bn_stats(ln_stats[:, t, h, :], xt[:, 512 * h:512 * h + 512]))
                vec.bn_aggr(ln_mv[:, t, :], ln_stats[:, t]).then_inc(var_ready, 1)
                dve.wait_ge(var_ready, n)
                if i + j > 0:
                    dve.wait_ge(ln_in, 32 * (2 * i + j))
                link(vec.scalar_tensor_tensor(xt, xt, ln_mv[:, t, 0:1], ln_rows[:, 0, :], ALU.subtract, ALU.mult))
                dve.wait_ge(ln_scale, n)
                vec.scalar_tensor_tensor(xt, xt, ln_rs[:, t:t + 1], ln_rows[:, 1, :], ALU.mult, ALU.add).then_inc(x_ready, 1)

            def rotate(part, name, rows, sin_of, cos_of, tmp, rt):
                ps = PT.arrived(dve, name)
                vec.tensor_tensor(tmp, rt(ps), sin_of, ALU.mult).then_inc(PT.free(name), 1)
                link(vec.tensor_tensor(part, part, cos_of, ALU.mult))
                PT.taken(dve, name)
                return vec.tensor_tensor(part, part, tmp, ALU.add)

            def gqa_project():
                for n in range(NORMED + 1):
                    if n < NORMED:
                        raw = g_k[:, n] if n < 2 else g_qT[:, n - 2]
                        gain = cols2[:, ROW_KN:ROW_KN + 1] if n < 2 else cols2[:, ROW_QN:ROW_QN + 1]
                        dve.wait_ge(rs_ready, n + 1)
                        vec.scalar_tensor_tensor(raw, raw, gain, g_rs[:, n % 2], ALU.mult, ALU.mult).then_inc(normed, 1)
                    if n >= 1:
                        raw = g_k[:, n - 1] if n < 3 else g_qT[:, n - 3]
                        dve.wait_ge(normed, n)
                        if n >= 2:
                            dve.wait_ge(roped, n - 1)
                        rotate(raw[:, 0:S], f"0rt{n - 1}", None, grid_sin, grid_cos, g_rot, lambda ps: ps[:, 0:S])\
                            .then_inc(roped, 1)

            def mla_project():
                vec.memset(m_kpe[0:HD, :], 0.0).then_inc(kpe_zero, 1)
                pe_rows = slice(HD, MLA_QK)
                dve.wait_ge(rs_ready, NORMED + 1)
                for c in range(2):
                    last = vec.scalar_tensor_tensor(m_ckv[:, c, :], m_ckv[:, c, :], cols2[:, ROW_MKN + c:ROW_MKN + c + 1],
                                                    m_rskv, ALU.mult, ALU.mult)
                last.then_inc(normed, 1)
                dve.wait_ge(rs_ready, NORMED + 2)
                for c in range(3):
                    last = vec.scalar_tensor_tensor(m_cq[:, c, :], m_cq[:, c, :], cols2[:, ROW_MQN + c:ROW_MQN + c + 1],
                                                    m_rsq, ALU.mult, ALU.mult)
                last.then_inc(normed, 1)
                dve.wait_ge(grid_in, 16)
                rotate(m_kpe[pe_rows, 0:S], "1rtk", None, grid_sin[pe_rows, :], grid_cos[pe_rows, :], m_rot[pe_rows, 0:S],
                       lambda ps: ps[pe_rows, 0:S]).then_inc(kpe_ready, 1)
                dve.wait_ge(kpe_ready, 1)
                for j in range(1, 8, 2):
                    ps = PROJ.arrived(dve, f"1kn{j}")
                    vec.tensor_copy(m_kT[0:HD, 2 * j, :], ps[0:HD, :])
                    vec.tensor_copy(m_kT[0:HD, 2 * j + 1, :], ps[HD:P, :]).then_inc(PROJ.free(f"1kn{j}"), 1)
                for j in range(1, 8, 2):
                    ps = PROJ.arrived(dve, f"1v{j}")
                    vec.tensor_copy(m_v[:, j // 2, 512:1024], ps[:, :]).then_inc(PROJ.free(f"1v{j}"), 1)
                wide = lambda a: a[pe_rows, :].unsqueeze(1).to_broadcast([PE_DIM, 2, S])
                for j in range(8):
                    if j >= 1:
                        dve.wait_ge(roped, NORMED + j)
                    rotate(m_qT[pe_rows, 2 * j:2 * j + 2, :], f"1rt{j}", None, wide(grid_sin), wide(grid_cos),
                           m_rot[pe_rows, :].rearrange("p (a b) -> p a b", a=2),
                           lambda ps: ps[pe_rows, :].rearrange("p (a b) -> p a b", a=2)).then_inc(roped, 1)

            def attention(i):
                prob, U = buffers(i)[0], UNITS[i]
                order = [(h, u) for h in range(HEADS) for u in range(U)]
                for n in range(len(order) + 1):
                    if n < len(order):
                        h, u = order[n]
                        slot = n % (2 * U)
                        ps = SC.arrived(dve, f"{i}s{h}_{u}")
                        if u < 2:
                            last = vec.tensor_reduce(neg_max[:, slot, 0:1], ps[:, :], axis=AX.X, op=ALU.max, negate=True)
                        else:
                            last = vec.tensor_reduce(neg_max[:, slot, :], ps[:, :].rearrange("p (t k) -> p t k", t=TT),
                                                     axis=AX.X, op=ALU.max, negate=True)
                        last.then_inc(max_ready, 1)
                    if n >= 1:
                        h, u = order[n - 1]
                        slot = (n - 1) % (2 * U)
                        tiles_of = 1 if u < 2 else TT
                        SC.taken(dve, f"{i}s{h}_{u}")
                        link(vec.reciprocal(total[:, slot, 0:tiles_of], total[:, slot, 0:tiles_of]))
                        for t in range(tiles_of):
                            part = slice(0, 512) if u < 2 else slice(t * S, t * S + S)
                            last = vec.tensor_scalar(prob[:, slot, part], prob[:, slot, part], total[:, slot, t:t + 1],
                                                     None, ALU.mult)
                        last.then_inc(prob_ready, 1)

            every = mod[:, :].rearrange("p (n s) -> p n s", s=2)
            link(vec.tensor_tensor(every, every, cols2[:, ROW_ADA:ROW_ADA + DEPTH * MODC].unsqueeze(2)
                                   .to_broadcast([P, DEPTH * MODC, 2]), ALU.add))
            scales = mod[:, :].rearrange("p (l m n) -> p l m n", l=2 * DEPTH, m=3)[:, :, 1, :]
            vec.tensor_scalar_add(scales, scales, 1.0).then_inc(mod_ready, 1)
            dve.wait_ge(mod_ready, 1)
            link(vec.tensor_scalar(cols2[:, ROW_QN:ROW_QN + 1], cols2[:, ROW_QN:ROW_QN + 1], HD ** -0.5, None, ALU.mult))
            widen(0, "ga", 0)
            dve.wait_ge(first_in, 5 * 16)
            dve.wait_ge(nf_scale, 1)
            for t in range(TT):
                vec.scalar_tensor_tensor(x[:, t, :], x[:, t, :], nf_stat[:, t:t + 1], nf_row, ALU.mult, ALU.mult)\
                    .then_inc(x_first, 1)
            for i in range(DEPTH):
                hidden, n_tok = buffers(i)[3:]
                if i == 1:
                    widen(1, "ga", 0)
                for t in XT_ORDER[i]:
                    modulate(i, f"{i}xT{t}1", t, 0)
                if i == 0:
                    widen(0, "ga", 1)
                (gqa_project, mla_project)[i]()
                attention(i)
                PROJ.taken(dve, *gate_fills(i, "ga", NT[i] // TT - 1))
                for t in range(NT[i] + 1):
                    if t < NT[i]:
                        for h in range(2):
                            residual(t, h, OT, f"{i}wo{t}{h}")
                        layer_norm(i, 0, t)
                    if t >= 1:
                        modulate(i, f"{i}hT{t - 1}1", t - 1, 3)
                widen(i, "gm", 0)
                per = UP_PER[i]
                for n in range(FFK // per):
                    PROJ.taken(dve, f"{i}up{n}")
                    part = hidden[:, n * per:(n + 1) * per, :]
                    vec.tensor_tensor(part, part, part, ALU.mult).then_inc(hidden_ready, 1)
                    if n == GM_AT[0] and NT[i] > TT:
                        widen(i, "gm", 1)
                PROJ.taken(dve, *gate_fills(i, "gm", NT[i] // TT - 1))
                for h in range(2):
                    for t in range(NT[i]):
                        residual(t, h, down_banks(h, t), f"{i}down{h}{t}")
                        if h == 1:
                            layer_norm(i, 1, t)

        @block.gpsimd
        def _(pool):
            for n in range(2):
                pool.wait_ge(roped, n + 1)
                for a in range(2):
                    for half in range(2):
                        nc.gpsimd.tensor_copy(g_kT[half * HD:half * HD + HD, 2 * n + a, :], g_k[a * HD:a * HD + HD, n, :])\
                            .then_inc(k_copied, 1)
            pool.wait_ge(roped, NORMED)
            pool.dma_start(grid, dram["grid_mla"]).then_inc(grid_in, 16)

            def norm_rows(i, j, after):
                pool.wait_ge(x_ready, after)
                for n, name in enumerate(("ln_g_2", "ln_b_2")):
                    pool.dma_start(ln_rows[:, n, :], dram[name][i, j].partition_broadcast(P)).then_inc(ln_in, 16)

            norm_rows(0, 1, ln_count[0, 0, NT[0] - 1])
            norm_rows(1, 0, ln_count[0, 1, NT[0] - 1])
            pool.wait_ge(kpe_ready, 1)
            for n in range(4):
                nc.gpsimd.tensor_copy(m_kT[HD:MLA_QK, 4 * n:4 * n + 4, :],
                                      m_kpe[HD:MLA_QK, :].unsqueeze(1).to_broadcast([PE_DIM, 4, 2 * S])).then_inc(k_copied, 1)
            norm_rows(1, 1, ln_count[1, 0, NT[1] - 1])


def build(nc, T, dram, out):
    with ExitStack() as ctx:
        def sb(name, shape, dt=F32):
            return ctx.enter_context(nc.sbuf_tensor(name, shape, dt))

        names = []

        def sem(name):
            names.append(name)
            return ctx.enter_context(nc.semaphore(f"{name}_{len(names)}"))

        n_f32 = dram["f32_tables"].shape[1]
        n_bf16 = dram["bf16_tables"].shape[1]
        chip = {"consts": sb("consts", [P, n_f32]), "masks": sb("masks", [P, n_bf16], BF16),
                "ring": sb("ring", [P, N_SLOTS, SLOT])}
        x = sb("x_sb", [P, TT, D])
        cos, sin = sb("cos", [P, S]), sb("sin", [P, S])
        chip.update(x=x[:, :, :], cos=cos[:, :], sin=sin[:, :])
        chip["mod"] = sb("mod", [P, DEPTH * 2 * MODC])
        chip["cols2"] = sb("cols2", [P, N_ROWS2])[:, :]
        chip["silu_c"] = sb("silu_c", [P, KD, 2])[:, :, :]
        chip["work"] = sb("work", [P, 30540])
        chip["psum"] = [ctx.enter_context(nc.psum_tensor(f"bank{i}", [P, 512], F32)) for i in range(8)]

        prologue(nc, T, dram, sem, chip)
        layer_sems = []

        def layer_sem(name):
            layer_sems.append(sem(name))
            return layer_sems[-1]

        with nc.Fori(0, DEPTH) as l:
            first_layer(nc, l, T, dram, layer_sem, chip)
            for s in layer_sems:
                nc.gpsimd.sem_clear(s)
            nc.all_engine_barrier()

        second_block(nc, T, dram, out, sem, chip)


_INS = ["x", "positions", "norm_mix", "w_in", "b_gate", "nsa_cmp_pos_k", "nsa_cmp_pos_v", "nsa_cmp_wk1",
        "nsa_cmp_wk2", "nsa_cmp_wv1", "nsa_cmp_wv2", "gla_w_alpha", "gla_b_alpha", "gla_norm", "fox_b_f",
        "w_branch", "w_out", "norm_ff", "w_ff1", "w_ff2", "norm_final",
        "c_2", "ctx_2", "c_ctx_2", "w_ada_2", "b_ada_2", "ln_g_2", "ln_b_2", "mlp_w1_2", "mlp_w2_2",
        "gqa_w_qkv_2", "gqa_q_norm_2", "gqa_k_norm_2", "gqa_w_o_2", "mla_w_in_2", "mla_q_norm_2",
        "mla_kv_norm_2", "mla_w_uq_2", "mla_w_ukv_2", "mla_w_o_2"]


def kernel(**inputs):
    import concourse.bacc as _bacc
    import ml_dtypes
    from concourse.bass_utils import run_bass_kernel_spmd as _run

    nc = _bacc.Bacc("TRN2", target_bir_lowering=False, num_devices=1)
    f32, bf16 = constants()
    T, arrays, dram = {}, {}, {}
    T["f32"], arrays["f32_tables"] = packed(f32, np.float32)
    T["bf16"], arrays["bf16_tables"] = packed(bf16, ml_dtypes.bfloat16)
    arrays["grid_gqa"] = grid_tables(HD, 0, HD)
    arrays["grid_mla"] = grid_tables(PE_DIM, HD, HD)
    for name in _INS:
        arrays[name] = np.ascontiguousarray(inputs[name])
    for name, a in arrays.items():
        dram[name] = nc.dram_tensor(name, a.shape, mybir.dt.from_np(a.dtype), kind="ExternalInput").ap()
    out = nc.dram_tensor("out", (1, S, D), F32, kind="ExternalOutput").ap()
    build(nc, T, dram, out)
    r = _run(nc, [arrays], core_ids=[0])
    return r.results[0]["out"]
```

```python
from contextlib import ExitStack

import numpy as np

import concourse.bass as bass
from concourse import mybir

F32, BF16, I32, U16 = mybir.dt.float32, mybir.dt.bfloat16, mybir.dt.int32, mybir.dt.uint16
F32R = mybir.dt.float32r
ACT = mybir.ActivationFunctionType
ALU = mybir.AluOpType
AX = mybir.AxisListType

P = 128
D, S, DEPTH = 1024, 256, 2
KD = D // P
TT = S // P
HD = 64
HALF_HEADS = 4
N_CMP, CMP_LEN, CMP_STRIDE, CMP_HID = 15, 32, 16, 256
N_GATE = 24
GLA_H, GLA_DV, GLA_RANK, GLA_TAU = 4, 128, 16, 16.0
FFK = 4 * D // P
THIN = 32
EPS = 1e-6
NEG = -1e30
GELU_C = 0.7978845608028654
ROT_HALF, ROPE_THETA = 8, 500000.0
GRID_W, GRID_THETA = 64, 10000.0
HEADS, KV_HEADS = 16, 4
Q_RANK, KV_RANK, PE_DIM = 384, 256, 32
MLA_QK = HD + PE_DIM
ALPHA = (2.0 * DEPTH) ** 0.25
MOD_PARTS = 6
MODC = MOD_PARTS * KD

ROW_ADA, ROW_QN, ROW_KN, ROW_MQN, ROW_MKN, ROW_C, N_ROWS2 = 0, 96, 97, 98, 101, 103, 119

Q0, KC0, KS0 = 0, 512, 768
SBQ0, SBK0, SBV0 = 1304, 1816, 2328
GLQ0, GLV0, GLA0, GLG0 = 2840, 3352, 3864, 3880
FXQ0, FXK0, FXV0, GATE0 = 4392, 4904, 5416, 5936

ROW_MIX, ROW_FF, ROW_GATE, ROW_GLB, ROW_GLN, ROW_PEK, ROW_PEV, N_ROWS = 0, 8, 16, 48, 50, 51, 67, 83

LEVELS = [128, 0, 64, 32, 16, 8, 4, 2, 1]
SLOT = 528 * KD
N_SLOTS = 4
SPLIT_HALF = 2 * D
WORK = 30336
MAGIC = 1.5 * 2.0 ** 23
TWO_PI_PARTS = (6.28125, 0.0019340515136718750, 1.2556659146019e-06)


def constants():
    i = np.arange(P)
    row, col = i[:, None], i[None, :]
    rot = np.zeros((P, P), np.float32)
    for half in (0, HD):
        for d in range(ROT_HALF):
            rot[half + ROT_HALF + d, half + d] = -1.0
            rot[half + d, half + ROT_HALF + d] = 1.0
    levels = [(row == col)]
    for h in LEVELS[2:]:
        s, t = row, col
        levels.append((s // (2 * h) == t // (2 * h)) & (s % (2 * h) < h) & (t % (2 * h) >= h))
    inv = (ROPE_THETA ** (-np.arange(0, 2 * ROT_HALF, 2) / (2 * ROT_HALF))).astype(np.float32)
    inv_col = np.zeros((P, 1), np.float32)
    for half in (0, HD):
        for d in range(2 * ROT_HALF):
            inv_col[half + d, 0] = inv[d % ROT_HALF]
    end = np.arange(N_CMP) * CMP_STRIDE + CMP_LEN - 1
    seen = np.stack([end[None, :] <= (tt * P + i)[:, None] for tt in range(TT)], 1).reshape(P, -1)
    f32 = {
        "ident": np.eye(P),
        "neg_from": -1.0 * (row >= col),
        "neg_upto": -1.0 * (row <= col),
        "neg_ones": -np.ones((P, P)),
        "rot": rot,
        "inv_freq": inv_col,
        "one": np.ones((P, 1)), "eps": np.full((P, 1), EPS),
        "cmp_seen": seen, "cmp_bias": np.where(seen, 0.0, NEG),
        "head_sel": np.repeat(np.eye(P)[:, :8], P, axis=1),
        "ones": np.ones((P, S)),
        "sum4": np.tile(np.eye(THIN), (4, 1)),
        "head_mean": np.kron(np.eye(2), np.ones((HD, HD))) / HD,
    }
    bf16 = {
        "ident": np.eye(P),
        "causal": np.where(col > row, NEG, 0.0),
        "strict": np.where(row >= col, NEG, 0.0),
        "levels": np.stack(levels, 1).reshape(P, -1),
    }
    return f32, bf16


def grid_tables(rot_dim, start, period):
    axis, half = rot_dim // 2, rot_dim // 4
    swap, angle = np.zeros((P, P), np.float32), np.zeros((P, S), np.float32)
    inv = (GRID_THETA ** (-np.arange(0, axis, 2, dtype=np.float32) / np.float32(axis))).astype(np.float32)
    tok = np.arange(S)
    for base in range(start, P, period):
        for a, place in enumerate((tok // GRID_W, tok % GRID_W)):
            for j in range(half):
                lo = base + a * axis + j
                hi = lo + half
                swap[hi, lo], swap[lo, hi] = -1.0, 1.0
                angle[lo] = angle[hi] = place.astype(np.float32) * inv[j]
    return np.concatenate([swap, np.cos(angle), np.sin(angle)], 1).astype(np.float32)


def packed(tables, dtype):
    at, parts, n = {}, [], 0
    for name, a in tables.items():
        at[name] = (n, a.shape[1])
        parts.append(np.asarray(a, np.float32))
        n += a.shape[1]
    return at, np.concatenate(parts, 1).astype(dtype)


class Banks:

    def __init__(self, sem, label, banks, uses):
        assert len(set(uses)) == len(uses), label
        self.order = {name: i for i, name in enumerate(uses)}
        self.banks, self.filled, self.n = banks, 0, len(banks)
        self.full = sem(label + "_full")
        self.free_sems = [sem(f"{label}_free{b}") for b in range(self.n)]

    def bank(self, name):
        return self.banks[self.order[name] % self.n]

    def claim(self, pe, name):
        i = self.order[name]
        assert i == self.filled, (name, i, self.filled)
        self.filled += 1
        if i >= self.n:
            pe.wait_ge(self.free_sems[i % self.n], i // self.n)
        return self.bank(name)

    def arrived(self, eng, name):
        eng.wait_ge(self.full, self.order[name] + 1)
        return self.bank(name)

    def taken(self, eng, *names):
        for name in names:
            i = self.order[name]
            eng.wait_ge(self.free_sems[i % self.n], i // self.n + 1)

    def free(self, name):
        return self.free_sems[self.order[name] % self.n]


class Weights:

    def __init__(self, sem, label, ring, tiles):
        self.tiles, self.ring = tiles, ring
        self.order = {tile[0]: i for i, tile in enumerate(tiles)}
        self.loaded = [sem(f"{label}_loaded{s}") for s in range(N_SLOTS)]
        count, self.ready = [0] * N_SLOTS, []
        for i, (_, _, _, sources, _) in enumerate(tiles):
            count[i % N_SLOTS] += 16 * len(sources)
            self.ready.append(count[i % N_SLOTS])

    def slot(self, i):
        _, k, n, _, _ = self.tiles[i]
        return self.ring[:, i % N_SLOTS, 0:k * n].rearrange("p (k n) -> p k n", k=k)

    def load(self, sp):
        for i, (_, _, _, sources, _) in enumerate(self.tiles):
            if i >= N_SLOTS:
                sp.wait_ge(*self.tiles[i - N_SLOTS][4])
            for part, src in sources:
                sp.dma_start(self.slot(i)[part], src).then_inc(self.loaded[i % N_SLOTS], 16)

    def arrived(self, pe, name):
        i = self.order[name]
        pe.wait_ge(self.loaded[i % N_SLOTS], self.ready[i])
        return self.slot(i)


class Split:

    def __init__(self, sem, label, weights, ring_low, buffers, halves, freed):
        self.weights, self.ring_low, self.buffers, self.freed = weights, ring_low, buffers, freed
        self.order = {(name, half): (i, axis) for i, (name, half, axis) in enumerate(halves)}
        self.high_made, self.cut = sem(label + "_high_made"), sem(label + "_cut")

    def part(self, name, half, low):
        i = self.weights.order[name]
        _, k, n, _, _ = self.weights.tiles[i]
        slot = self.ring_low[i % N_SLOTS][:, 0:k * n] if low else self.weights.ring[:, i % N_SLOTS, 0:k * n]
        tile = slot.rearrange("p (k n) -> p k n", k=k)
        if self.order[name, half][1] == "k":
            return tile[:, k // 2 * half:k // 2 * (half + 1), :]
        return tile[:, :, n // 2 * half:n // 2 * (half + 1)]

    def high(self, name, half):
        k = self.part(name, half, True).shape[1]
        buffer = self.buffers[self.order[name, half][0] % len(self.buffers)]
        return buffer[:, :].rearrange("p (k n) -> p k n", k=k)

    def make_high(self, nc, act, name, half):
        i = self.order[name, half][0]
        self.weights.arrived(act, name)
        if i >= len(self.buffers):
            act.wait_ge(*self.freed[i - len(self.buffers)])
        nc.scalar.activation(self.high(name, half), self.part(name, half, False), ACT.Copy).then_inc(self.high_made, 1)

    def make_low(self, nc, dve, name, half):
        dve.wait_ge(self.high_made, self.order[name, half][0] + 1)
        nc.vector.tensor_tensor(self.part(name, half, True), self.part(name, half, False),
                                self.high(name, half).bitcast(F32), ALU.subtract).then_inc(self.cut, 1)

    def arrived(self, pe, name, half):
        pe.wait_ge(self.cut, self.order[name, half][0] + 1)
        return self.high(name, half), self.part(name, half, True)


def product(nc, out, a, b, start, stop):
    nc.tensor.matmul(out, a[0], b[1], start=start, stop=False)
    nc.tensor.matmul(out, a[1], b[0], start=False, stop=False)
    return nc.tensor.matmul(out, a[0], b[0], start=False, stop=stop)


class Chain:

    def __init__(self, eng, sem):
        self.eng, self.sem, self.n = eng, sem, 0

    def __call__(self, ins):
        self.n += 1
        ins.then_inc(self.sem, 1)
        self.eng.wait_ge(self.sem, self.n)


class Carver:

    def __init__(self, whole, at=0):
        self.whole, self.at = whole, at

    def take(self, *dims):
        n = int(np.prod(dims))
        part = self.whole[:, self.at:self.at + n]
        self.at += -(-n // 8) * 8
        assert self.at <= self.whole.shape[1], ("SBUF work space", self.at)
        if len(dims) == 1:
            return part
        names = "abcde"[:len(dims)]
        spec = f"p ({' '.join(names)}) -> p {' '.join(names)}"
        return part.rearrange(spec, **{c: d for c, d in zip(names, dims)})


def first_layer(nc, l, T, dram, sem, chip):
    x, consts, masks = chip["x"], chip["consts"], chip["masks"]
    cos, sin, silu_c = chip["cos"], chip["sin"], chip["silu_c"]
    work = Carver(chip["work"])

    cols = work.take(N_ROWS)
    w_alpha, fox_b = work.take(GLA_H * HD), work.take(8)
    hT = work.take(KD, S)
    after_hT = work.at
    nsaT = work.take(6, S)
    hid_c = work.take(2, 2, 2 * N_CMP)
    gelu_t, gelu_e = work.take(2, 2 * N_CMP), work.take(2, 2 * N_CMP)
    kcT, kc_sin = work.take(N_CMP), work.take(N_CMP)
    vc = work.take(2, HD)
    vs, vw = work.take(TT, P), work.take(TT, P)
    g_nsa = work.take(TT, N_GATE)
    p_cmp = work.take(2, 4, TT, N_CMP)
    stat_cmp = work.take(2, 4, TT)
    qk_at = work.at
    sb_qk = work.take(KD, S)
    sbq, sbk = sb_qk[:, 0:4, :], sb_qk[:, 4:8, :]
    sbv = work.take(TT, 512)
    gle = work.take(TT, 512)
    gla_b = work.take(2, S)
    att = work.take(2, 3, 2, P)
    fxq, fxk = work.take(4, S), work.take(4, S)
    fxv = work.take(TT, 512)
    log_f, fox_t = work.take(TT, 8), work.take(TT, 8)
    fox_row = work.take(S)
    gates = work.take(4 * KD, S)
    yT = work.take(4 * 4, S)
    prob, probT = work.take(2, 3 * P), work.take(2, 3 * P)
    sb_at = work.at
    sb_u, sb_p = work.take(2, 3 * P), work.take(2, 3 * P)
    neg_max, total = work.take(2, TT), work.take(2, TT)
    stat, rstd = work.take(TT), work.take(TT)
    gl_stat, gl_rstd = work.take(TT, GLA_H), work.take(TT, GLA_H)
    early = Carver(gates.rearrange("p a b -> p (a b)"))
    rows, wk2, wv2 = early.take(P), early.take(2, HD), early.take(2, HD)
    glq, glk = early.take(2, S), early.take(2, S)
    glv, glg = early.take(TT, 512), early.take(TT, 512)
    gla_t, glaT = early.take(2, S), early.take(S)
    lv_d, lv_q, lv_k = early.take(2, 512), early.take(2, 512), early.take(2, 512)
    flat_y = yT.rearrange("p a b -> p (a b)")
    xn = flat_y[:, 0:TT * D].rearrange("p (t d) -> p t d", t=TT)
    sq = flat_y[:, TT * D:TT * D + D]
    pcT = [yT[:, 4:8, :], yT[:, 12:16, :]]
    blk = Carver(chip["work"], sb_at).take(2, CMP_LEN // 2, THIN)
    mix_t = fxv
    hid_p = fxv[:, 1, :].rearrange("p (i n) -> p i n", i=2)
    ada_p = gla_b.rearrange("p c s -> p (c s)")
    mixedT = sb_qk
    rounded = chip["rounded"]
    late_high = [rounded(f"late_high{n}", qk_at + n * SPLIT_HALF, SPLIT_HALF) for n in range(2)]
    early_high = [rounded(f"early_high{n}", qk_at + (2 + n) * SPLIT_HALF, SPLIT_HALF) for n in range(2)]
    hidden_at = qk_at + 4 * SPLIT_HALF
    hidden = Carver(chip["work"], hidden_at).take(FFK, S)
    hidden_low, hidden_high = rounded("hidden_low", hidden_at, FFK, S), rounded("hidden_high", hidden_at + FFK * S, FFK, S)
    hT_low, hT_high = rounded("hT_low", after_hT - KD * S, KD, S), rounded("hT_high", after_hT, KD, S)

    K = lambda name: consts[:, T["f32"][name][0]:sum(T["f32"][name])]
    M = lambda name: masks[:, T["bf16"][name][0]:sum(T["bf16"][name])]
    ident, one, eps = K("ident"), K("one"), K("eps")
    head_sel = K("head_sel").rearrange("p (h t) -> p h t", h=8)
    level_mask = M("levels").bitcast(U16).rearrange("p (n t) -> p n t", n=len(LEVELS) - 1)

    jobs = []
    for c in range(HALF_HEADS):
        for g in range(2):
            jobs += [("slc", c, g), ("win", c, g)]
    jobs += [("fox", h // 2, h % 2) for h in range(8)]
    jobs += [("sb", h // 2, h % 2) for h in range(8)]
    NJ = len(jobs)

    ada_steps = [i for i in range(4 * KD) if i % 8 in (1, 4, 6)]
    step_fills, step_tiles = [], []
    for i in range(4 * KD):
        if i % 4 == 0:
            step_tiles.append(("gate", i // 4))
        step_fills.append(f"g{i}")
        if i - 1 in ada_steps:
            step_fills.append(f"adT{ada_steps.index(i - 1)}")
        if i in ada_steps:
            step_fills.append(f"ada{ada_steps.index(i)}")
            step_tiles.append(("ada", ada_steps.index(i)))

    LV = [f"lv{n}_{par}" for n in range(len(LEVELS)) for par in range(2)]
    proj_uses = (["params"] + [f"xT{c}" for c in range(4)]
                 + ["q0", "q1", "kc", "vc", "vs", "kskw", "vwg", "rope0", "rope1", "rope2"]
                 + ["hk", "hv"]
                 + ["gq", "gk", "ga", "gg0", "gg1", "la", "gv0", "gv1"]
                 + ["sq0", "sq1", "sk0", "sk1", "sv0", "sv1", "fq0", "fq1", "fk0", "fk1",
                    "fv0", "fv1", "ff", "fc", "gyT0", "gyT1"]
                 + step_fills
                 + [f"br{n}_{f}" for n in range(4) for f in range(KD // 2)]
                 + [f"wo{h}{t}" for h in range(2) for t in range(TT)]
                 + [f"yT{c}" for c in range(4)]
                 + [f"up{i}" for i in range(FFK // 2)])
    PROJ = Banks(sem, "proj", chip["psum"][0:2], proj_uses)
    SC = Banks(sem, "score", chip["psum"][2:4], ["hkT", "hvT", "kc2", "rope_kc", "vc2", "cmp0", "cmp1"] + [f"s{j}" for j in range(NJ)] + ["down0", "down1"])
    PT = Banks(sem, "turn", chip["psum"][4:6],
               LV + [f"pc{g}{i}" for g in range(2) for i in range(2)]
               + [f"p{j}" for j in range(NJ) if jobs[j][0] != "sb"])
    OT = Banks(sem, "out", chip["psum"][6:8],
               ["go0", "go1"] + [f"o_{k}{c}" for k in ("nsa", "fox", "sb") for c in range(HALF_HEADS)]
               + ["down2", "down3"])

    def done(name):
        return PROJ.full, PROJ.order[name] + 1

    w_in = dram["w_in"][bass.ds(l, 1)].rearrange("l (k p) n -> p (l k) n", p=P)
    whole = (slice(None), slice(None), slice(None))

    def in_tile(name, c0, n, last):
        return name, KD, n, [(whole, w_in[:, :, c0:c0 + n])], done(last)

    down_used = sem("down_used")
    branch = dram["w_branch"][bass.ds(l, 1)].rearrange("l n c d -> (l n) c d")

    def branch_tile(n):
        if n == 0:
            src = branch[0].rearrange("(g c d) m -> g d c m", g=2, d=HD)
            parts = [((slice(g * HD, g * HD + HD), slice(None), slice(None)), src[g]) for g in range(2)]
        else:
            parts = [(whole, branch[n].rearrange("(c p) m -> p c m", p=P))]
        return f"branch{n}", 4, D, parts, done(f"br{n}_{KD // 2 - 1}")

    def layer_of(name):
        return dram[name][bass.ds(l, 1)]

    wk1 = layer_of("nsa_cmp_wk1").rearrange("l (k p) n -> p (l k) n", p=P)
    wv1 = layer_of("nsa_cmp_wv1").rearrange("l (k p) n -> p (l k) n", p=P)
    w_out = layer_of("w_out").rearrange("l (k p) n -> p (l k) n", p=P)
    w_ff1 = layer_of("w_ff1").rearrange("l (k p) n -> p (l k) n", p=P)
    w_ff2 = layer_of("w_ff2").rearrange("l (k p) n -> p (l k) n", p=P)
    def blocks(name, c0, order, last):
        parts = [((slice(None), slice(None), slice(i * HD, (i + 1) * HD)),
                  w_in[:, :, c0 + b * HD:c0 + (b + 1) * HD]) for i, b in enumerate(order)]
        return name, KD, 512, parts, done(last)

    q_tile = blocks("q", Q0, [0, 4, 1, 5, 2, 6, 3, 7], "q1")
    cmp_tile = blocks("cmp", KC0, [0, 0, 1, 1, 2, 2, 3, 3], "vc")
    tiles = [q_tile, cmp_tile, in_tile("kvs", KS0, 256, "kskw"), in_tile("kwg", KS0 + 256, 280, "vwg"),
             ("wk1", 16, CMP_HID, [(whole, wk1)], done("hk")), ("wv1", 16, CMP_HID, [(whole, wv1)], done("hv")),
             in_tile("glqk", GLQ0, 512, "gk"), in_tile("glag", GLA0, 528, "gg1"), in_tile("glv", GLV0, 512, "gv1"),
             in_tile("sbq", SBQ0, 512, "sq1"), in_tile("sbk", SBK0, 512, "sk1"), in_tile("sbv", SBV0, 512, "sv1"),
             in_tile("fxq", FXQ0, 512, "fq1"), in_tile("fxk", FXK0, 512, "fk1"), in_tile("fxv", FXV0, 520, "ff")]
    w_ada = layer_of("w_ada_2").rearrange("l (k p) n -> p (l k) n", p=P)
    for kind, i in step_tiles:
        if kind == "gate":
            tiles.append(in_tile(f"gate{i}", GATE0 + 512 * i, 512, f"g{4 * i + 3}"))
        else:
            tiles.append((f"ada{i}", KD, 512, [(whole, w_ada[:, :, 512 * i:512 * i + 512])], done(f"ada{i}")))
    tiles += [branch_tile(n) for n in range(4)]
    tiles += [(f"out{h}", KD, 512, [(whole, w_out[:, :, 512 * h:512 * h + 512])], done(f"wo{h}1")) for h in range(2)]
    tiles += [(f"up{i}", KD, 512, [(whole, w_ff1[:, :, 512 * i:512 * i + 512])], done(f"up{2 * i + 1}")) for i in range(8)]
    tiles += [(f"down{i}", 4, D, [(whole, w_ff2[:, 4 * i:4 * i + 4, :])], (down_used, 2 * i + 2)) for i in range(8)]
    W = Weights(sem, "w", chip["ring"], tiles)
    halves = [(f"up{i}", b, "n") for i in range(8) for b in range(2)] + [(f"down{i}", b, "k") for i in range(8) for b in range(2)]
    X = Split(sem, "ff", W, chip["ring_low"], early_high + late_high, halves,
              [done(f"up{n}") for n in range(16)] + [(down_used, n + 1) for n in range(15)])

    rows_in = sem("rows_in")
    small_in = sem("small_in")
    rstd_ready = sem("rstd_ready")
    xn_ready = sem("xn_ready")
    gelu_x2 = sem("gelu_x2")
    gelu_in = sem("gelu_in")
    gelu_exp = sem("gelu_exp")
    roped = sem("roped")
    gate_ready = sem("gate_ready")
    cmp_in = sem("cmp_in")
    cmp_exp = sem("cmp_exp")
    cmp_ready = sem("cmp_ready")
    gl_gate = sem("gl_gate")
    la_log = sem("la_log")
    lv_diff = sem("lv_diff")
    lv_exp = sem("lv_exp")
    lv_ready = sem("lv_ready")
    gl_scale = sem("gl_scale")
    fox_log = sem("fox_log")
    fox_ready = sem("fox_ready")
    max_ready = sem("max_ready")
    prob_ready = sem("prob_ready")
    sb_log = sem("sb_log")
    sb_soft = sem("sb_soft")
    sb_later = sem("sb_later")
    mix_gate = sem("mix_gate")
    mixed_ready = sem("mixed_ready")
    hT_cut = sem("hT_cut")
    hidden_squared = sem("hidden_squared")
    hidden_ready = sem("hidden_ready")
    act_self, dve_self = sem("act_self"), sem("dve_self")

    with nc.Block() as block:

        @block.sync
        def _(sp):
            W.load(sp)

        @block.tensor
        def _(pe):
            def mm(out, lhsT, rhs, start, stop):
                return nc.tensor.matmul(out, lhsT, rhs, start=start, stop=stop)

            def turn(out, src):
                return nc.tensor.transpose(out, src, ident[0:src.shape[0], 0:src.shape[0]])

            def gemm_T(out, w, cols):
                for k in range(KD):
                    last = mm(out, w[:, k, cols], hT[:, k, :], k == 0, k == KD - 1)
                return last

            def gemm(out, w, cols, t):
                for k in range(KD):
                    last = mm(out, hT[:, k, t * P:t * P + P], w[:, k, cols], k == 0, k == KD - 1)
                return last

            def turn_x(name, ready):
                pe.wait_ge(xn_ready, ready)
                for c in range(4):
                    ps = PROJ.claim(pe, f"{name}{c}")
                    for k in range(2):
                        for t in range(TT):
                            last = turn(ps[:, (2 * k + t) * P:(2 * k + t + 1) * P],
                                        xn[:, t, (2 * c + k) * P:(2 * c + k + 1) * P])
                    last.then_inc(PROJ.full, 1)

            def pairs(names, w, c0):
                for i, name in enumerate(names):
                    ps = PROJ.claim(pe, name)
                    for k in range(2):
                        at = c0 + (2 * i + k) * P
                        last = gemm_T(ps[:, k * S:(k + 1) * S], w, slice(at, at + P))
                    last.then_inc(PROJ.full, 1)

            def thin(ps, thin_T, w, chunks):
                for k in range(chunks):
                    rows_of = slice(k % 4 * THIN, k % 4 * THIN + THIN)
                    last = mm(ps[rows_of, 0:w.shape[2]], thin_T[:, k, :], w[:, k, :], k < 4, k >= chunks - 4)
                return last

            pe.wait_ge(rows_in, 7 * 16)
            turn(PROJ.claim(pe, "params")[:, 0:N_ROWS], rows[0:N_ROWS, :]).then_inc(PROJ.full, 1)
            turn_x("xT", TT)

            w = W.arrived(pe, "q")
            PROJ.taken(pe, "xT2", "xT3")
            for i in range(2):
                ps = PROJ.claim(pe, f"q{i}")
                for k in range(2):
                    c = 2 * i + k
                    last = gemm_T(ps[:, k * S:(k + 1) * S], w, slice(c * P, (c + 1) * P))
                last.then_inc(PROJ.full, 1)
            w = W.arrived(pe, "cmp")
            for i, name in enumerate(("kc", "vc")):
                ps = PROJ.claim(pe, name)
                for g in range(2):
                    last = gemm_T(ps[:, g * S:(g + 1) * S], w, slice((2 * i + g) * P, (2 * i + g + 1) * P))
                last.then_inc(PROJ.full, 1)
            w = W.arrived(pe, "kvs")
            ps = PROJ.claim(pe, "vs")
            for t in range(TT):
                last = gemm(ps[:, t * P:(t + 1) * P], w, slice(P, 2 * P), t)
            last.then_inc(PROJ.full, 1)
            ps = PROJ.claim(pe, "kskw")
            gemm_T(ps[:, 0:S], w, slice(0, P))
            w = W.arrived(pe, "kwg")
            gemm_T(ps[:, S:2 * S], w, slice(0, P)).then_inc(PROJ.full, 1)
            ps = PROJ.claim(pe, "vwg")
            for t in range(TT):
                last = gemm(ps[:, t * 152:(t + 1) * 152], w, slice(P, 280), t)
            last.then_inc(PROJ.full, 1)

            for i in range(3):
                ps = PROJ.claim(pe, f"rope{i}")
                PROJ.taken(pe, ("q0", "q1", "kskw")[i])
                mm(ps[:, :], K("rot"), nsaT[:, 2 * i:2 * i + 2, :], True, True).then_inc(PROJ.full, 1)

            for i, name in enumerate(("hk", "hv")):
                w = W.arrived(pe, ("wk1", "wv1")[i])
                ps = PROJ.claim(pe, name)
                PROJ.taken(pe, ("kc", "vc")[i])
                thin(ps, blk[:, i], w, CMP_LEN // 2).then_inc(PROJ.full, 1)
            for i, name in enumerate(("hk", "hv")):
                ps = SC.claim(pe, name + "T")
                PROJ.taken(pe, name)
                for m in range(2):
                    last = mm(ps[:, m * 2 * N_CMP:(m + 1) * 2 * N_CMP], hid_p[:, i, m * P:(m + 1) * P],
                              K("sum4")[:, 0:2 * N_CMP], True, True)
                last.then_inc(SC.full, 1)

            pairs(["gq"], W.arrived(pe, "glqk"), 0)
            pairs(["gk"], W.arrived(pe, "glqk"), S)
            w = W.arrived(pe, "glag")
            gemm_T(PROJ.claim(pe, "ga")[0:GLA_RANK, 0:S], w, slice(0, GLA_RANK)).then_inc(PROJ.full, 1)

            ps = SC.claim(pe, "kc2")
            pe.wait_ge(small_in, 4 * 16)
            SC.taken(pe, "hkT")
            for g in range(2):
                for m in range(2):
                    last = mm(ps[g * HD:(g + 1) * HD, 0:N_CMP], wk2[:, m, :],
                              hid_c[:, 0, m, g * N_CMP:(g + 1) * N_CMP], m == 0, m == 1)
            last.then_inc(SC.full, 1)
            gemm(PROJ.claim(pe, "gg0")[:, :], w, slice(GLA_RANK, 528), 0).then_inc(PROJ.full, 1)
            ps = SC.claim(pe, "rope_kc")
            SC.taken(pe, "kc2")
            mm(ps[:, 0:N_CMP], K("rot"), kcT, True, True).then_inc(SC.full, 1)
            ps = SC.claim(pe, "vc2")
            SC.taken(pe, "hvT")
            for g in range(2):
                for m in range(2):
                    last = mm(ps[0:N_CMP, g * HD:(g + 1) * HD], hid_c[:, 1, m, g * N_CMP:(g + 1) * N_CMP],
                              wv2[:, m, :], m == 0, m == 1)
            last.then_inc(SC.full, 1)
            gemm(PROJ.claim(pe, "gg1")[:, :], w, slice(GLA_RANK, 528), 1).then_inc(PROJ.full, 1)
            ps = PROJ.claim(pe, "la")
            PROJ.taken(pe, "ga")
            for c in range(2):
                last = mm(ps[:, c * S:(c + 1) * S], w_alpha[0:GLA_RANK, c * P:(c + 1) * P], glaT[0:GLA_RANK, :], True, True)
            last.then_inc(PROJ.full, 1)
            w = W.arrived(pe, "glv")
            for t in range(TT):
                gemm(PROJ.claim(pe, f"gv{t}")[:, :], w, slice(0, 512), t).then_inc(PROJ.full, 1)

            pe.wait_ge(roped, 4)
            for g in range(2):
                ps = SC.claim(pe, f"cmp{g}")
                for c in range(4):
                    for t in range(TT):
                        at = (c * TT + t) * N_CMP
                        last = mm(ps[:, at:at + N_CMP], nsaT[g * HD:(g + 1) * HD, c, t * P:(t + 1) * P],
                                  kcT[g * HD:(g + 1) * HD, :], True, True)
                last.then_inc(SC.full, 1)

            def level(n):
                if LEVELS[n] == 0:
                    PROJ.taken(pe, "gq", "gk")
                else:
                    pe.wait_ge(lv_ready, n + (n == 0))
                at = max(n - 1, 0) % 2
                q = glq if LEVELS[n] == 0 else lv_q[:, at].rearrange("p (c s) -> p c s", c=2)
                k = glk if LEVELS[n] == 0 else lv_k[:, at].rearrange("p (c s) -> p c s", c=2)
                for par in range(2):
                    ps = PT.claim(pe, f"lv{n}_{par}")
                    r = slice(par * HD, (par + 1) * HD)
                    for c in range(2):
                        for t in ([1] if LEVELS[n] == P else range(TT)):
                            at = c * P if LEVELS[n] == P else (t * 2 + c) * P
                            s = 0 if LEVELS[n] == P else t
                            last = mm(ps[:, at:at + P], k[r, c, s * P:(s + 1) * P], q[r, c, t * P:(t + 1) * P], True, True)
                    last.then_inc(PT.full, 1)

            w = W.arrived(pe, "sbq")
            for i in range(2):
                ps = PROJ.claim(pe, f"sq{i}")
                for k in range(2):
                    last = gemm_T(ps[:, k * S:(k + 1) * S], w, slice((2 * i + k) * P, (2 * i + k + 1) * P))
                last.then_inc(PROJ.full, 1)
                level(i)
            w = W.arrived(pe, "sbk")
            for i in range(2):
                ps = PROJ.claim(pe, f"sk{i}")
                for k in range(2):
                    last = gemm_T(ps[:, k * S:(k + 1) * S], w, slice((2 * i + k) * P, (2 * i + k + 1) * P))
                last.then_inc(PROJ.full, 1)
                level(2 + i)
            w = W.arrived(pe, "sbv")
            for t in range(TT):
                gemm(PROJ.claim(pe, f"sv{t}")[:, :], w, slice(0, 512), t).then_inc(PROJ.full, 1)
                level(4 + t)
            w = W.arrived(pe, "fxq")
            for i in range(2):
                ps = PROJ.claim(pe, f"fq{i}")
                for k in range(2):
                    last = gemm_T(ps[:, k * S:(k + 1) * S], w, slice((2 * i + k) * P, (2 * i + k + 1) * P))
                last.then_inc(PROJ.full, 1)
                level(6 + i)
            w = W.arrived(pe, "fxk")
            for i in range(2):
                ps = PROJ.claim(pe, f"fk{i}")
                for k in range(2):
                    last = gemm_T(ps[:, k * S:(k + 1) * S], w, slice((2 * i + k) * P, (2 * i + k + 1) * P))
                last.then_inc(PROJ.full, 1)
                if i == 0:
                    level(8)
            w = W.arrived(pe, "fxv")
            for t in range(TT):
                gemm(PROJ.claim(pe, f"fv{t}")[:, :], w, slice(0, 512), t).then_inc(PROJ.full, 1)
            ps = PROJ.claim(pe, "ff")
            for t in range(TT):
                last = gemm(ps[:, t * 8:(t + 1) * 8], w, slice(512, 520), t)
            last.then_inc(PROJ.full, 1)

            PT.taken(pe, "lv8_0", "lv8_1")
            PROJ.taken(pe, "gv0", "gv1")
            for t in range(TT):
                ps = OT.claim(pe, f"go{t}")
                for h in range(GLA_H):
                    dv = slice(h * GLA_DV, (h + 1) * GLA_DV)
                    last = mm(ps[:, dv], att[:, h % 2, t, h // 2, :], glv[:, t, dv], True, t == 0)
                    if t == 1:
                        last = mm(ps[:, dv], att[:, h % 2, 2, h // 2, :], glv[:, 0, dv], False, True)
                last.then_inc(OT.full, 1)

            for g in range(2):
                pe.wait_ge(cmp_ready, g + 1)
                for i in range(2):
                    ps = PT.claim(pe, f"pc{g}{i}")
                    for c in range(2):
                        for t in range(TT):
                            at = (c * TT + t) * P
                            last = turn(ps[0:N_CMP, at:at + P], p_cmp[:, g, 2 * i + c, t, :])
                    last.then_inc(PT.full, 1)

            ps = PROJ.claim(pe, "fc")
            pe.wait_ge(fox_ready, 1)
            upto = consts[:, T["f32"]["neg_upto"][0]:T["f32"]["neg_upto"][0] + S]
            mm(ps[0:8, 0:S], log_f[:, 0, :], upto, True, False)
            mm(ps[0:8, P:S], log_f[:, 1, :], upto[:, 0:P], False, True).then_inc(PROJ.full, 1)

            for t in range(TT):
                ps = PROJ.claim(pe, f"gyT{t}")
                OT.taken(pe, f"go{t}")
                for h in range(GLA_H):
                    last = turn(ps[:, h * P:(h + 1) * P], gle[:, t, h * GLA_DV:(h + 1) * GLA_DV])
                last.then_inc(PROJ.full, 1)

            def scores(j):
                kind, c, par = jobs[j]
                r = slice(par * HD, (par + 1) * HD)
                ps = SC.claim(pe, f"s{j}")
                if kind == "sb":
                    mm(ps[:, 0:S], sbk[r, c, 0:P], sbq[r, c, :], True, False)
                    mm(ps[:, S:S + P], sbk[r, c, P:S], sbq[r, c, P:S], False, False)
                    mm(ps[:, 0:P], M("ident"), M("strict"), False, False)
                    mm(ps[:, S:S + P], M("ident"), M("strict"), False, True).then_inc(SC.full, 1)
                    return
                for t in range(TT):
                    n = (t + 1) * P
                    at = t * P
                    if kind == "fox":
                        mm(ps[:, at:at + n], fxq[r, c, t * P:(t + 1) * P], fxk[r, c, 0:n], True, False)
                        mm(ps[:, at:at + n], head_sel[0:8, 2 * c + par, :], fox_row[0:8, 0:n], False, False)
                    else:
                        mm(ps[:, at:at + n], nsaT[r, c, t * P:(t + 1) * P], nsaT[r, 4 + (kind == "win"), 0:n], True, False)
                    last = mm(ps[:, at + n - P:at + n], M("ident"), M("causal"), False, True)
                last.then_inc(SC.full, 1)

            def turned(j):
                kind, c, par = jobs[j]
                if kind == "sb":
                    ps = SC.bank(f"s{j}")
                    pe.wait_ge(sb_soft, j - 23)
                    sp_ = sb_p[:, j % 2]
                    add = lambda out, neg, rhs: nc.tensor.matmul(out, K(neg), rhs, start=False, stop=True, skip_group_check=True)
                    add(ps[:, 0:S], "neg_from", sp_[:, 0:S])
                    add(ps[:, P:S], "neg_ones", sp_[:, S:S + P])
                    add(ps[:, S:S + P], "neg_from", sp_[:, S:S + P]).then_inc(sb_later, 1)
                    return
                ps = PT.claim(pe, f"p{j}")
                pe.wait_ge(prob_ready, j + 1)
                p = prob[:, j % 2]
                turn(ps[:, 0:P], p[:, 0:P])
                turn(ps[:, P:2 * P], p[:, P:2 * P])
                turn(ps[:, 2 * P:3 * P], p[:, 2 * P:3 * P]).then_inc(PT.full, 1)

            def output(j):
                kind, c, par = jobs[j]
                r = slice(par * HD, (par + 1) * HD)
                group = "nsa" if kind in ("slc", "win") else kind
                name = f"o_{group}{c}"
                first, last_of = (kind != "win"), (kind != "slc")
                ps = OT.claim(pe, name) if first and par == 0 else OT.bank(name)
                if kind == "slc":
                    PT.taken(pe, f"pc{par}{c // 2}")
                    mm(ps[r, 0:S], vc[0:N_CMP, par, :], pcT[par][0:N_CMP, c, :], True, False)
                if kind == "sb":
                    SC.taken(pe, f"s{j}")
                    p, v = probT[:, j % 2], sbv[:, :, (2 * c + par) * HD:(2 * c + par + 1) * HD]
                else:
                    PT.taken(pe, f"p{j}")
                    p = probT[:, j % 2]
                    v = {"slc": vs, "win": vw}[kind][:, :, r] if kind != "fox" else \
                        fxv[:, :, (2 * c + par) * HD:(2 * c + par + 1) * HD]
                mm(ps[r, 0:S], v[:, 0, :], p[:, 0:S], kind in ("sb", "fox"), False)
                last = mm(ps[r, P:S], v[:, 1, :], p[:, S:S + P], False, last_of)
                if par == 1 and last_of:
                    last.then_inc(OT.full, 1)

            PROJ.taken(pe, "vs", "vwg")
            SC.taken(pe, "vc2")
            for i in range(NJ + 2):
                if i < 4 * KD:
                    w = W.arrived(pe, f"gate{i // 4}")
                    gemm_T(PROJ.claim(pe, f"g{i}")[:, 0:S], w, slice(i % 4 * P, (i % 4 + 1) * P)).then_inc(PROJ.full, 1)
                if i - 1 in ada_steps:
                    n = ada_steps.index(i - 1)
                    ps = PROJ.claim(pe, f"adT{n}")
                    PROJ.taken(pe, f"ada{n}")
                    for c in range(4):
                        last = mm(ps[:, 2 * c:2 * c + 2], ada_p[:, c * P:(c + 1) * P], K("sum4")[:, 0:2], True, True)
                    last.then_inc(PROJ.full, 1)
                if i in ada_steps:
                    n = ada_steps.index(i)
                    w = W.arrived(pe, f"ada{n}")
                    thin(PROJ.claim(pe, f"ada{n}"), silu_c, w, KD).then_inc(PROJ.full, 1)
                if i == 15:
                    PROJ.taken(pe, "fc", "fv0", "fv1", "fk0", "fk1")
                if i < NJ:
                    scores(i)
                if 1 <= i <= NJ:
                    turned(i - 1)
                if i >= 2:
                    output(i - 2)

            for n in range(4):
                w = W.arrived(pe, f"branch{n}")
                if n == 0:
                    PROJ.taken(pe, "gyT0", "gyT1")
                    OT.taken(pe, "o_sb2", "o_sb3")
                for f in range(KD // 2):
                    ps = PROJ.claim(pe, f"br{n}_{f}")
                    for k in range(2):
                        for c in range(4):
                            last = mm(ps[:, k * S:(k + 1) * S], w[:, c, (2 * f + k) * P:(2 * f + k + 1) * P],
                                      yT[:, 4 * n + c, :], c == 0, c == 3)
                    last.then_inc(PROJ.full, 1)
            pe.wait_ge(mixed_ready, 3 * KD // 2)
            for h in range(2):
                w = W.arrived(pe, f"out{h}")
                for t in range(TT):
                    ps = PROJ.claim(pe, f"wo{h}{t}")
                    for k in range(KD):
                        last = mm(ps[:, :], mixedT[:, k, t * P:(t + 1) * P], w[:, k, :], k == 0, k == KD - 1)
                    last.then_inc(PROJ.full, 1)

            turn_x("yT", 2 * TT)
            PROJ.taken(pe, "yT2", "yT3")
            pe.wait_ge(hT_cut, KD // 2)
            for i in range(8):
                for b in range(2):
                    w = X.arrived(pe, f"up{i}", b)
                    ps = PROJ.claim(pe, f"up{2 * i + b}")
                    for c in range(2):
                        for k in range(KD):
                            last = product(nc, ps[:, c * S:(c + 1) * S], [part[:, k, c * P:(c + 1) * P] for part in w],
                                           [part[:, k, :] for part in (hT_high, hT_low)], k == 0, k == KD - 1)
                    last.then_inc(PROJ.full, 1)
            downs = [SC.claim(pe, "down0"), SC.claim(pe, "down1"), OT.claim(pe, "down2"), OT.claim(pe, "down3")]
            for i in range(8):
                for b in range(2):
                    w = X.arrived(pe, f"down{i}", b)
                    pe.wait_ge(hidden_ready, 2 * i + b + 1)
                    for k in range(2):
                        c = 4 * i + 2 * b + k
                        for t in range(TT):
                            for h in range(2):
                                last = product(nc, downs[2 * t + h][:, :], [part[:, c, t * P:(t + 1) * P] for part in (hidden_high, hidden_low)],
                                               [part[:, k, 512 * h:512 * h + 512] for part in w], c == 0, c == FFK - 1)
                                if c == FFK - 1:
                                    last.then_inc((SC, OT)[t].full, 1)
                    if c < FFK - 1:
                        last.then_inc(down_used, 1)

        @block.scalar
        def _(act):
            link = Chain(act, act_self)

            def f(out, in_, func, **kw):
                return nc.scalar.activation(out, in_, func, **kw)

            def copy(out, in_, **kw):
                return f(out, in_, ACT.Copy, **kw)

            def take(name, out, in_=slice(None), **kw):
                ps = PROJ.arrived(act, name)
                copy(out, ps[:, in_], **kw).then_inc(PROJ.free(name), 1)

            def row_scale():
                for t in range(TT):
                    link(f(sq, x[:, t, :], ACT.Square, accum_out=stat[:, t:t + 1]))
                link(f(stat, stat, ACT.Ln, scale=1.0 / D, bias=eps))
                f(rstd, stat, ACT.Exp, scale=-0.5).then_inc(rstd_ready, 1)

            def take_hT(name, row, high=None):
                for c in range(4):
                    ps = PROJ.arrived(act, f"{name}{c}")
                    for k in range(2 * (high is not None)):
                        copy(high[:, 2 * c + k, :], ps[:, k * S:k * S + S], scale=cols[:, row + 2 * c + k:row + 2 * c + k + 1])
                    copy(hT[:, 2 * c, :], ps[:, 0:S], scale=cols[:, row + 2 * c:row + 2 * c + 1])
                    copy(hT[:, 2 * c + 1, :], ps[:, S:2 * S], scale=cols[:, row + 2 * c + 1:row + 2 * c + 2])\
                        .then_inc(PROJ.free(f"{name}{c}"), 1)

            def log1p_exp_neg_abs(out, in_):
                link(f(out, in_, ACT.Abs))
                link(f(out, out, ACT.Exp, scale=-1.0))
                return f(out, out, ACT.Ln, bias=one)

            def level_exp(k):
                act.wait_ge(lv_diff, k + 1)
                link(f(lv_d[:, k % 2], lv_d[:, k % 2], ACT.Abs))
                f(lv_d[:, k % 2], lv_d[:, k % 2], ACT.Exp, scale=-1.0 / GLA_TAU).then_inc(lv_exp, 1)

            def row_load(at, n, src):
                act.dma_start(rows[at:at + n, :], src).then_inc(rows_in, 16)

            row_load(ROW_MIX, KD, layer_of("norm_mix").rearrange("l (r p) -> (l r) p", p=P))
            row_load(ROW_FF, KD, layer_of("norm_ff").rearrange("l (r p) -> (l r) p", p=P))
            row_load(ROW_GATE, 4 * KD, layer_of("b_gate").rearrange("l (r p) -> (l r) p", p=P))
            row_load(ROW_GLB, 2, layer_of("gla_b_alpha").rearrange("l (r p) -> (l r) p", p=P))
            row_load(ROW_GLN, 1, layer_of("gla_norm"))
            row_load(ROW_PEK, 16, layer_of("nsa_cmp_pos_k").rearrange("l (r a) d -> (l r) (a d)", a=2))
            row_load(ROW_PEV, 16, layer_of("nsa_cmp_pos_v").rearrange("l (r a) d -> (l r) (a d)", a=2))
            act.dma_start(wk2, layer_of("nsa_cmp_wk2").rearrange("l (k p) n -> p (l k) n", p=P)).then_inc(small_in, 16)
            act.dma_start(wv2, layer_of("nsa_cmp_wv2").rearrange("l (k p) n -> p (l k) n", p=P)).then_inc(small_in, 16)
            act.dma_start(w_alpha[0:GLA_RANK, :], layer_of("gla_w_alpha").rearrange("l r n -> (l r) n")).then_inc(small_in, 16)
            act.dma_start(fox_b, layer_of("fox_b_f").partition_broadcast(P).rearrange("p l h -> p (l h)")).then_inc(small_in, 16)

            row_scale()
            ps = PROJ.arrived(act, "params")
            copy(cols[:, 0:ROW_GATE], ps[:, 0:ROW_GATE])
            copy(cols[:, ROW_GATE:ROW_GLB], ps[:, ROW_GATE:ROW_GLB], scale=-1.0)
            link(copy(cols[:, ROW_GLB:N_ROWS], ps[:, ROW_GLB:N_ROWS]))
            copy(kc_sin, ps[:, 0:N_CMP]).then_inc(PROJ.free("params"), 1)
            take_hT("xT", ROW_MIX)

            for i in range(2):
                take(f"q{i}", nsaT[:, 2 * i:2 * i + 2, :].rearrange("p a b -> p (a b)"), scale=HD ** -0.5)
            take("vs", vs.rearrange("p a b -> p (a b)"), slice(0, S))
            take("kskw", nsaT[:, 4:6, :].rearrange("p a b -> p (a b)"))
            ps = PROJ.arrived(act, "vwg")[:, 0:TT * 152].rearrange("p (t n) -> p t n", t=TT)
            copy(vw, ps[:, :, 0:P])
            f(g_nsa, ps[:, :, P:152], ACT.Exp, scale=-1.0).then_inc(PROJ.free("vwg"), 1)
            for i, name in enumerate(("hk", "hv")):
                take(name, hid_p[:, i], slice(0, CMP_HID))
            for i, name in enumerate(("hkT", "hvT")):
                ps = SC.arrived(act, name)[:, 0:4 * N_CMP].rearrange("p (m n) -> p m n", m=2)
                f(gelu_t, ps, ACT.Square).then_inc(gelu_x2, 1)
                act.wait_ge(gelu_in, i + 1)
                f(gelu_e, gelu_t, ACT.Exp, scale=-2.0 * GELU_C).then_inc(gelu_exp, 1)
                SC.taken(act, name)

            take("gq", glq.rearrange("p a b -> p (a b)"), scale=HD ** -0.5)
            take("gk", glk.rearrange("p a b -> p (a b)"))
            ps = PROJ.arrived(act, "ga")
            copy(glaT[0:GLA_RANK, :], ps[0:GLA_RANK, 0:S]).then_inc(PROJ.free("ga"), 1)
            ps = SC.arrived(act, "kc2")
            copy(kcT, ps[:, 0:N_CMP]).then_inc(SC.free("kc2"), 1)
            for t in range(TT):
                ps = PROJ.arrived(act, f"gg{t}")
                copy(glg[:, t, :], ps[:, :])
                f(gle[:, t, :], ps[:, :], ACT.Exp, scale=-1.0).then_inc(PROJ.free(f"gg{t}"), 1)
                if t == 0:
                    ps = SC.arrived(act, "vc2")
                    copy(vc[0:N_CMP], ps[0:N_CMP, 0:P].rearrange("p (g d) -> p g d", g=2)).then_inc(SC.free("vc2"), 1)
            ps = PROJ.arrived(act, "la")
            for c in range(2):
                link(f(gla_t[:, c, :], ps[:, c * S:(c + 1) * S], ACT.Abs, bias=cols[:, ROW_GLB + c:ROW_GLB + c + 1]))
            link(f(gla_t, gla_t, ACT.Exp, scale=-1.0))
            f(gla_t, gla_t, ACT.Ln, bias=one).then_inc(la_log, 1)
            for t in range(TT):
                take(f"gv{t}", glv[:, t, :])

            for g in range(2):
                act.wait_ge(cmp_in, g + 1)
                f(p_cmp[:, g], p_cmp[:, g], ACT.Exp).then_inc(cmp_exp, 1)

            level_exp(0)
            level_exp(1)
            for i, (name, out, kw) in enumerate((
                    ("sq0", sbq[:, 0:2, :], {"scale": HD ** -0.5}), ("sq1", sbq[:, 2:4, :], {"scale": HD ** -0.5}),
                    ("sk0", sbk[:, 0:2, :], {}), ("sk1", sbk[:, 2:4, :], {}),
                    ("sv0", sbv[:, 0:1, :], {}), ("sv1", sbv[:, 1:2, :], {}),
                    ("fq0", fxq[:, 0:2, :], {"scale": HD ** -0.5}), ("fq1", fxq[:, 2:4, :], {"scale": HD ** -0.5}),
                    ("fk0", fxk[:, 0:2, :], {}), ("fk1", fxk[:, 2:4, :], {}),
                    ("fv0", fxv[:, 0:1, :], {}), ("fv1", fxv[:, 1:2, :], {}))):
                take(name, out.rearrange("p a b -> p (a b)"), **kw)
                if 2 <= i + 1 <= len(LEVELS) - 2:
                    level_exp(i + 1)
            PROJ.taken(act, "ff")
            log1p_exp_neg_abs(log_f, fox_t).then_inc(fox_log, 1)

            for t in range(TT):
                ps = OT.arrived(act, f"go{t}")
                for h in range(GLA_H):
                    link(f(gla_t[:, 0, 0:P], ps[:, h * P:(h + 1) * P], ACT.Square, accum_out=gl_stat[:, t, h:h + 1]))
                link(f(gl_stat[:, t], gl_stat[:, t], ACT.Ln, scale=1.0 / GLA_DV, bias=eps))
                f(gl_rstd[:, t], gl_stat[:, t], ACT.Exp, scale=-0.5).then_inc(gl_scale, 1)

            for g in range(2):
                for i in range(2):
                    ps = PT.arrived(act, f"pc{g}{i}")
                    copy(pcT[g][0:N_CMP, 2 * i:2 * i + 2, :], ps[0:N_CMP, :].rearrange("p (c s) -> p c s", c=2))\
                        .then_inc(PT.free(f"pc{g}{i}"), 1)
            ps = PROJ.arrived(act, "fc")
            copy(fox_row[0:8, :], ps[0:8, 0:S]).then_inc(PROJ.free("fc"), 1)
            for t in range(TT):
                ps = PROJ.arrived(act, f"gyT{t}")
                copy(yT[:, 8:12, t * P:(t + 1) * P], ps[:, :].rearrange("p (h s) -> p h s", h=GLA_H),
                     scale=cols[:, ROW_GLN:ROW_GLN + 1]).then_inc(PROJ.free(f"gyT{t}"), 1)

            for i in range(NJ + 2):
                if i < 4 * KD:
                    ps = PROJ.arrived(act, f"g{i}")
                    f(gates[:, i, :], ps[:, 0:S], ACT.Exp, scale=-1.0, bias=cols[:, ROW_GATE + i:ROW_GATE + i + 1])\
                        .then_inc(PROJ.free(f"g{i}"), 1)
                if i - 1 in ada_steps:
                    n = ada_steps.index(i - 1)
                    ps = PROJ.arrived(act, f"adT{n}")
                    copy(chip["mod"][:, bass.ds(l * (2 * MODC) + 8 * n, 8)], ps[:, 0:8]).then_inc(PROJ.free(f"adT{n}"), 1)
                if i in ada_steps:
                    take(f"ada{ada_steps.index(i)}", ada_p)
                if i < NJ and jobs[i][0] == "sb":
                    ps = SC.arrived(act, f"s{i}")
                    log1p_exp_neg_abs(sb_u[:, i % 2], ps[:, 0:3 * P]).then_inc(sb_log, 1)
                elif i < NJ:
                    act.wait_ge(max_ready, i + 1)
                    ps = SC.arrived(act, f"s{i}")
                    f(prob[:, i % 2, 0:P], ps[:, 0:P], ACT.Exp, bias=neg_max[:, i % 2, 0:1],
                      accum_out=total[:, i % 2, 0:1])
                    f(prob[:, i % 2, P:3 * P], ps[:, P:3 * P], ACT.Exp, bias=neg_max[:, i % 2, 1:2],
                      accum_out=total[:, i % 2, 1:2]).then_inc(SC.free(f"s{i}"), 1)
                if 1 <= i <= NJ and jobs[i - 1][0] == "sb":
                    act.wait_ge(sb_later, i - 24)
                    ps = SC.arrived(act, f"s{i - 1}")
                    f(probT[:, (i - 1) % 2], ps[:, 0:3 * P], ACT.Exp).then_inc(SC.free(f"s{i - 1}"), 1)
                elif 1 <= i <= NJ:
                    ps = PT.arrived(act, f"p{i - 1}")
                    copy(probT[:, (i - 1) % 2], ps[:, 0:3 * P]).then_inc(PT.free(f"p{i - 1}"), 1)
                if i >= 2:
                    kind, c, par = jobs[i - 2]
                    if kind != "slc" and par == 1:
                        group, at = {"win": ("nsa", 0), "sb": ("sb", 4), "fox": ("fox", 12)}[kind]
                        ps = OT.arrived(act, f"o_{group}{c}")
                        copy(yT[:, at + c, :], ps[:, 0:S]).then_inc(OT.free(f"o_{group}{c}"), 1)

            for b in range(2):
                X.make_high(nc, act, "up0", b)
            PROJ.taken(act, "wo10", "wo11")
            row_scale()
            take_hT("yT", ROW_FF, hT_high)
            for b in range(2):
                X.make_high(nc, act, "up1", b)
            for i in range(FFK // 2):
                ps = PROJ.arrived(act, f"up{i}")
                part = hidden[:, 2 * i:2 * i + 2, :].rearrange("p a b -> p (a b)")
                f(part, ps[:, :], ACT.Relu).then_inc(PROJ.free(f"up{i}"), 1)
                PROJ.taken(act, f"up{i}")
                link(f(hidden_high[:, 2 * i:2 * i + 2, :].rearrange("p a b -> p (a b)"), part, ACT.Square))
                f(part, part, ACT.Square).then_inc(hidden_squared, 1)
                if i + 4 < len(halves):
                    X.make_high(nc, act, *halves[i + 4][0:2])
            for name, b, _ in halves[FFK // 2 + 4:]:
                X.make_high(nc, act, name, b)

        @block.vector
        def _(dve):
            link = Chain(dve, dve_self)
            vec = nc.vector

            def norm(count):
                dve.wait_ge(rstd_ready, count)
                for t in range(TT):
                    vec.tensor_scalar(xn[:, t, :], x[:, t, :], rstd[:, t:t + 1], None, ALU.mult).then_inc(xn_ready, 1)

            def sigmoid(e):
                link(vec.tensor_scalar_add(e, e, 1.0))
                link(vec.reciprocal(e, e))

            norm(1)
            link(vec.memset(att[:, :, 0:2].rearrange("p a b c d -> p a (b c d)"), 0.0))

            link(vec.memset(blk[:, :, :, 2 * N_CMP:THIN], 0.0))
            for i, name in enumerate(("kc", "vc")):
                if i == 0:
                    PROJ.taken(dve, "params")
                ps = PROJ.arrived(dve, name)
                row = (ROW_PEK, ROW_PEV)[i]
                for g in range(2):
                    tok = ps[:, g * S:(g + 1) * S].rearrange("p (n b r) -> p r b n", n=16, r=2)
                    for r in range(2):
                        h = slice(r * HD, (r + 1) * HD)
                        for a in range(2):
                            last = vec.tensor_tensor(blk[h, i, 8 * a:8 * a + 8, g * N_CMP:(g + 1) * N_CMP], tok[h, r, :, a:a + N_CMP],
                                                     cols[h, row + 8 * a:row + 8 * a + 8].unsqueeze(2).to_broadcast([HD, 8, N_CMP]),
                                                     ALU.add)
                last.then_inc(PROJ.free(name), 1)

            cos2 = cos.unsqueeze(1).to_broadcast([P, 2, S])
            sin2 = sin.unsqueeze(1).to_broadcast([P, 2, S])
            for i in range(3):
                ps = PROJ.arrived(dve, f"rope{i}")
                part = nsaT[:, 2 * i:2 * i + 2, :]
                turn = mix_t[:, 0, :].rearrange("p (a b) -> p a b", a=2)
                vec.tensor_tensor(turn, ps[:, :].rearrange("p (a b) -> p a b", a=2), sin2, ALU.mult)\
                    .then_inc(PROJ.free(f"rope{i}"), 1)
                link(vec.tensor_tensor(part, part, cos2, ALU.mult))
                PROJ.taken(dve, f"rope{i}")
                vec.tensor_tensor(part, part, turn, ALU.add).then_inc(roped, 1)
                dve.wait_ge(roped, i + 1)

            for i, name in enumerate(("hkT", "hvT")):
                ps = SC.arrived(dve, name)[:, 0:4 * N_CMP].rearrange("p (m n) -> p m n", m=2)
                dve.wait_ge(gelu_x2, i + 1)
                link(vec.tensor_scalar(gelu_t, gelu_t, 0.044715, 1.0, ALU.mult, ALU.add))
                vec.tensor_tensor(gelu_t, gelu_t, ps, ALU.mult).then_inc(gelu_in, 1)
                dve.wait_ge(gelu_exp, i + 1)
                sigmoid(gelu_e)
                vec.tensor_tensor(hid_c[:, i], gelu_e, ps, ALU.mult).then_inc(SC.free(name), 1)
            last_tok = CMP_LEN - 1
            ps = SC.arrived(dve, "rope_kc")
            vec.tensor_tensor(kc_sin, ps[:, 0:N_CMP], sin[:, last_tok:S:CMP_STRIDE], ALU.mult).then_inc(SC.free("rope_kc"), 1)
            link(vec.tensor_tensor(kcT, kcT, cos[:, last_tok:S:CMP_STRIDE], ALU.mult))
            SC.taken(dve, "rope_kc")
            vec.tensor_tensor(kcT, kcT, kc_sin, ALU.add).then_inc(roped, 1)
            PROJ.taken(dve, "vwg")
            sigmoid(g_nsa)
            nsa_gate = g_nsa.rearrange("p t (h k) -> p k h t", k=3)

            for t in range(TT):
                PROJ.taken(dve, f"gg{t}")
                sigmoid(gle[:, t, :])
                link(vec.tensor_tensor(gle[:, t, :], gle[:, t, :], glg[:, t, :], ALU.mult))
            dve.wait_ge(la_log, 1)
            ps = PROJ.arrived(dve, "la")
            vec.tensor_scalar(gla_b[:, 0, :], ps[:, 0:S], cols[:, ROW_GLB:ROW_GLB + 1], 0.0, ALU.add, ALU.min)
            vec.tensor_scalar(gla_b[:, 1, :], ps[:, S:2 * S], cols[:, ROW_GLB + 1:ROW_GLB + 2], 0.0, ALU.add, ALU.min)\
                .then_inc(PROJ.free("la"), 1)
            PROJ.taken(dve, "la")
            link(vec.tensor_tensor(gla_t, gla_b, gla_t, ALU.subtract))
            for c in range(2):
                link(vec.tensor_tensor_scan(gla_b[:, c, :], K("ones"), gla_t[:, c, :], 0.0, ALU.mult, ALU.add))

            bias = K("cmp_bias").rearrange("p (t n) -> p t n", t=TT).unsqueeze(1).to_broadcast([P, 4, TT, N_CMP])
            seen = K("cmp_seen").rearrange("p (t n) -> p t n", t=TT).unsqueeze(1).to_broadcast([P, 4, TT, N_CMP])
            for g in range(2):
                ps = SC.arrived(dve, f"cmp{g}")
                pc, st = p_cmp[:, g], stat_cmp[:, g]
                wide = st.unsqueeze(3).to_broadcast([P, 4, TT, N_CMP])
                vec.tensor_tensor(pc, ps[:, 0:4 * TT * N_CMP].rearrange("p (c t n) -> p c t n", c=4, t=TT), bias, ALU.add)\
                    .then_inc(SC.free(f"cmp{g}"), 1)
                SC.taken(dve, f"cmp{g}")
                link(vec.tensor_reduce(st, pc, axis=AX.X, op=ALU.max))
                vec.tensor_tensor(pc, pc, wide, ALU.subtract).then_inc(cmp_in, 1)
                dve.wait_ge(cmp_exp, g + 1)
                link(vec.tensor_tensor(pc, pc, seen, ALU.mult))
                link(vec.tensor_reduce(st, pc, axis=AX.X, op=ALU.add))
                link(vec.tensor_scalar_max(st, st, 1e-30))
                link(vec.reciprocal(st, st))
                link(vec.tensor_tensor(st, st, nsa_gate[:, 0, 4 * g:4 * g + 4, :], ALU.mult))
                vec.tensor_tensor(pc, pc, wide, ALU.mult).then_inc(cmp_ready, 1)

            prepared = [0]

            def prepare(n):
                h, k = LEVELS[n], prepared[0]
                prepared[0] += 1
                b = gla_b.rearrange("p c s -> p (c s)").rearrange("p (n j) -> p n j", j=2 * h)
                d = lv_d[:, k % 2]
                vec.tensor_tensor(d.rearrange("p (n j) -> p n j", j=2 * h), b,
                                  b[:, :, h - 1:h].to_broadcast([P, 512 // (2 * h), 2 * h]), ALU.subtract).then_inc(lv_diff, 1)
                dve.wait_ge(lv_exp, k + 1)
                vec.tensor_tensor(lv_q[:, k % 2], glq.rearrange("p c s -> p (c s)"), d, ALU.mult)
                vec.tensor_tensor(lv_k[:, k % 2], glk.rearrange("p c s -> p (c s)"), d, ALU.mult).then_inc(lv_ready, 1)

            def merge(n):
                for par in range(2):
                    name = f"lv{n}_{par}"
                    ps = PT.arrived(dve, name)
                    if LEVELS[n] == P:
                        vec.tensor_copy(att[:, par, 2].rearrange("p c t -> p (c t)"), ps[:, 0:2 * P])\
                            .then_inc(PT.free(name), 1)
                    else:
                        vec.copy_predicated(att[:, par, 0:2].rearrange("p b c t -> p (b c) t"),
                                            level_mask[:, n - 1:n, :].to_broadcast([P, 4, P]),
                                            ps[:, :].rearrange("p (a t) -> p a t", a=4)).then_inc(PT.free(name), 1)
                PT.taken(dve, f"lv{n}_0", f"lv{n}_1")

            PROJ.taken(dve, "gq", "gk")
            prepare(0)
            prepare(2)
            merge(0)
            merge(1)
            for n in range(3, len(LEVELS)):
                prepare(n)
                merge(n - 1)
            merge(len(LEVELS) - 1)

            dve.wait_ge(small_in, 4 * 16)
            ps = PROJ.arrived(dve, "ff")
            vec.tensor_tensor(fox_t, ps[:, 0:TT * 8].rearrange("p (t h) -> p t h", t=TT),
                              fox_b.unsqueeze(1).to_broadcast([P, TT, 8]), ALU.add).then_inc(PROJ.free("ff"), 1)
            dve.wait_ge(fox_log, 1)
            vec.scalar_tensor_tensor(log_f, fox_t, 0.0, log_f, ALU.min, ALU.subtract).then_inc(fox_ready, 1)

            for t in range(TT):
                dve.wait_ge(gl_scale, t + 1)
                ps = OT.arrived(dve, f"go{t}")
                for h in range(GLA_H):
                    dv = slice(h * GLA_DV, (h + 1) * GLA_DV)
                    last = vec.scalar_tensor_tensor(gle[:, t, dv], ps[:, dv], gl_rstd[:, t, h:h + 1], gle[:, t, dv],
                                                    ALU.mult, ALU.mult)
                last.then_inc(OT.free(f"go{t}"), 1)

            for i in range(NJ):
                kind, c, par = jobs[i]
                if kind != "sb":
                    ps = SC.arrived(dve, f"s{i}")
                    vec.tensor_reduce(neg_max[:, i % 2, 0:1], ps[:, 0:P], axis=AX.X, op=ALU.max, negate=True)
                    vec.tensor_reduce(neg_max[:, i % 2, 1:2], ps[:, P:3 * P], axis=AX.X, op=ALU.max, negate=True)\
                        .then_inc(max_ready, 1)
                PROJ.taken(dve, f"g{i}")
                sigmoid(gates[:, i, :])
                if kind == "sb":
                    dve.wait_ge(sb_log, i - 23)
                    ps = SC.arrived(dve, f"s{i}")
                    vec.scalar_tensor_tensor(sb_p[:, i % 2], ps[:, 0:3 * P], 0.0, sb_u[:, i % 2], ALU.max, ALU.add)\
                        .then_inc(sb_soft, 1)
                    continue
                SC.taken(dve, f"s{i}")
                link(vec.reciprocal(total[:, i % 2], total[:, i % 2]))
                if kind != "fox":
                    branch_of = 1 if kind == "slc" else 2
                    link(vec.tensor_tensor(total[:, i % 2], total[:, i % 2], nsa_gate[:, branch_of, 4 * par + c, :], ALU.mult))
                vec.tensor_scalar(prob[:, i % 2, 0:P], prob[:, i % 2, 0:P], total[:, i % 2, 0:1], None, ALU.mult)
                vec.tensor_scalar(prob[:, i % 2, P:3 * P], prob[:, i % 2, P:3 * P], total[:, i % 2, 1:2], None, ALU.mult)\
                    .then_inc(prob_ready, 1)

            for n in range(4):
                for fc in range(KD // 2):
                    name = f"br{n}_{fc}"
                    ps = PROJ.arrived(dve, name)[:, :].rearrange("p (a b) -> p a b", a=2)
                    gate = gates[:, n * KD + 2 * fc:n * KD + 2 * fc + 2, :]
                    mixed = mixedT[:, 2 * fc:2 * fc + 2, :]
                    if n == 0:
                        vec.tensor_tensor(mixed, ps, gate, ALU.mult).then_inc(PROJ.free(name), 1)
                        continue
                    part = mix_t[:, fc % 2, :].rearrange("p (a b) -> p a b", a=2)
                    vec.tensor_tensor(part, ps, gate, ALU.mult).then_inc(PROJ.free(name), 1)
                    PROJ.taken(dve, name)
                    vec.tensor_tensor(mixed, mixed, part, ALU.add).then_inc(mixed_ready, 1)
                if n > 0:
                    dve.wait_ge(mixed_ready, 4 * n)
            for b in range(2):
                X.make_low(nc, dve, "up0", b)
            for h in range(2):
                for t in range(TT):
                    ps = PROJ.arrived(dve, f"wo{h}{t}")
                    part = x[:, t, 512 * h:512 * h + 512]
                    vec.tensor_tensor(part, part, ps[:, :], ALU.add).then_inc(PROJ.free(f"wo{h}{t}"), 1)
            norm(2)

            for c in range(KD // 2):
                PROJ.taken(dve, f"yT{c}")
                part = slice(2 * c, 2 * c + 2)
                vec.tensor_tensor(hT_low[:, part, :], hT[:, part, :], hT_high[:, part, :].bitcast(F32), ALU.subtract)\
                    .then_inc(hT_cut, 1)
            for b in range(2):
                X.make_low(nc, dve, "up1", b)
            for i in range(FFK // 2):
                dve.wait_ge(hidden_squared, i + 1)
                part = slice(2 * i, 2 * i + 2)
                vec.tensor_tensor(hidden_low[:, part, :], hidden[:, part, :], hidden_high[:, part, :].bitcast(F32), ALU.subtract)\
                    .then_inc(hidden_ready, 1)
                if i + 4 < len(halves):
                    X.make_low(nc, dve, *halves[i + 4][0:2])
            for name, b, _ in halves[FFK // 2 + 4:]:
                X.make_low(nc, dve, name, b)
            for t in range(TT):
                for h in range(2):
                    name = f"down{2 * t + h}"
                    bank = (SC, OT)[t]
                    ps = bank.arrived(dve, name)
                    part = x[:, t, 512 * h:512 * h + 512]
                    vec.tensor_tensor(part, part, ps[:, :], ALU.add).then_inc(bank.free(name), 1)


def prologue(nc, T, dram, sem, chip):
    x, consts, masks, cos, sin = (chip[n] for n in ("x", "consts", "masks", "cos", "sin"))
    work = Carver(chip["work"])
    pos, rows = work.take(S), work.take(P)
    cols, silu_c = chip["cols2"], chip["silu_c"]
    silu_t = work.take(2, KD)
    ident = consts[:, T["f32"]["ident"][0]:sum(T["f32"]["ident"])]
    angle, turns, part = work.take(S), work.take(S), work.take(S)
    tables_in, x_in = sem("tables_in"), sem("x_in")
    sin_arg, cos_arg = sem("sin_arg"), sem("cos_arg")
    sin_cos = sem("sin_cos")
    rows_in = sem("rows2_in")
    cols_full = sem("cols2_full")
    silu_exp = sem("silu_exp")
    pro_self, silu_done = sem("pro_self"), sem("silu_done")

    with nc.Block() as block:

        @block.sync
        def _(sp):
            sp.dma_start(pos.bitcast(I32), dram["positions"].partition_broadcast(P).rearrange("p b s -> p (b s)"))\
                .then_inc(tables_in, 16)
            sp.dma_start(consts[:, :], dram["f32_tables"]).then_inc(tables_in, 16)
            sp.dma_start(masks[:, :], dram["bf16_tables"]).then_inc(tables_in, 16)
            sp.dma_start(x, dram["x"].rearrange("b (t p) d -> p (b t) d", p=P)).then_inc(x_in, 16)
            sp.wait_ge(x_in, 16)

        @block.tensor
        def _(pe):
            pe.wait_ge(tables_in, 3 * 16)
            pe.wait_ge(rows_in, 9 * 16)
            nc.tensor.transpose(chip["psum"][0][:, 0:N_ROWS2], rows[0:N_ROWS2, :], ident[0:N_ROWS2, 0:N_ROWS2])\
                .then_inc(cols_full, 1)

        @block.vector
        def _(dve):
            link = Chain(dve, pro_self)
            vec = nc.vector
            link(vec.memset(silu_c, 0.0))
            inv = consts[:, T["f32"]["inv_freq"][0]:T["f32"]["inv_freq"][0] + 1]
            dve.wait_ge(tables_in, 3 * 16)
            link(vec.tensor_copy(angle, pos.bitcast(I32)))
            link(vec.tensor_scalar(angle, angle, inv, None, ALU.mult))
            link(vec.tensor_scalar(turns, angle, float(1 / (2 * np.pi)), None, ALU.mult))
            link(vec.tensor_scalar(turns, turns, MAGIC, None, ALU.add))
            link(vec.tensor_scalar(turns, turns, -MAGIC, None, ALU.add))
            for c in TWO_PI_PARTS:
                link(vec.scalar_tensor_tensor(angle, turns, -c, angle, ALU.mult, ALU.add))
            limit = 3.1415925
            vec.tensor_scalar(part, angle, limit, -limit, ALU.min, ALU.max).then_inc(sin_arg, 1)
            link(vec.tensor_scalar(angle, angle, float(np.pi / 2), None, ALU.add))
            link(vec.tensor_scalar(turns, angle, float(np.pi), float(-2 * np.pi), ALU.is_gt, ALU.mult))
            link(vec.tensor_tensor(angle, angle, turns, ALU.add))
            vec.tensor_scalar(angle, angle, limit, -limit, ALU.min, ALU.max).then_inc(cos_arg, 1)
            dve.wait_ge(silu_exp, 1)
            link(vec.tensor_scalar_add(silu_t, silu_t, 1.0))
            link(vec.reciprocal(silu_t, silu_t))
            vec.tensor_tensor(silu_c[:, :, 0:2].rearrange("p k s -> p s k"), silu_t,
                              cols[:, ROW_C:N_ROWS2].rearrange("p (s k) -> p s k", s=2), ALU.mult)

        @block.scalar
        def _(act):
            def row_load(at, n, src, c0=0, width=P):
                act.dma_start(rows[at:at + n, c0:c0 + width], src).then_inc(rows_in, 16)

            row_load(ROW_ADA, 2 * MODC, dram["b_ada_2"].rearrange("l (r p) -> (l r) p", p=P))
            for half in range(2):
                row_load(ROW_QN, 1, dram["gqa_q_norm_2"], half * HD, HD)
                row_load(ROW_KN, 1, dram["gqa_k_norm_2"], half * HD, HD)
            row_load(ROW_MQN, 3, dram["mla_q_norm_2"].rearrange("l (r p) -> (l r) p", p=P))
            row_load(ROW_MKN, 2, dram["mla_kv_norm_2"].rearrange("l (r p) -> (l r) p", p=P))
            c_rows = dram["c_2"].rearrange("b (r p) -> (b r) p", p=P)
            row_load(ROW_C, KD, c_rows)
            act.dma_start(rows[ROW_C + KD:N_ROWS2, :], dram["c_ctx_2"].rearrange("(r p) -> r p", p=P)).then_inc(rows_in, 16)
            act.wait_ge(cols_full, 1)
            ps = chip["psum"][0]
            nc.scalar.activation(cols, ps[:, 0:N_ROWS2], ACT.Copy)
            nc.scalar.activation(silu_t, ps[:, ROW_C:N_ROWS2].rearrange("p (s k) -> p s k", s=2), ACT.Exp, scale=-1.0)\
                .then_inc(silu_exp, 1)
            act.wait_ge(sin_arg, 1)
            nc.scalar.activation(sin, part, ACT.Sin)
            act.wait_ge(cos_arg, 1)
            nc.scalar.activation(cos, angle, ACT.Sin)


def second_block(nc, T, dram, out, sem, chip):
    x, consts, mod, cols2 = chip["x"], chip["consts"], chip["mod"], chip["cols2"]
    work = Carver(chip["work"])

    xc = work.take(TT, D)
    hT = work.take(KD, 2 * S)
    gate_rows = work.take(2, D)
    ln_rows = work.take(2, D)
    grid = work.take(P + 2 * S)
    z = work.take(2, 512)
    small = Carver(chip["cos"])
    ln_stats, ln_mv, ln_rs = small.take(4, 2, 6), small.take(4, 2), small.take(4)
    neg_max, total = small.take(6, 2), small.take(6, 2)
    nf_stat = small.take(TT)
    late = work.at
    gate_src = z.rearrange("p a b -> p (a b)").rearrange("p (k j) -> p k j", k=KD)
    grid_swap, grid_cos, grid_sin = grid[:, 0:P], grid[:, P:P + S], grid[:, P + S:P + 2 * S]
    g = Carver(chip["work"], late)
    g_qT = g.take(KD, 2 * S)
    g_kT = g.take(KV_HEADS, 2 * S)
    g_k = g.take(2, 2 * S)
    g_v = g.take(4, KV_HEADS * HD)
    g_prob, g_turn = g.take(6, 512), g.take(2, 6, S)
    g_yT = g.take(KD, 2 * S)
    g_sq, g_rs, g_rot = g_prob[:, 0:2], g_prob[:, 2:4], g_prob[:, 4, 0:S]
    nf_row, nf_junk = (g_yT.rearrange("p a b -> p (a b)")[:, n * D:(n + 1) * D] for n in range(2))
    m = Carver(chip["work"], late)
    m_kT = m.take(HEADS, 2 * S)
    m_qT = m.take(HEADS, S)
    m_v = m.take(4, HEADS * HD)
    m_cq, m_ckv = m.take(3, S), m.take(2, 2 * S)
    early = Carver(hT.rearrange("p a b -> p (a b)"))
    m_prob, m_turn = early.take(4, 512), early.take(2, 4, S)
    m_yT = xc.rearrange("p a b -> p (a b)").rearrange("p (c s) -> p c s", c=KD)
    flat_xc = xc.rearrange("p a b -> p (a b)")
    m_sqkv = flat_xc[:, 0:4 * S].rearrange("p (c s) -> p c s", c=2)
    m_sqq = flat_xc[:, 4 * S:7 * S].rearrange("p (c s) -> p c s", c=3)
    m_rskv, m_rsq = z[:, 0], z[:, 1, 0:S]
    m_kpe, m_rot = gate_rows[:, 1, 0:512], gate_rows[:, 1, 512:1024]
    rounded = chip["rounded"]
    half_high = [rounded(f"half_high{n}", late + n * SPLIT_HALF, SPLIT_HALF) for n in range(3)]
    at = late + 3 * SPLIT_HALF
    hT_low, hT_high = rounded("hT_low2", TT * D, KD, 2 * S), rounded("hT_high2", at, KD, 2 * S)
    at += KD * 2 * S
    hidden = Carver(chip["work"], at).take(KD, 2 * S)
    hidden_low, hidden_high = rounded("hidden_low2", at, KD, 2 * S), rounded("hidden_high2", at + KD * 2 * S, KD, 2 * S)

    tok = [x[:, 0, :], x[:, 1, :], xc[:, 0, :], xc[:, 1, :]]
    K = lambda name: consts[:, T["f32"][name][0]:sum(T["f32"][name])]
    ident, eps = K("ident"), K("eps")

    def mod_col(i, part, k, s):
        at = ((i * MOD_PARTS + part) * KD + k) * 2 + s
        return mod[:, at:at + 1]

    NT = [4, 2]
    UNITS = [3, 2]
    NORMED = 10
    XT_ORDER = [(2, 3, 0, 1), (0, 1, 2, 3)]
    UP_PER = [1, 2]
    GM_AT = [2, 5]
    QUARTERS = FFK // KD

    def gate_fills(i, kind, s):
        return [f"{i}{kind}{s}{h}" for h in range(2)]

    proj, score, turned, outs = [], [], [], []
    for i in range(DEPTH):
        streams = NT[i] // TT
        proj += [f"{i}xT{t}{h}" for t in XT_ORDER[i] for h in range(2)]
        if i == 0:
            proj += ["0v0"] + gate_fills(0, "ga", 0) + ["0v1"] + gate_fills(0, "ga", 1)
            proj += [f"0a{n}" for n in range(NORMED)]
            score += [f"0ms{n}" for n in range(NORMED)]
            turned += [f"0rt{n}" for n in range(NORMED)]
        else:
            proj += ["1ckv0"] + gate_fills(1, "ga", 0) + ["1ckv1", "1kpe", "1cq0", "1cq1"]
            proj += [f"1kn{j}" for j in range(8)] + [f"1v{j}" for j in range(8)] + [f"1qf{j}" for j in range(8)]
            score += ["1mskv", "1msq"]
            turned += ["1rtk"] + [f"1rt{j}" for j in range(8)]
        units = [(h, u) for h in range(HEADS) for u in range(UNITS[i])]
        score += [f"{i}s{h}_{u}" for h, u in units]
        turned += [f"{i}t{h}_{u}" for h, u in units]
        outs += [f"{i}o{h}" for h in range(HEADS)] + [f"{i}wo{t}{h}" for t in range(NT[i]) for h in range(2)]
        proj += [f"{i}hT{t}{h}" for t in range(NT[i]) for h in range(2)]
        for q in range(QUARTERS):
            for n in range(KD // UP_PER[i]):
                proj.append(f"{i}up{q}_{n}")
                for s in range(streams):
                    if q == 0 and n == GM_AT[s]:
                        proj += gate_fills(i, "gm", s)
            score += [f"{i}down{q}0{t}" for t in range(2)]
            outs += [f"{i}down{q}0{t}" for t in range(2, NT[i])]
            turned += [f"{i}down{q}1{t}" for t in range(2)]
            proj += [f"{i}down{q}1{t}" for t in range(2, NT[i])]
    PROJ = Banks(sem, "proj2", chip["psum"][0:2], proj)
    SC = Banks(sem, "score2", chip["psum"][2:4], score)
    PT = Banks(sem, "turn2", chip["psum"][4:6], turned)
    OT = Banks(sem, "out2", chip["psum"][6:8], outs)

    def down_banks(h, t):
        return ((SC, OT), (PT, PROJ))[h][t // 2]

    whole = (slice(None), slice(None), slice(None))
    down_used = sem("down_used2")

    def chunked(a):
        return a.rearrange("(k p) n -> p k n", p=P)

    def done(bank, name):
        return bank.full, bank.order[name] + 1

    def up_done(i, q, j, b):
        return done(PROJ, f"{i}up{q}_{(4 * j + 2 * b + 1) // UP_PER[i]}")

    halves, freed = [], []
    w_qkv, w_in = chunked(dram["gqa_w_qkv_2"][0]), chunked(dram["mla_w_in_2"][0])
    w_uq = chunked(dram["mla_w_uq_2"][0])
    w_ukv = dram["mla_w_ukv_2"][0].rearrange("(k p) (h e d) -> k e p h d", p=P, e=2, d=HD)
    qw, kvw = HEADS * HD, 2 * KV_HEADS * HD
    uq_half = HEADS * MLA_QK // 2
    tiles = [("0kv", KD, kvw, [(whole, w_qkv[:, :, qw:qw + kvw])], done(PROJ, "0a1"))]
    tiles += [(f"0q{j}", KD, 512, [(whole, w_qkv[:, :, 512 * j:512 * j + 512])], done(PROJ, f"0a{4 * j + 5}"))
              for j in range(2)]
    for i in range(DEPTH):
        if i == 1:
            tiles += [("1ckv", KD, KV_RANK + PE_DIM, [(whole, w_in[:, :, Q_RANK:])], done(PROJ, "1kpe")),
                      ("1cq", KD, Q_RANK, [(whole, w_in[:, :, 0:Q_RANK])], done(PROJ, "1cq1")),
                      ("1ukv", 4, HEADS * HD, [((slice(None), 2 * e + k, slice(None)), w_ukv[k, e])
                                               for e in range(2) for k in range(2)], done(PROJ, "1v7"))]
            tiles += [(f"1uq{j}", 3, uq_half, [(whole, w_uq[:, :, uq_half * j:uq_half * (j + 1)])],
                       done(PROJ, f"1qf{4 * j + 3}")) for j in range(2)]
        w_o = chunked(dram[("gqa_w_o_2", "mla_w_o_2")[i]][0])
        w1, w2 = chunked(dram["mlp_w1_2"][i]), chunked(dram["mlp_w2_2"][i])
        last = NT[i] - 1
        tiles += [(f"{i}wo{h}", KD, 512, [(whole, w_o[:, :, 512 * h:512 * h + 512])], done(OT, f"{i}wo{last}{h}"))
                  for h in range(2)]
        for q in range(QUARTERS):
            for j in range(2):
                at = (2 * q + j) * 512
                tiles.append((f"{i}up{q}{j}", KD, 512, [(whole, w1[:, :, at:at + 512])], up_done(i, q, j, 1)))
                halves += [(f"{i}up{q}{j}", b, "n") for b in range(2)]
                freed += [up_done(i, q, j, b) for b in range(2)]
            for h in range(2):
                tiles.append((f"{i}down{q}{h}", KD, 512, [(whole, w2[:, KD * q:KD * q + KD, 512 * h:512 * h + 512])],
                              done(down_banks(h, last), f"{i}down{q}{h}{last}")))
                halves += [(f"{i}down{q}{h}", b, "k") for b in range(2)]
                freed += [(down_used, 8 * i + 2 * q + h + 1), done(down_banks(h, last), f"{i}down{q}{h}{last}")]
    W = Weights(sem, "w2", chip["ring"], tiles)
    X = Split(sem, "mlp", W, chip["ring_low"], half_high, halves, freed)

    first_in = sem("first_in")
    grid_in = sem("grid_in")
    ln_in = sem("ln_in")
    out_in = sem("out_done")
    nf_scale = sem("nf_scale")
    x_first = sem("x_first")
    mod_ready = sem("mod_ready")
    gate_wide = sem("gate_wide")
    rs_ready = sem("rs_ready")
    normed = sem("normed")
    roped = sem("roped2")
    k_copied = sem("k_copied")
    max_ready = sem("max_ready2")
    prob_ready = sem("prob_ready2")
    var_ready = sem("var_ready")
    ln_scale = sem("ln_scale")
    x_ready = sem("x_ready")
    hT_cut = sem("hT_cut2")
    hidden_squared = sem("hidden_squared2")
    hidden_ready = sem("hidden_ready2")
    kpe_ready = sem("kpe_ready")
    kpe_zero = sem("kpe_zero")
    act_self, dve_self = sem("act_self2"), sem("dve_self2")

    ln_order = [(i, j, t) for i in range(DEPTH) for j in range(2) for t in range(NT[i])]
    ln_count = {key: n + 1 for n, key in enumerate(ln_order)}
    gate_order = [(i, kind, s) for i in range(DEPTH) for kind in ("ga", "gm") for s in range(NT[i] // TT)]
    gate_count = {key: n + 1 for n, key in enumerate(gate_order)}
    def halves_of(i):
        return halves[len(halves) // DEPTH * i:len(halves) // DEPTH * (i + 1)]

    unit_base = [0, HEADS * UNITS[0]]
    up_base = [0, FFK // UP_PER[0]]
    cut_base = [0, NT[0]]

    def unit(i, h, u):
        return unit_base[i] + h * UNITS[i] + u

    def buffers(i):
        return ((g_prob, g_turn, g_yT, 2 * S), (m_prob, m_turn, m_yT, S))[i]

    def x_arrived(eng, i, t):
        if i == 1:
            eng.wait_ge(x_ready, ln_count[0, 1, t])
        elif t < TT:
            eng.wait_ge(x_first, t + 1)
        else:
            eng.wait_ge(first_in, 5 * 16)

    with nc.Block() as block:

        @block.sync
        def _(sp):
            W.load(sp)
            for t in range(TT):
                sp.wait_ge(x_ready, ln_count[1, 1, t])
                sp.dma_start(out.rearrange("b (t p) d -> p (b t) d", p=P)[:, t, :], x[:, t, :]).then_inc(out_in, 16)
            sp.wait_ge(out_in, TT * 16)

        @block.tensor
        def _(pe):
            def mm(o, lhsT, rhs, start, stop):
                return nc.tensor.matmul(o, lhsT, rhs, start=start, stop=stop)

            def turn(o, src):
                return nc.tensor.transpose(o, src, ident)

            def turn_tile(names, t):
                for h, name in enumerate(names):
                    ps = PROJ.claim(pe, name)
                    for k in range(4):
                        last = turn(ps[:, k * P:k * P + P], tok[t][:, (4 * h + k) * P:(4 * h + k + 1) * P])
                    last.then_inc(PROJ.full, 1)

            def turn_gate(i, kind, s):
                pe.wait_ge(gate_wide, gate_count[i, kind, s])
                for h, name in enumerate(gate_fills(i, kind, s)):
                    ps = PROJ.claim(pe, name)
                    for k in range(4):
                        last = turn(ps[:, k * P:k * P + P], gate_src[:, 4 * h + k, :])
                    last.then_inc(PROJ.full, 1)

            def gemm_T(o, w, cols, n=2 * S, chunks=KD, src=None):
                src = hT if src is None else src
                for k in range(chunks):
                    last = mm(o, w[:, k, cols], src[:, k, 0:n], k == 0, k == chunks - 1)
                return last

            def gqa_project():
                w = W.arrived(pe, "0kv")
                kw = KV_HEADS * HD
                for j in range(2):
                    ps = PROJ.claim(pe, f"0v{j}")
                    for b in range(2):
                        for k in range(KD):
                            t = 2 * j + b
                            last = mm(ps[:, b * kw:(b + 1) * kw], hT[:, k, t * P:t * P + P], w[:, k, kw:2 * kw],
                                      k == 0, k == KD - 1)
                    last.then_inc(PROJ.full, 1)
                    turn_gate(0, "ga", j)
                for n in range(NORMED + 2):
                    if n < NORMED:
                        if n >= 2 and n % 4 == 2:
                            w = W.arrived(pe, f"0q{n // 4}")
                        c = n if n < 2 else (n - 2) % 4
                        gemm_T(PROJ.claim(pe, f"0a{n}")[:, :], w, slice(c * P, c * P + P)).then_inc(PROJ.full, 1)
                    if 1 <= n <= NORMED:
                        PROJ.taken(pe, f"0a{n - 1}")
                        mm(SC.claim(pe, f"0ms{n - 1}")[:, :], K("head_mean"), g_sq[:, (n - 1) % 2], True, True)\
                            .then_inc(SC.full, 1)
                    if n >= 2:
                        pe.wait_ge(normed, n - 1)
                        raw = g_k[:, n - 2] if n < 4 else g_qT[:, n - 4]
                        mm(PT.claim(pe, f"0rt{n - 2}")[:, 0:S], grid_swap, raw[:, 0:S], True, True).then_inc(PT.full, 1)

            def mla_project():
                w = W.arrived(pe, "1ckv")
                for j in range(2):
                    gemm_T(PROJ.claim(pe, f"1ckv{j}")[:, :], w, slice(j * P, j * P + P)).then_inc(PROJ.full, 1)
                    if j == 0:
                        turn_gate(1, "ga", 0)
                gemm_T(PROJ.claim(pe, "1kpe")[HD:MLA_QK, :], w, slice(KV_RANK, KV_RANK + PE_DIM)).then_inc(PROJ.full, 1)
                w = W.arrived(pe, "1cq")
                for j in range(2):
                    ps = PROJ.claim(pe, f"1cq{j}")
                    for b in range(2 - j):
                        c = 2 * j + b
                        last = gemm_T(ps[:, b * S:b * S + S], w, slice(c * P, c * P + P), S)
                    last.then_inc(PROJ.full, 1)
                PROJ.taken(pe, "1ckv0", "1ckv1")
                ps = SC.claim(pe, "1mskv")
                for c in range(2):
                    last = mm(ps[:, :], K("ones")[:, 0:P], m_sqkv[:, c, :], c == 0, c == 1)
                last.then_inc(SC.full, 1)
                PROJ.taken(pe, "1cq0", "1cq1")
                ps = SC.claim(pe, "1msq")
                for c in range(3):
                    last = mm(ps[:, 0:S], K("ones")[:, 0:P], m_sqq[:, c, :], c == 0, c == 2)
                last.then_inc(SC.full, 1)
                PROJ.taken(pe, "1kpe")
                pe.wait_ge(kpe_zero, 1)
                pe.wait_ge(grid_in, 16)
                mm(PT.claim(pe, "1rtk")[0:MLA_QK, 0:S], grid_swap[0:MLA_QK, 0:MLA_QK], m_kpe[0:MLA_QK, 0:S], True, True)\
                    .then_inc(PT.full, 1)
                w = W.arrived(pe, "1ukv")
                pe.wait_ge(normed, NORMED + 1)
                for j in range(8):
                    gemm_T(PROJ.claim(pe, f"1kn{j}")[:, :], w[:, 0:2], slice(j * P, j * P + P), chunks=2, src=m_ckv)\
                        .then_inc(PROJ.full, 1)
                for j in range(8):
                    ps = PROJ.claim(pe, f"1v{j}")
                    for c in range(2):
                        last = mm(ps[:, :], m_ckv[:, c, (j // 2) * P:(j // 2 + 1) * P],
                                  w[:, 2 + c, 512 * (j % 2):512 * (j % 2) + 512], c == 0, c == 1)
                    last.then_inc(PROJ.full, 1)
                pe.wait_ge(normed, NORMED + 2)
                for j in range(9):
                    if j < 8:
                        if j % 4 == 0:
                            w = W.arrived(pe, f"1uq{j // 4}")
                        ps = PROJ.claim(pe, f"1qf{j}")
                        for b in range(2):
                            at = (2 * j + b) % 8 * MLA_QK
                            last = gemm_T(ps[0:MLA_QK, b * S:b * S + S], w, slice(at, at + MLA_QK), S, 3, m_cq)
                        last.then_inc(PROJ.full, 1)
                    if j >= 1:
                        PROJ.taken(pe, f"1qf{j - 1}")
                        mm(PT.claim(pe, f"1rt{j - 1}")[0:MLA_QK, :], grid_swap[0:MLA_QK, 0:MLA_QK],
                           m_qT[0:MLA_QK, 2 * j - 2:2 * j, :].rearrange("p a b -> p (a b)"), True, True).then_inc(PT.full, 1)

            def operands(i, h):
                if i == 0:
                    rows, kv = slice(h % 2 * HD, h % 2 * HD + HD), h // (HEADS // KV_HEADS)
                    return g_qT[rows, h // 2, :], g_kT[rows, kv, :], g_v[:, :, kv * HD:kv * HD + HD]
                return m_qT[0:MLA_QK, h, :], m_kT[0:MLA_QK, h, :], m_v[:, :, h * HD:h * HD + HD]

            def attention(i):
                prob, turned_p = buffers(i)[0:2]
                U = UNITS[i]
                for h in range(HEADS + 2):
                    for u in range(U):
                        if h < HEADS:
                            q, k, _ = operands(i, h)
                            if u == 0:
                                pe.wait_ge(roped, (3 if i == 0 else NORMED + 1) + h // 2)
                            ps = SC.claim(pe, f"{i}s{h}_{u}")
                            if u < 2:
                                last = mm(ps[:, :], q[:, u * P:u * P + P], k, True, True)
                            else:
                                for t in range(TT):
                                    last = mm(ps[:, t * S:t * S + S], q[:, S + t * P:S + t * P + P], k[:, S:2 * S], True, True)
                            last.then_inc(SC.full, 1)
                        if 1 <= h <= HEADS:
                            n = unit(i, h - 1, u)
                            src = prob[:, ((h - 1) * U + u) % (2 * U)]
                            pe.wait_ge(prob_ready, n + 1)
                            ps = PT.claim(pe, f"{i}t{h - 1}_{u}")
                            for b in range(4):
                                at = b if u < 2 else b % 2 * 2 + b // 2
                                last = turn(ps[:, b * P:b * P + P], src[:, at * P:at * P + P])
                            last.then_inc(PT.full, 1)
                    if h >= 2:
                        v = operands(i, h - 2)[2]
                        half = slice((h - 2) % 2 * HD, (h - 2) % 2 * HD + HD)
                        PT.taken(pe, *[f"{i}t{h - 2}_{u}" for u in range(U)])
                        ps = OT.claim(pe, f"{i}o{h - 2}")
                        keys = turned_p[:, (h - 2) % 2]
                        for b in range(4):
                            last = mm(ps[half, 0:S], v[:, b, :], keys[:, b, :], b == 0, b == 3)
                        if U == 3:
                            for b in range(2):
                                last = mm(ps[half, S:2 * S], v[:, 2 + b, :], keys[:, 4 + b, :], b == 0, b == 1)
                        last.then_inc(OT.full, 1)

            for i in range(DEPTH):
                yT, n_tok = buffers(i)[2:]
                for t in XT_ORDER[i]:
                    x_arrived(pe, i, t)
                    turn_tile([f"{i}xT{t}{h}" for h in range(2)], t)
                PROJ.taken(pe, *[f"{i}xT{t}{h}" for t in XT_ORDER[i] for h in range(2)])
                if i == 0:
                    gqa_project()
                    pe.wait_ge(k_copied, 8)
                else:
                    mla_project()
                    pe.wait_ge(k_copied, 12)
                attention(i)

                OT.taken(pe, f"{i}o{HEADS - 2}", f"{i}o{HEADS - 1}")
                w = [W.arrived(pe, f"{i}wo{h}") for h in range(2)]
                for t in range(NT[i] + 1):
                    if t < NT[i]:
                        for h in range(2):
                            ps = OT.claim(pe, f"{i}wo{t}{h}")
                            for c in range(KD):
                                last = mm(ps[:, :], yT[:, c, t * P:t * P + P], w[h][:, c, :], c == 0, c == KD - 1)
                            last.then_inc(OT.full, 1)
                    if t >= 1:
                        pe.wait_ge(x_ready, ln_count[i, 0, t - 1])
                        turn_tile([f"{i}hT{t - 1}{h}" for h in range(2)], t - 1)

                pe.wait_ge(hT_cut, cut_base[i] + NT[i])
                per = UP_PER[i]
                src = [part[:, :, 0:n_tok] for part in (hT_high, hT_low)]
                for q in range(QUARTERS):
                    for n in range(KD // per):
                        ps = PROJ.claim(pe, f"{i}up{q}_{n}")
                        for b in range(per):
                            c = n * per + b
                            w = X.arrived(pe, f"{i}up{q}{c // 4}", c // 2 % 2)
                            cols = slice(c % 2 * P, c % 2 * P + P)
                            for k in range(KD):
                                last = product(nc, ps[:, b * n_tok:(b + 1) * n_tok], [part[:, k, cols] for part in w],
                                               [part[:, k, :] for part in src], k == 0, k == KD - 1)
                        last.then_inc(PROJ.full, 1)
                        for s in range(NT[i] // TT):
                            if q == 0 and n == GM_AT[s]:
                                turn_gate(i, "gm", s)
                    for h in range(2):
                        for b in range(2):
                            w = X.arrived(pe, f"{i}down{q}{h}", b)
                            pe.wait_ge(hidden_ready, up_base[i] + (q * KD + 4 * b + 3) // per + 1)
                            for t in range(NT[i]):
                                banks, name = down_banks(h, t), f"{i}down{q}{h}{t}"
                                ps = banks.claim(pe, name) if b == 0 else banks.bank(name)
                                for k in range(4):
                                    last = product(nc, ps[:, :], [part[:, 4 * b + k, t * P:t * P + P] for part in (hidden_high, hidden_low)],
                                                   [part[:, k, :] for part in w], b + k == 0, 4 * b + k == KD - 1)
                                if b == 1:
                                    last.then_inc(banks.full, 1)
                            if b == 0:
                                last.then_inc(down_used, 1)

        @block.scalar
        def _(act):
            f = nc.scalar.activation
            link = Chain(act, act_self)

            def copy(o, src, **kw):
                return f(o, src, ACT.Copy, **kw)

            def modulate(i, name, t, part, high=None):
                ps = PROJ.arrived(act, name)
                for k in range(4):
                    if high is not None:
                        f(high[:, k, t * P:t * P + P], ps[:, k * P:k * P + P], ACT.Identity,
                          scale=mod_col(i, part + 1, k, t // TT), bias=mod_col(i, part, k, t // TT))
                    last = f(hT[:, k, t * P:t * P + P], ps[:, k * P:k * P + P], ACT.Identity,
                             scale=mod_col(i, part + 1, k, t // TT), bias=mod_col(i, part, k, t // TT))
                last.then_inc(PROJ.free(name), 1)

            def take_gate(i, kind, s):
                for h, name in enumerate(gate_fills(i, kind, s)):
                    ps = PROJ.arrived(act, name)
                    copy(gate_rows[:, s, 512 * h:512 * h + 512], ps[:, :]).then_inc(PROJ.free(name), 1)

            def scale_of(banks, name, part, o, mean):
                ps = banks.arrived(act, name)
                f(o, ps[:, 0:o.shape[1]], ACT.Ln, scale=mean, bias=eps).then_inc(banks.free(name), 1)
                banks.taken(act, name)
                f(o, o, ACT.Exp, scale=-0.5).then_inc(rs_ready, 1)

            def gqa_project():
                for j in range(2):
                    ps = PROJ.arrived(act, f"0v{j}")
                    copy(g_v[:, 2 * j:2 * j + 2, :].rearrange("p a b -> p (a b)"), ps[:, :]).then_inc(PROJ.free(f"0v{j}"), 1)
                    take_gate(0, "ga", j)
                for n in range(NORMED + 1):
                    if n < NORMED:
                        ps = PROJ.arrived(act, f"0a{n}")
                        copy(g_k[:, n] if n < 2 else g_qT[:, n - 2], ps[:, :])
                        f(g_sq[:, n % 2], ps[:, :], ACT.Square).then_inc(PROJ.free(f"0a{n}"), 1)
                    if n >= 1:
                        if n >= 3:
                            act.wait_ge(normed, n - 2)
                        scale_of(SC, f"0ms{n - 1}", None, g_rs[:, (n - 1) % 2], 1.0)

            def mla_project():
                for j in range(2):
                    ps = PROJ.arrived(act, f"1ckv{j}")
                    copy(m_ckv[:, j, :], ps[:, :])
                    f(m_sqkv[:, j, :], ps[:, :], ACT.Square).then_inc(PROJ.free(f"1ckv{j}"), 1)
                    if j == 0:
                        take_gate(1, "ga", 0)
                ps = PROJ.arrived(act, "1kpe")
                copy(m_kpe[HD:MLA_QK, :], ps[HD:MLA_QK, :]).then_inc(PROJ.free("1kpe"), 1)
                for j in range(2):
                    ps = PROJ.arrived(act, f"1cq{j}")
                    n = (2 - j) * S
                    copy(m_cq[:, 2 * j:2 * j + 2 - j, :].rearrange("p a b -> p (a b)"), ps[:, 0:n])
                    f(m_sqq[:, 2 * j:2 * j + 2 - j, :].rearrange("p a b -> p (a b)"), ps[:, 0:n], ACT.Square)\
                        .then_inc(PROJ.free(f"1cq{j}"), 1)
                scale_of(SC, "1mskv", None, m_rskv, 1.0 / KV_RANK)
                scale_of(SC, "1msq", None, m_rsq, 1.0 / Q_RANK)
                for j in range(0, 8, 2):
                    ps = PROJ.arrived(act, f"1kn{j}")
                    copy(m_kT[0:HD, 2 * j, :], ps[0:HD, :])
                    copy(m_kT[0:HD, 2 * j + 1, :], ps[HD:P, :]).then_inc(PROJ.free(f"1kn{j}"), 1)
                for j in range(0, 8, 2):
                    ps = PROJ.arrived(act, f"1v{j}")
                    copy(m_v[:, j // 2, 0:512], ps[:, :]).then_inc(PROJ.free(f"1v{j}"), 1)
                for j in range(8):
                    ps = PROJ.arrived(act, f"1qf{j}")
                    copy(m_qT[0:MLA_QK, 2 * j:2 * j + 2, :].rearrange("p a b -> p (a b)"), ps[0:MLA_QK, :],
                         scale=MLA_QK ** -0.5).then_inc(PROJ.free(f"1qf{j}"), 1)

            def attention(i):
                prob, turned_p, yT = buffers(i)[0:3]
                U = UNITS[i]
                for h in range(HEADS + 2):
                    for u in range(U):
                        if h < HEADS:
                            n = unit(i, h, u)
                            slot = (h * U + u) % (2 * U)
                            act.wait_ge(max_ready, n + 1)
                            ps = SC.arrived(act, f"{i}s{h}_{u}")
                            for t in range(1 if u < 2 else TT):
                                part = slice(0, 512) if u < 2 else slice(t * S, t * S + S)
                                last = f(prob[:, slot, part], ps[:, part], ACT.Exp, bias=neg_max[:, slot, t:t + 1],
                                         accum_out=total[:, slot, t:t + 1])
                            last.then_inc(SC.free(f"{i}s{h}_{u}"), 1)
                        if 1 <= h <= HEADS:
                            name = f"{i}t{h - 1}_{u}"
                            ps = PT.arrived(act, name)
                            keys = turned_p[:, (h - 1) % 2]
                            if u < 2:
                                o, src = keys[:, 0:4, u * P:u * P + P], ps[:, :].rearrange("p (b t) -> p b t", b=4)
                            else:
                                o, src = keys[:, 4:6, :].rearrange("p a b -> p (a b)"), ps[:, :]
                            copy(o, src).then_inc(PT.free(name), 1)
                    if h >= 2:
                        half = slice((h - 2) % 2 * HD, (h - 2) % 2 * HD + HD)
                        ps = OT.arrived(act, f"{i}o{h - 2}")
                        n = yT.shape[2]
                        copy(yT[half, (h - 2) // 2, :], ps[half, 0:n]).then_inc(OT.free(f"{i}o{h - 2}"), 1)

            def ln_rstd(i, j, t):
                act.wait_ge(var_ready, ln_count[i, j, t])
                link(f(ln_rs[:, t:t + 1], ln_mv[:, t, 1:2], ACT.Ln, bias=eps))
                f(ln_rs[:, t:t + 1], ln_rs[:, t:t + 1], ACT.Exp, scale=-0.5).then_inc(ln_scale, 1)

            act.dma_start(nf_row, dram["norm_final"].partition_broadcast(P)).then_inc(first_in, 16)
            act.dma_start(xc, dram["ctx_2"].rearrange("b (t p) d -> p (b t) d", p=P)).then_inc(first_in, 16)
            act.dma_start(grid, dram["grid_gqa"]).then_inc(first_in, 16)
            for n, name in enumerate(("ln_g_2", "ln_b_2")):
                act.dma_start(ln_rows[:, n, :], dram[name][0, 0].partition_broadcast(P)).then_inc(first_in, 16)
            for t in range(TT):
                link(f(nf_junk, x[:, t, :], ACT.Square, accum_out=nf_stat[:, t:t + 1]))
            link(f(nf_stat, nf_stat, ACT.Ln, scale=1.0 / D, bias=eps))
            f(nf_stat, nf_stat, ACT.Exp, scale=-0.5).then_inc(nf_scale, 1)
            act.wait_ge(mod_ready, 1)
            for i in range(DEPTH):
                n_tok = buffers(i)[3]
                for t in XT_ORDER[i]:
                    modulate(i, f"{i}xT{t}0", t, 0)
                (gqa_project, mla_project)[i]()
                attention(i)
                own = halves_of(i)

                def make(n):
                    if n < len(own):
                        X.make_high(nc, act, *own[n][0:2])

                for n in range(3):
                    make(n)
                for t in range(NT[i] + 1):
                    if t < NT[i]:
                        ln_rstd(i, 0, t)
                    if t >= 1:
                        modulate(i, f"{i}hT{t - 1}0", t - 1, 3, hT_high)
                per = UP_PER[i]
                for q in range(QUARTERS):
                    for n in range(KD // per):
                        name = f"{i}up{q}_{n}"
                        ps = PROJ.arrived(act, name)
                        part = hidden[:, n * per:(n + 1) * per, 0:n_tok]
                        f(part, ps[:, :].rearrange("p (a b) -> p a b", a=per), ACT.Relu).then_inc(PROJ.free(name), 1)
                        PROJ.taken(act, name)
                        link(f(hidden_high[:, n * per:(n + 1) * per, 0:n_tok], part, ACT.Square))
                        f(part, part, ACT.Square).then_inc(hidden_squared, 1)
                        for s in range(NT[i] // TT):
                            if q == 0 and n == GM_AT[s]:
                                take_gate(i, "gm", s)
                        if (n + 1) * per % 2 == 0:
                            make(8 * q + (n + 1) * per // 2 + 2)
                    for n in range(4):
                        make(8 * q + 4 + n + 3)
                for t in range(NT[i]):
                    ln_rstd(i, 1, t)

        @block.vector
        def _(dve):
            link = Chain(dve, dve_self)
            vec = nc.vector

            def widen(i, kind, s):
                part = {"ga": 2, "gm": 5}[kind]
                at = (i * MOD_PARTS + part) * KD * 2
                src = mod[:, at:at + 2 * KD].rearrange("p (k s) -> p k s", s=2)[:, :, s:s + 1]
                if gate_count[i, kind, s] > 1:
                    i0, kind0, s0 = gate_order[gate_count[i, kind, s] - 2]
                    PROJ.taken(dve, *gate_fills(i0, kind0, s0))
                vec.tensor_copy(gate_src, src.to_broadcast([P, KD, P])).then_inc(gate_wide, 1)
                dve.wait_ge(gate_wide, gate_count[i, kind, s])

            def modulate(i, name, t, part, high=None):
                ps = PROJ.arrived(dve, name)
                for k in range(4):
                    if high is not None:
                        vec.tensor_scalar(high[:, 4 + k, t * P:t * P + P], ps[:, k * P:k * P + P],
                                          mod_col(i, part + 1, 4 + k, t // TT), mod_col(i, part, 4 + k, t // TT),
                                          ALU.mult, ALU.add)
                    last = vec.tensor_scalar(hT[:, 4 + k, t * P:t * P + P], ps[:, k * P:k * P + P],
                                             mod_col(i, part + 1, 4 + k, t // TT), mod_col(i, part, 4 + k, t // TT),
                                             ALU.mult, ALU.add)
                last.then_inc(PROJ.free(name), 1)

            def residual(t, h, banks, name, keep=ALPHA):
                ps = banks.arrived(dve, name)
                half = slice(512 * h, 512 * h + 512)
                vec.tensor_tensor(z[:, h, :], ps[:, :], gate_rows[:, t // TT, half], ALU.mult).then_inc(banks.free(name), 1)
                banks.taken(dve, name)
                link(vec.scalar_tensor_tensor(tok[t][:, half], tok[t][:, half], keep, z[:, h, :], ALU.mult, ALU.add))

            def layer_norm(i, j, t):
                n, xt = ln_count[i, j, t], tok[t]
                for h in range(2):
                    link(vec.bn_stats(ln_stats[:, t, h, :], xt[:, 512 * h:512 * h + 512]))
                vec.bn_aggr(ln_mv[:, t, :], ln_stats[:, t]).then_inc(var_ready, 1)
                dve.wait_ge(var_ready, n)
                if i + j > 0:
                    dve.wait_ge(ln_in, 32 * (2 * i + j))
                link(vec.scalar_tensor_tensor(xt, xt, ln_mv[:, t, 0:1], ln_rows[:, 0, :], ALU.subtract, ALU.mult))
                dve.wait_ge(ln_scale, n)
                vec.scalar_tensor_tensor(xt, xt, ln_rs[:, t:t + 1], ln_rows[:, 1, :], ALU.mult, ALU.add).then_inc(x_ready, 1)

            def rotate(part, name, rows, sin_of, cos_of, tmp, rt):
                ps = PT.arrived(dve, name)
                vec.tensor_tensor(tmp, rt(ps), sin_of, ALU.mult).then_inc(PT.free(name), 1)
                link(vec.tensor_tensor(part, part, cos_of, ALU.mult))
                PT.taken(dve, name)
                return vec.tensor_tensor(part, part, tmp, ALU.add)

            def gqa_project():
                for n in range(NORMED + 1):
                    if n < NORMED:
                        raw = g_k[:, n] if n < 2 else g_qT[:, n - 2]
                        gain = cols2[:, ROW_KN:ROW_KN + 1] if n < 2 else cols2[:, ROW_QN:ROW_QN + 1]
                        dve.wait_ge(rs_ready, n + 1)
                        vec.scalar_tensor_tensor(raw, raw, gain, g_rs[:, n % 2], ALU.mult, ALU.mult).then_inc(normed, 1)
                    if n >= 1:
                        raw = g_k[:, n - 1] if n < 3 else g_qT[:, n - 3]
                        dve.wait_ge(normed, n)
                        if n >= 2:
                            dve.wait_ge(roped, n - 1)
                        rotate(raw[:, 0:S], f"0rt{n - 1}", None, grid_sin, grid_cos, g_rot, lambda ps: ps[:, 0:S])\
                            .then_inc(roped, 1)

            def mla_project():
                vec.memset(m_kpe[0:HD, :], 0.0).then_inc(kpe_zero, 1)
                pe_rows = slice(HD, MLA_QK)
                dve.wait_ge(rs_ready, NORMED + 1)
                for c in range(2):
                    last = vec.scalar_tensor_tensor(m_ckv[:, c, :], m_ckv[:, c, :], cols2[:, ROW_MKN + c:ROW_MKN + c + 1],
                                                    m_rskv, ALU.mult, ALU.mult)
                last.then_inc(normed, 1)
                dve.wait_ge(rs_ready, NORMED + 2)
                for c in range(3):
                    last = vec.scalar_tensor_tensor(m_cq[:, c, :], m_cq[:, c, :], cols2[:, ROW_MQN + c:ROW_MQN + c + 1],
                                                    m_rsq, ALU.mult, ALU.mult)
                last.then_inc(normed, 1)
                dve.wait_ge(grid_in, 16)
                rotate(m_kpe[pe_rows, 0:S], "1rtk", None, grid_sin[pe_rows, :], grid_cos[pe_rows, :], m_rot[pe_rows, 0:S],
                       lambda ps: ps[pe_rows, 0:S]).then_inc(kpe_ready, 1)
                dve.wait_ge(kpe_ready, 1)
                for j in range(1, 8, 2):
                    ps = PROJ.arrived(dve, f"1kn{j}")
                    vec.tensor_copy(m_kT[0:HD, 2 * j, :], ps[0:HD, :])
                    vec.tensor_copy(m_kT[0:HD, 2 * j + 1, :], ps[HD:P, :]).then_inc(PROJ.free(f"1kn{j}"), 1)
                for j in range(1, 8, 2):
                    ps = PROJ.arrived(dve, f"1v{j}")
                    vec.tensor_copy(m_v[:, j // 2, 512:1024], ps[:, :]).then_inc(PROJ.free(f"1v{j}"), 1)
                wide = lambda a: a[pe_rows, :].unsqueeze(1).to_broadcast([PE_DIM, 2, S])
                for j in range(8):
                    if j >= 1:
                        dve.wait_ge(roped, NORMED + j)
                    rotate(m_qT[pe_rows, 2 * j:2 * j + 2, :], f"1rt{j}", None, wide(grid_sin), wide(grid_cos),
                           m_rot[pe_rows, :].rearrange("p (a b) -> p a b", a=2),
                           lambda ps: ps[pe_rows, :].rearrange("p (a b) -> p a b", a=2)).then_inc(roped, 1)

            def attention(i):
                prob, U = buffers(i)[0], UNITS[i]
                order = [(h, u) for h in range(HEADS) for u in range(U)]
                for n in range(len(order) + 1):
                    if n < len(order):
                        h, u = order[n]
                        slot = n % (2 * U)
                        ps = SC.arrived(dve, f"{i}s{h}_{u}")
                        if u < 2:
                            last = vec.tensor_reduce(neg_max[:, slot, 0:1], ps[:, :], axis=AX.X, op=ALU.max, negate=True)
                        else:
                            last = vec.tensor_reduce(neg_max[:, slot, :], ps[:, :].rearrange("p (t k) -> p t k", t=TT),
                                                     axis=AX.X, op=ALU.max, negate=True)
                        last.then_inc(max_ready, 1)
                    if n >= 1:
                        h, u = order[n - 1]
                        slot = (n - 1) % (2 * U)
                        tiles_of = 1 if u < 2 else TT
                        SC.taken(dve, f"{i}s{h}_{u}")
                        link(vec.reciprocal(total[:, slot, 0:tiles_of], total[:, slot, 0:tiles_of]))
                        for t in range(tiles_of):
                            part = slice(0, 512) if u < 2 else slice(t * S, t * S + S)
                            last = vec.tensor_scalar(prob[:, slot, part], prob[:, slot, part], total[:, slot, t:t + 1],
                                                     None, ALU.mult)
                        last.then_inc(prob_ready, 1)

            every = mod[:, :].rearrange("p (n s) -> p n s", s=2)
            link(vec.tensor_tensor(every, every, cols2[:, ROW_ADA:ROW_ADA + DEPTH * MODC].unsqueeze(2)
                                   .to_broadcast([P, DEPTH * MODC, 2]), ALU.add))
            scales = mod[:, :].rearrange("p (l m n) -> p l m n", l=2 * DEPTH, m=3)[:, :, 1, :]
            vec.tensor_scalar_add(scales, scales, 1.0).then_inc(mod_ready, 1)
            dve.wait_ge(mod_ready, 1)
            link(vec.tensor_scalar(cols2[:, ROW_QN:ROW_QN + 1], cols2[:, ROW_QN:ROW_QN + 1], HD ** -0.5, None, ALU.mult))
            widen(0, "ga", 0)
            dve.wait_ge(first_in, 5 * 16)
            dve.wait_ge(nf_scale, 1)
            for t in range(TT):
                vec.scalar_tensor_tensor(x[:, t, :], x[:, t, :], nf_stat[:, t:t + 1], nf_row, ALU.mult, ALU.mult)\
                    .then_inc(x_first, 1)
            for i in range(DEPTH):
                n_tok = buffers(i)[3]
                if i == 1:
                    widen(1, "ga", 0)
                for t in XT_ORDER[i]:
                    modulate(i, f"{i}xT{t}1", t, 0)
                if i == 0:
                    widen(0, "ga", 1)
                (gqa_project, mla_project)[i]()
                attention(i)
                own = halves_of(i)

                def make(n):
                    if n < len(own):
                        X.make_low(nc, dve, *own[n][0:2])

                for n in range(3):
                    make(n)
                PROJ.taken(dve, *gate_fills(i, "ga", NT[i] // TT - 1))
                for t in range(NT[i] + 1):
                    if t < NT[i]:
                        for h in range(2):
                            residual(t, h, OT, f"{i}wo{t}{h}")
                        layer_norm(i, 0, t)
                    if t >= 1:
                        modulate(i, f"{i}hT{t - 1}1", t - 1, 3, hT_high)
                        PROJ.taken(dve, f"{i}hT{t - 1}0", f"{i}hT{t - 1}1")
                        part = slice((t - 1) * P, t * P)
                        vec.tensor_tensor(hT_low[:, :, part], hT[:, :, part], hT_high[:, :, part].bitcast(F32), ALU.subtract)\
                            .then_inc(hT_cut, 1)
                widen(i, "gm", 0)
                per = UP_PER[i]
                for q in range(QUARTERS):
                    for n in range(KD // per):
                        dve.wait_ge(hidden_squared, up_base[i] + (q * KD) // per + n + 1)
                        part = slice(n * per, (n + 1) * per)
                        vec.tensor_tensor(hidden_low[:, part, 0:n_tok], hidden[:, part, 0:n_tok],
                                          hidden_high[:, part, 0:n_tok].bitcast(F32), ALU.subtract).then_inc(hidden_ready, 1)
                        if q == 0 and n == GM_AT[0] and NT[i] > TT:
                            widen(i, "gm", 1)
                        if (n + 1) * per % 2 == 0:
                            make(8 * q + (n + 1) * per // 2 + 2)
                    if q == 0:
                        PROJ.taken(dve, *gate_fills(i, "gm", NT[i] // TT - 1))
                    for h in range(2):
                        make(8 * q + 4 + 2 * h + 3)
                        for t in range(NT[i]):
                            residual(t, h, down_banks(h, t), f"{i}down{q}{h}{t}", ALPHA if q == 0 else 1.0)
                            if q == QUARTERS - 1 and h == 1:
                                layer_norm(i, 1, t)
                        make(8 * q + 5 + 2 * h + 3)

        @block.gpsimd
        def _(pool):
            for n in range(2):
                pool.wait_ge(roped, n + 1)
                for a in range(2):
                    for half in range(2):
                        nc.gpsimd.tensor_copy(g_kT[half * HD:half * HD + HD, 2 * n + a, :], g_k[a * HD:a * HD + HD, n, :])\
                            .then_inc(k_copied, 1)
            pool.wait_ge(roped, NORMED)
            pool.dma_start(grid, dram["grid_mla"]).then_inc(grid_in, 16)

            def norm_rows(i, j, after):
                pool.wait_ge(x_ready, after)
                for n, name in enumerate(("ln_g_2", "ln_b_2")):
                    pool.dma_start(ln_rows[:, n, :], dram[name][i, j].partition_broadcast(P)).then_inc(ln_in, 16)

            norm_rows(0, 1, ln_count[0, 0, NT[0] - 1])
            norm_rows(1, 0, ln_count[0, 1, NT[0] - 1])
            pool.wait_ge(kpe_ready, 1)
            for n in range(4):
                nc.gpsimd.tensor_copy(m_kT[HD:MLA_QK, 4 * n:4 * n + 4, :],
                                      m_kpe[HD:MLA_QK, :].unsqueeze(1).to_broadcast([PE_DIM, 4, 2 * S])).then_inc(k_copied, 1)
            norm_rows(1, 1, ln_count[1, 0, NT[1] - 1])


def build(nc, T, dram, out):
    with ExitStack() as ctx:
        def sb(name, shape, dt=F32):
            return ctx.enter_context(nc.sbuf_tensor(name, shape, dt))

        names = []

        def sem(name):
            names.append(name)
            return ctx.enter_context(nc.semaphore(f"{name}_{len(names)}"))

        n_f32 = dram["f32_tables"].shape[1]
        n_bf16 = dram["bf16_tables"].shape[1]
        chip = {"consts": sb("consts", [P, n_f32]), "masks": sb("masks", [P, n_bf16], BF16),
                }
        at = nc.sbuf_base
        chip["ring"] = sb("ring", [P, N_SLOTS, SLOT])
        chip["ring_low"] = [nc.alloc_sbuf_tensor_at(f"ring_low{n}", [P, SLOT], F32R, offset=at + 4 * n * SLOT)
                            for n in range(N_SLOTS)]
        x = sb("x_sb", [P, TT, D])
        cos, sin = sb("cos", [P, S]), sb("sin", [P, S])
        chip.update(x=x[:, :, :], cos=cos[:, :], sin=sin[:, :])
        chip["mod"] = sb("mod", [P, DEPTH * 2 * MODC])
        chip["cols2"] = sb("cols2", [P, N_ROWS2])[:, :]
        chip["silu_c"] = sb("silu_c", [P, KD, THIN])[:, :, :]
        work_base = nc.sbuf_base
        chip["work"] = sb("work", [P, WORK])

        def rounded(name, at, *dims):
            n = int(np.prod(dims))
            assert at + n <= WORK, (name, at, n)
            return nc.alloc_sbuf_tensor_at(name, [P, *dims], F32R, offset=work_base + 4 * at)

        chip["rounded"] = rounded
        chip["psum"] = [ctx.enter_context(nc.psum_tensor(f"bank{i}", [P, 512], F32)) for i in range(8)]

        prologue(nc, T, dram, sem, chip)
        layer_sems = []

        def layer_sem(name):
            layer_sems.append(sem(name))
            return layer_sems[-1]

        with nc.Fori(0, DEPTH) as l:
            first_layer(nc, l, T, dram, layer_sem, chip)
            for s in layer_sems:
                nc.gpsimd.sem_clear(s)
            nc.all_engine_barrier()

        second_block(nc, T, dram, out, sem, chip)


_INS = ["x", "positions", "norm_mix", "w_in", "b_gate", "nsa_cmp_pos_k", "nsa_cmp_pos_v", "nsa_cmp_wk1",
        "nsa_cmp_wk2", "nsa_cmp_wv1", "nsa_cmp_wv2", "gla_w_alpha", "gla_b_alpha", "gla_norm", "fox_b_f",
        "w_branch", "w_out", "norm_ff", "w_ff1", "w_ff2", "norm_final",
        "c_2", "ctx_2", "c_ctx_2", "w_ada_2", "b_ada_2", "ln_g_2", "ln_b_2", "mlp_w1_2", "mlp_w2_2",
        "gqa_w_qkv_2", "gqa_q_norm_2", "gqa_k_norm_2", "gqa_w_o_2", "mla_w_in_2", "mla_q_norm_2",
        "mla_kv_norm_2", "mla_w_uq_2", "mla_w_ukv_2", "mla_w_o_2"]


def kernel(**inputs):
    import concourse.bacc as _bacc
    import ml_dtypes
    from concourse.bass_utils import run_bass_kernel_spmd as _run

    nc = _bacc.Bacc("TRN2", target_bir_lowering=False, num_devices=1)
    f32, bf16 = constants()
    T, arrays, dram = {}, {}, {}
    T["f32"], arrays["f32_tables"] = packed(f32, np.float32)
    T["bf16"], arrays["bf16_tables"] = packed(bf16, ml_dtypes.bfloat16)
    arrays["grid_gqa"] = grid_tables(HD, 0, HD)
    arrays["grid_mla"] = grid_tables(PE_DIM, HD, HD)
    for name in _INS:
        arrays[name] = np.ascontiguousarray(inputs[name])
    for name, a in arrays.items():
        dram[name] = nc.dram_tensor(name, a.shape, mybir.dt.from_np(a.dtype), kind="ExternalInput").ap()
    out = nc.dram_tensor("out", (1, S, D), F32, kind="ExternalOutput").ap()
    build(nc, T, dram, out)
    r = _run(nc, [arrays], core_ids=[0])
    return r.results[0]["out"]
```

```python
from contextlib import ExitStack

import numpy as np

import concourse.bass as bass
from concourse import mybir

F32, BF16, I32, U16 = mybir.dt.float32, mybir.dt.bfloat16, mybir.dt.int32, mybir.dt.uint16
F32R = mybir.dt.float32r
ACT = mybir.ActivationFunctionType
ALU = mybir.AluOpType
AX = mybir.AxisListType

P = 128
D, S, DEPTH = 1024, 256, 2
KD = D // P
TT = S // P
HD = 64
HALF_HEADS = 4
N_CMP, CMP_LEN, CMP_STRIDE, CMP_HID = 15, 32, 16, 256
N_GATE = 24
GLA_H, GLA_DV, GLA_RANK, GLA_TAU = 4, 128, 16, 16.0
FFK = 4 * D // P
THIN = 32
EPS = 1e-6
NEG = -1e30
GELU_C = 0.7978845608028654
ROT_HALF, ROPE_THETA = 8, 500000.0
GRID_W, GRID_THETA = 64, 10000.0
HEADS, KV_HEADS = 16, 4
Q_RANK, KV_RANK, PE_DIM = 384, 256, 32
MLA_QK = HD + PE_DIM
ALPHA = (2.0 * DEPTH) ** 0.25
MOD_PARTS = 6
MODC = MOD_PARTS * KD

ROW_ADA, ROW_QN, ROW_KN, ROW_MQN, ROW_MKN, ROW_C, N_ROWS2 = 0, 96, 97, 98, 101, 103, 119

Q0, KC0, KS0 = 0, 512, 768
SBQ0, SBK0, SBV0 = 1304, 1816, 2328
GLQ0, GLV0, GLA0, GLG0 = 2840, 3352, 3864, 3880
FXQ0, FXK0, FXV0, GATE0 = 4392, 4904, 5416, 5936

ROW_MIX, ROW_FF, ROW_GATE, ROW_GLB, ROW_GLN, ROW_PEK, ROW_PEV, N_ROWS = 0, 8, 16, 48, 50, 51, 67, 83

LEVELS = [128, 0, 64, 32, 16, 8, 4, 2, 1]
SLOT = 528 * KD
N_SLOTS = 4
SPLIT_HALF = 2 * D
WORK = 30336
MAGIC = 1.5 * 2.0 ** 23
TWO_PI_PARTS = (6.28125, 0.0019340515136718750, 1.2556659146019e-06)


def constants():
    i = np.arange(P)
    row, col = i[:, None], i[None, :]
    rot = np.zeros((P, P), np.float32)
    for half in (0, HD):
        for d in range(ROT_HALF):
            rot[half + ROT_HALF + d, half + d] = -1.0
            rot[half + d, half + ROT_HALF + d] = 1.0
    levels = [(row == col)]
    for h in LEVELS[2:]:
        s, t = row, col
        levels.append((s // (2 * h) == t // (2 * h)) & (s % (2 * h) < h) & (t % (2 * h) >= h))
    inv = (ROPE_THETA ** (-np.arange(0, 2 * ROT_HALF, 2) / (2 * ROT_HALF))).astype(np.float32)
    inv_col = np.zeros((P, 1), np.float32)
    for half in (0, HD):
        for d in range(2 * ROT_HALF):
            inv_col[half + d, 0] = inv[d % ROT_HALF]
    end = np.arange(N_CMP) * CMP_STRIDE + CMP_LEN - 1
    seen = np.stack([end[None, :] <= (tt * P + i)[:, None] for tt in range(TT)], 1).reshape(P, -1)
    f32 = {
        "ident": np.eye(P),
        "neg_from": -1.0 * (row >= col),
        "neg_upto": -1.0 * (row <= col),
        "neg_ones": -np.ones((P, P)),
        "rot": rot,
        "inv_freq": inv_col,
        "one": np.ones((P, 1)), "eps": np.full((P, 1), EPS),
        "cmp_seen": seen, "cmp_bias": np.where(seen, 0.0, NEG),
        "head_sel": np.repeat(np.eye(P)[:, :8], P, axis=1),
        "ones": np.ones((P, S)),
        "sum4": np.tile(np.eye(THIN), (4, 1)),
        "head_mean": np.kron(np.eye(2), np.ones((HD, HD))) / HD,
    }
    bf16 = {
        "ident": np.eye(P),
        "causal": np.where(col > row, NEG, 0.0),
        "strict": np.where(row >= col, NEG, 0.0),
        "levels": np.stack(levels, 1).reshape(P, -1),
    }
    return f32, bf16


def grid_tables(rot_dim, start, period):
    axis, half = rot_dim // 2, rot_dim // 4
    swap, angle = np.zeros((P, P), np.float32), np.zeros((P, S), np.float32)
    inv = (GRID_THETA ** (-np.arange(0, axis, 2, dtype=np.float32) / np.float32(axis))).astype(np.float32)
    tok = np.arange(S)
    for base in range(start, P, period):
        for a, place in enumerate((tok // GRID_W, tok % GRID_W)):
            for j in range(half):
                lo = base + a * axis + j
                hi = lo + half
                swap[hi, lo], swap[lo, hi] = -1.0, 1.0
                angle[lo] = angle[hi] = place.astype(np.float32) * inv[j]
    return np.concatenate([swap, np.cos(angle), np.sin(angle)], 1).astype(np.float32)


def packed(tables, dtype):
    at, parts, n = {}, [], 0
    for name, a in tables.items():
        at[name] = (n, a.shape[1])
        parts.append(np.asarray(a, np.float32))
        n += a.shape[1]
    return at, np.concatenate(parts, 1).astype(dtype)


class Banks:

    def __init__(self, sem, label, banks, uses):
        assert len(set(uses)) == len(uses), label
        self.order = {name: i for i, name in enumerate(uses)}
        self.banks, self.filled, self.n = banks, 0, len(banks)
        self.full = sem(label + "_full")
        self.free_sems = [sem(f"{label}_free{b}") for b in range(self.n)]

    def bank(self, name):
        return self.banks[self.order[name] % self.n]

    def claim(self, pe, name):
        i = self.order[name]
        assert i == self.filled, (name, i, self.filled)
        self.filled += 1
        if i >= self.n:
            pe.wait_ge(self.free_sems[i % self.n], i // self.n)
        return self.bank(name)

    def arrived(self, eng, name):
        eng.wait_ge(self.full, self.order[name] + 1)
        return self.bank(name)

    def taken(self, eng, *names):
        for name in names:
            i = self.order[name]
            eng.wait_ge(self.free_sems[i % self.n], i // self.n + 1)

    def free(self, name):
        return self.free_sems[self.order[name] % self.n]


class Weights:

    def __init__(self, sem, label, ring, slots, tiles, before={}):
        self.tiles, self.ring, self.slots, self.before = tiles, ring, slots, before
        self.order = {tile[0]: i for i, tile in enumerate(tiles)}
        self.loaded = [sem(f"{label}_loaded{s}") for s in range(N_SLOTS)]
        count, self.ready, held, self.last = [0] * N_SLOTS, [], {}, []
        for i, (_, _, _, sources, _) in enumerate(tiles):
            count[slots[i]] += 16 * len(sources)
            self.ready.append(count[slots[i]])
            self.last.append(held.get(slots[i]))
            held[slots[i]] = i

    def slot(self, i):
        _, k, n, _, _ = self.tiles[i]
        return self.ring[:, self.slots[i], 0:k * n].rearrange("p (k n) -> p k n", k=k)

    def load(self, sp, first=0, stop=None):
        for i, (name, _, _, sources, _) in list(enumerate(self.tiles))[first:stop]:
            if self.last[i] is not None:
                sp.wait_ge(*self.tiles[self.last[i]][4])
            if name in self.before:
                sp.wait_ge(*self.before[name])
            for part, src in sources:
                sp.dma_start(self.slot(i)[part], src).then_inc(self.loaded[self.slots[i]], 16)

    def arrived(self, pe, name):
        i = self.order[name]
        pe.wait_ge(self.loaded[self.slots[i]], self.ready[i])
        return self.slot(i)


class Split:

    def __init__(self, sem, label, weights, ring_low, buffers, parts, freed):
        self.weights, self.ring_low, self.buffers, self.freed, self.parts = weights, ring_low, buffers, freed, parts
        self.order = {part[0:2]: i for i, part in enumerate(parts)}
        self.high_made, self.cut = sem(label + "_high_made"), sem(label + "_cut")

    def part(self, i, low):
        name, _, axis, start, size = self.parts[i]
        at = self.weights.order[name]
        _, k, n, _, _ = self.weights.tiles[at]
        slot = self.weights.slots[at]
        slot = self.ring_low[slot][:, 0:k * n] if low else self.weights.ring[:, slot, 0:k * n]
        tile = slot.rearrange("p (k n) -> p k n", k=k)
        return tile[:, start:start + size, :] if axis == "k" else tile[:, :, start:start + size]

    def high(self, i):
        _, k, n = self.part(i, True).shape
        return self.buffers[i % len(self.buffers)][:, 0:k * n].rearrange("p (k n) -> p k n", k=k)

    def make_high(self, nc, act, *which):
        for i in which:
            if i < len(self.parts):
                self.weights.arrived(act, self.parts[i][0])
                if i >= len(self.buffers):
                    act.wait_ge(*self.freed[i - len(self.buffers)])
                nc.scalar.activation(self.high(i), self.part(i, False), ACT.Copy).then_inc(self.high_made, 1)

    def make_low(self, nc, dve, *which):
        for i in which:
            if i < len(self.parts):
                dve.wait_ge(self.high_made, i + 1)
                nc.vector.tensor_tensor(self.part(i, True), self.part(i, False), self.high(i).bitcast(F32), ALU.subtract)\
                    .then_inc(self.cut, 1)

    def arrived(self, pe, name, which):
        i = self.order[name, which]
        pe.wait_ge(self.cut, i + 1)
        return self.high(i), self.part(i, True)


def product(nc, out, a, b, start, stop):
    nc.tensor.matmul(out, a[0], b[1], start=start, stop=False)
    nc.tensor.matmul(out, a[1], b[0], start=False, stop=False)
    return nc.tensor.matmul(out, a[0], b[0], start=False, stop=stop)


class Chain:

    def __init__(self, eng, sem):
        self.eng, self.sem, self.n = eng, sem, 0

    def __call__(self, ins):
        self.n += 1
        ins.then_inc(self.sem, 1)
        self.eng.wait_ge(self.sem, self.n)


class Carver:

    def __init__(self, whole, at=0):
        self.whole, self.at = whole, at

    def take(self, *dims):
        n = int(np.prod(dims))
        part = self.whole[:, self.at:self.at + n]
        self.at += -(-n // 8) * 8
        assert self.at <= self.whole.shape[1], ("SBUF work space", self.at)
        if len(dims) == 1:
            return part
        names = "abcde"[:len(dims)]
        spec = f"p ({' '.join(names)}) -> p {' '.join(names)}"
        return part.rearrange(spec, **{c: d for c, d in zip(names, dims)})


def first_layer(nc, l, T, dram, out, sem, chip):
    x, consts, masks = chip["x"], chip["consts"], chip["masks"]
    cos, sin, silu_c = chip["cos"], chip["sin"], chip["silu_c"]
    work = Carver(chip["work"])

    cols = work.take(N_ROWS)
    w_alpha, fox_b = work.take(GLA_H * HD), work.take(8)
    hT = work.take(KD, S)
    after_hT = work.at
    nsaT = work.take(6, S)
    hid_c = work.take(2, 2, 2 * N_CMP)
    gelu_t, gelu_e = work.take(2, 2 * N_CMP), work.take(2, 2 * N_CMP)
    kcT, kc_sin = work.take(N_CMP), work.take(N_CMP)
    vc = work.take(2, HD)
    vs, vw = work.take(TT, P), work.take(TT, P)
    g_nsa = work.take(TT, N_GATE)
    p_cmp = work.take(2, 4, TT, N_CMP)
    stat_cmp = work.take(2, 4, TT)
    qk_at = work.at
    sb_qk = work.take(KD, S)
    sbq, sbk = sb_qk[:, 0:4, :], sb_qk[:, 4:8, :]
    sbv = work.take(TT, 512)
    gle = work.take(TT, 512)
    gla_b = work.take(2, S)
    att = work.take(2, 3, 2, P)
    fxq, fxk = work.take(4, S), work.take(4, S)
    fxv = work.take(TT, 512)
    log_f, fox_t = work.take(TT, 8), work.take(TT, 8)
    fox_row = work.take(S)
    gates = work.take(4 * KD, S)
    yT = work.take(4 * 4, S)
    prob, probT = work.take(2, 3 * P), work.take(2, 3 * P)
    sb_at = work.at
    sb_u, sb_p = work.take(2, 3 * P), work.take(2, 3 * P)
    neg_max, total = work.take(2, TT), work.take(2, TT)
    stat, rstd = work.take(TT), work.take(TT)
    gl_stat, gl_rstd = work.take(TT, GLA_H), work.take(TT, GLA_H)
    early = Carver(gates.rearrange("p a b -> p (a b)"))
    rows, wk2, wv2 = early.take(P), early.take(2, HD), early.take(2, HD)
    glq, glk = early.take(2, S), early.take(2, S)
    glv, glg = early.take(TT, 512), early.take(TT, 512)
    gla_t, glaT = early.take(2, S), early.take(S)
    lv_d, lv_q, lv_k = early.take(2, 512), early.take(2, 512), early.take(2, 512)
    flat_y = yT.rearrange("p a b -> p (a b)")
    xn = flat_y[:, 0:TT * D].rearrange("p (t d) -> p t d", t=TT)
    wk1_sb = flat_y.rearrange("p (k n) -> p k n", k=CMP_LEN // 2)
    sq = flat_y[:, TT * D:TT * D + D]
    pcT = [yT[:, 4:8, :], yT[:, 12:16, :]]
    blk = Carver(chip["work"], sb_at).take(2, CMP_LEN // 2, THIN)
    mix_t = fxv
    hid_p = fxv[:, 1, :].rearrange("p (i n) -> p i n", i=2)
    ada_p = gla_b.rearrange("p c s -> p (c s)")
    mixedT = sb_qk
    rounded = chip["rounded"]
    late_high = [rounded(f"late_high{n}", qk_at + n * SPLIT_HALF, SPLIT_HALF) for n in range(2)]
    early_high = [rounded(f"early_high{n}", qk_at + (2 + n) * SPLIT_HALF, SPLIT_HALF) for n in range(2)]
    hidden_at = qk_at + 4 * SPLIT_HALF
    hidden = Carver(chip["work"], hidden_at).take(FFK, S)
    hidden_low, hidden_high = rounded("hidden_low", hidden_at, FFK, S), rounded("hidden_high", hidden_at + FFK * S, FFK, S)
    hT_low = rounded("hT_low", after_hT - KD * S, KD, S)
    hT_high = [chip["hT_high"], rounded("hT_high2", after_hT, KD, S)]
    x_kept = out.rearrange("b (t p) d -> p (b t) d", p=P)

    K = lambda name: consts[:, T["f32"][name][0]:sum(T["f32"][name])]
    M = lambda name: masks[:, T["bf16"][name][0]:sum(T["bf16"][name])]
    ident, one, eps = K("ident"), K("one"), K("eps")
    head_sel = K("head_sel").rearrange("p (h t) -> p h t", h=8)
    level_mask = M("levels").bitcast(U16).rearrange("p (n t) -> p n t", n=len(LEVELS) - 1)

    jobs = []
    for c in range(HALF_HEADS):
        for g in range(2):
            jobs += [("slc", c, g), ("win", c, g)]
    jobs += [("fox", h // 2, h % 2) for h in range(8)]
    jobs += [("sb", h // 2, h % 2) for h in range(8)]
    NJ = len(jobs)

    ada_steps = [i for i in range(4 * KD) if i % 8 in (1, 4, 6)]
    step_fills, step_tiles = [], []
    for i in range(4 * KD):
        if i % 4 == 0:
            step_tiles.append(("gate", i // 4))
        step_fills.append(f"g{i}")
        if i in (2, 3):
            step_fills.append(f"gyT{i - 2}")
        if i - 1 in ada_steps:
            step_fills.append(f"adT{ada_steps.index(i - 1)}")
        if i in ada_steps:
            step_fills.append(f"ada{ada_steps.index(i)}")
            step_tiles.append(("ada", ada_steps.index(i)))

    LV = [f"lv{n}_{par}" for n in range(len(LEVELS)) for par in range(2)]
    proj_uses = (["params"] + [f"xT{c}" for c in range(4)]
                 + ["q0", "q1", "kc", "vc", "kskw", "vs", "vwg"]
                 + ["gq", "gk", "hk", "hv", "ga", "gg0", "gg1", "gv0", "gv1"]
                 + ["sq0", "sq1", "sk0", "sk1", "sv0", "sv1", "fq0", "fq1", "fk0", "fk1",
                    "fv0", "fv1", "ff", "fc"]
                 + step_fills
                 + [f"br{n}_{f}" for n in range(4) for f in range(KD // 2)]
                 + [f"wo{h}{t}" for h in range(2) for t in range(TT)]
                 + [f"yT{c}" for c in range(4)]
                 + [f"up{i}" for i in range(FFK // 2)])
    PROJ = Banks(sem, "proj", chip["psum"][0:2], proj_uses)
    SC = Banks(sem, "score", chip["psum"][2:4], ["hkT", "hvT", "kc2", "la", "rope_kc", "vc2", "cmp0", "cmp1"] + [f"s{j}" for j in range(NJ)] + ["down0", "down1"])
    PT = Banks(sem, "turn", chip["psum"][4:6],
               [f"rope{i}" for i in range(3)] + LV + [f"pc{g}{i}" for g in range(2) for i in range(2)]
               + [f"p{j}" for j in range(NJ) if jobs[j][0] != "sb"])
    OT = Banks(sem, "out", chip["psum"][6:8],
               ["go0", "go1"] + [f"o_{k}{c}" for k in ("nsa", "fox", "sb") for c in range(HALF_HEADS)]
               + ["down2", "down3"])

    def done(name):
        return PROJ.full, PROJ.order[name] + 1

    w_in = dram["w_in"][bass.ds(l, 1)].rearrange("l (k p) n -> p (l k) n", p=P)
    whole = (slice(None), slice(None), slice(None))

    def in_tile(name, c0, n, last):
        return name, KD, n, [(whole, w_in[:, :, c0:c0 + n])], done(last)

    down_used = sem("down_used")
    branch = dram["w_branch"][bass.ds(l, 1)].rearrange("l n c d -> (l n) c d")

    def branch_tile(n):
        if n == 0:
            src = branch[0].rearrange("(g c d) m -> g d c m", g=2, d=HD)
            parts = [((slice(g * HD, g * HD + HD), slice(None), slice(None)), src[g]) for g in range(2)]
        else:
            parts = [(whole, branch[n].rearrange("(c p) m -> p c m", p=P))]
        return f"branch{n}", 4, D, parts, done(f"br{n}_{KD // 2 - 1}")

    def layer_of(name):
        return dram[name][bass.ds(l, 1)]

    wk1 = layer_of("nsa_cmp_wk1").rearrange("l (k p) n -> p (l k) n", p=P)
    wv1 = layer_of("nsa_cmp_wv1").rearrange("l (k p) n -> p (l k) n", p=P)
    w_out = layer_of("w_out").rearrange("l (k p) n -> p (l k) n", p=P)
    w_ff1 = layer_of("w_ff1").rearrange("l (k p) n -> p (l k) n", p=P)
    w_ff2 = layer_of("w_ff2").rearrange("l (k p) n -> p (l k) n", p=P)
    def blocks(name, c0, order, last):
        parts = [((slice(None), slice(None), slice(i * HD, (i + 1) * HD)),
                  w_in[:, :, c0 + b * HD:c0 + (b + 1) * HD]) for i, b in enumerate(order)]
        return name, KD, HD * len(order), parts, done(last)

    q_tiles = [blocks(f"q{i}", Q0, [2 * i, 2 * i + 4, 2 * i + 1, 2 * i + 5], f"q{i}") for i in range(2)]
    cmp_tile = blocks("cmp", KC0, [0, 0, 1, 1, 2, 2, 3, 3], "vc")
    tiles = [*q_tiles, cmp_tile, in_tile("kwg", KS0 + 256, 280, "vwg"), in_tile("kvs", KS0, 256, "vs"),
             in_tile("glqk", GLQ0, 512, "gk"),
             ("wv1", 16, CMP_HID, [(whole, wv1)], done("hv")),
             in_tile("glag", GLA0, 528, "gg1"), in_tile("glv", GLV0, 512, "gv1"),
             in_tile("sbq", SBQ0, 512, "sq1"), in_tile("sbk", SBK0, 512, "sk1"), in_tile("sbv", SBV0, 512, "sv1"),
             in_tile("fxq", FXQ0, 512, "fq1"), in_tile("fxk", FXK0, 512, "fk1"), in_tile("fxv", FXV0, 520, "ff")]
    w_ada = layer_of("w_ada_2").rearrange("l (k p) n -> p (l k) n", p=P)
    for kind, i in step_tiles:
        if kind == "gate":
            tiles.append(in_tile(f"gate{i}", GATE0 + 512 * i, 512, f"g{4 * i + 3}"))
        else:
            tiles.append((f"ada{i}", KD, 512, [(whole, w_ada[:, :, 512 * i:512 * i + 512])], done(f"ada{i}")))
    tiles += [branch_tile(n) for n in range(4)]
    tiles += [(f"out{h}", KD, 512, [(whole, w_out[:, :, 512 * h:512 * h + 512])], done(f"wo{h}1")) for h in range(2)]
    tiles += [(f"up{i}", KD, 512, [(whole, w_ff1[:, :, 512 * i:512 * i + 512])], done(f"up{2 * i + 1}")) for i in range(8)]
    tiles += [(f"down{i}", 4, D, [(whole, w_ff2[:, 4 * i:4 * i + 4, :])], (down_used, 2 * i + 2)) for i in range(8)]
    first_whole = [tile[0] for tile in tiles].index("gate0")
    slots = [n % (N_SLOTS - 1) for n in range(first_whole)] + [(N_SLOTS - 1 + n) % N_SLOTS for n in range(len(tiles) - first_whole)]
    W = Weights(sem, "w", chip["ring"], slots, tiles, {"gate0": done("ff")})

    half_used = sem("half_used")
    wide = [("n", 0, 256), ("n", 256, 256)]
    cuts = [("q0", wide[:1], ["q0"]), ("q1", wide[:1], ["q1"]), ("cmp", wide, ["kc", "vc"]), ("kwg", [("n", 0, P)], ["kskw"]),
            ("kvs", wide[:1], ["vs"]), ("kwg", [("n", P, 152)], ["vwg"]), ("glqk", wide, ["gq", "gk"]),
            ("glag", [("n", 0, GLA_RANK), ("n", GLA_RANK, 256), ("n", GLA_RANK + 256, 256)], ["ga", 1, "gg1"]),
            ("glv", wide, [2, "gv1"]), ("sbq", wide, ["sq0", "sq1"]), ("sbk", wide, ["sk0", "sk1"]), ("sbv", wide, [3, "sv1"]),
            ("fxq", wide, ["fq0", "fq1"]), ("fxk", wide, ["fk0", "fk1"]), ("fxv", [wide[0], ("n", 256, 264)], [4, "ff"])]
    parts = [(name, part[1], *part) for name, ranges, _ in cuts for part in ranges]
    freed = [(half_used, end) if isinstance(end, int) else done(end) for _, _, ends in cuts for end in ends]
    Y = Split(sem, "in", W, chip["ring_low"], chip["ring_high"], parts, freed)
    halves = [(f"up{i}", b, "n", 2 * P * b, 2 * P) for i in range(8) for b in range(2)]
    halves += [(f"down{i}", b, "k", 2 * b, 2) for i in range(8) for b in range(2)]
    X = Split(sem, "ff", W, chip["ring_low"], early_high + late_high, halves,
              [done(f"up{n}") for n in range(16)] + [(down_used, n + 1) for n in range(15)])

    rows_in = sem("rows_in")
    small_in = sem("small_in")
    rstd_ready = sem("rstd_ready")
    xn_ready = sem("xn_ready")
    gelu_x2 = sem("gelu_x2")
    gelu_in = sem("gelu_in")
    gelu_exp = sem("gelu_exp")
    roped = sem("roped")
    gate_ready = sem("gate_ready")
    cmp_in = sem("cmp_in")
    cmp_exp = sem("cmp_exp")
    cmp_ready = sem("cmp_ready")
    gl_gate = sem("gl_gate")
    la_log = sem("la_log")
    lv_diff = sem("lv_diff")
    lv_exp = sem("lv_exp")
    lv_ready = sem("lv_ready")
    gl_scale = sem("gl_scale")
    fox_log = sem("fox_log")
    fox_ready = sem("fox_ready")
    max_ready = sem("max_ready")
    prob_ready = sem("prob_ready")
    sb_log = sem("sb_log")
    sb_soft = sem("sb_soft")
    sb_later = sem("sb_later")
    mix_gate = sem("mix_gate")
    mixed_ready = sem("mixed_ready")
    wk1_in = sem("wk1_in")
    x_saved, x_back = sem("x_saved"), sem("x_back")
    hT_whole = sem("hT_whole")
    hT_cut = sem("hT_cut")
    hidden_squared = sem("hidden_squared")
    hidden_ready = sem("hidden_ready")
    act_self, dve_self = sem("act_self"), sem("dve_self")

    with nc.Block() as block:

        @block.sync
        def _(sp):
            def row_load(at, n, src):
                sp.dma_start(rows[at:at + n, :], src).then_inc(rows_in, 16)

            row_load(ROW_MIX, KD, layer_of("norm_mix").rearrange("l (r p) -> (l r) p", p=P))
            row_load(ROW_FF, KD, layer_of("norm_ff").rearrange("l (r p) -> (l r) p", p=P))
            row_load(ROW_GATE, 4 * KD, layer_of("b_gate").rearrange("l (r p) -> (l r) p", p=P))
            row_load(ROW_GLB, 2, layer_of("gla_b_alpha").rearrange("l (r p) -> (l r) p", p=P))
            row_load(ROW_GLN, 1, layer_of("gla_norm"))
            row_load(ROW_PEK, 16, layer_of("nsa_cmp_pos_k").rearrange("l (r a) d -> (l r) (a d)", a=2))
            row_load(ROW_PEV, 16, layer_of("nsa_cmp_pos_v").rearrange("l (r a) d -> (l r) (a d)", a=2))

            sp.dma_start(x_kept, x).then_inc(x_saved, 16)
            back_at = W.order["branch2"]
            W.load(sp, 0, 3)
            sp.wait_ge(*done("xT3"))
            sp.dma_start(wk1_sb, wk1).then_inc(wk1_in, 16)
            W.load(sp, 3, back_at)
            sp.wait_ge(hT_whole, 1)
            sp.wait_ge(x_saved, 16)
            sp.dma_start(x, x_kept).then_inc(x_back, 16)
            W.load(sp, back_at)

        @block.tensor
        def _(pe):
            def mm(out, lhsT, rhs, start, stop):
                return nc.tensor.matmul(out, lhsT, rhs, start=start, stop=stop)

            def turn(out, src):
                return nc.tensor.transpose(out, src, ident[0:src.shape[0], 0:src.shape[0]])

            mixer_x = (hT_high[0], hT_low)

            def gemm_T(out, w, cols):
                for k in range(KD):
                    last = product(nc, out, [part[:, k, cols] for part in w], [part[:, k, :] for part in mixer_x],
                                   k == 0, k == KD - 1)
                return last

            def gemm(out, w, cols, t):
                for k in range(KD):
                    last = product(nc, out, [part[:, k, t * P:t * P + P] for part in mixer_x], [part[:, k, cols] for part in w],
                                   k == 0, k == KD - 1)
                return last

            def token_major(name, tile, first=0):
                banks = [PROJ.claim(pe, f"{name}{t}") for t in range(TT)]
                for b in range(2):
                    w = Y.arrived(pe, tile, first + 256 * b)
                    for t in range(TT):
                        last = gemm(banks[t][:, 256 * b:256 * b + 256], w, slice(0, 256), t)
                        if b == 1:
                            last.then_inc(PROJ.full, 1)
                            yield t
                    if b == 0:
                        last.then_inc(half_used, 1)

            def pair(name, tile, which):
                w = Y.arrived(pe, tile, 256 * which)
                ps = PROJ.claim(pe, name)
                for k in range(2):
                    last = gemm_T(ps[:, k * S:(k + 1) * S], w, slice(k * P, k * P + P))
                last.then_inc(PROJ.full, 1)

            def turn_x(name, ready):
                pe.wait_ge(xn_ready, ready)
                for c in range(4):
                    ps = PROJ.claim(pe, f"{name}{c}")
                    for k in range(2):
                        for t in range(TT):
                            last = turn(ps[:, (2 * k + t) * P:(2 * k + t + 1) * P],
                                        xn[:, t, (2 * c + k) * P:(2 * c + k + 1) * P])
                    last.then_inc(PROJ.full, 1)

            def thin(ps, thin_T, w, chunks):
                for k in range(chunks):
                    rows_of = slice(k % 4 * THIN, k % 4 * THIN + THIN)
                    last = mm(ps[rows_of, 0:w.shape[2]], thin_T[:, k, :], w[:, k, :], k < 4, k >= chunks - 4)
                return last

            pe.wait_ge(rows_in, 7 * 16)
            turn(PROJ.claim(pe, "params")[:, 0:N_ROWS], rows[0:N_ROWS, :]).then_inc(PROJ.full, 1)
            turn_x("xT", TT)

            pe.wait_ge(hT_cut, KD // 2)
            for i in range(2):
                pair(f"q{i}", f"q{i}", 0)
            for i, name in enumerate(("kc", "vc")):
                pair(name, "cmp", i)
            ps = PROJ.claim(pe, "kskw")
            gemm_T(ps[:, S:2 * S], Y.arrived(pe, "kwg", 0), slice(0, P))
            w = Y.arrived(pe, "kvs", 0)
            gemm_T(ps[:, 0:S], w, slice(0, P)).then_inc(PROJ.full, 1)
            ps = PROJ.claim(pe, "vs")
            for t in range(TT):
                last = gemm(ps[:, t * P:(t + 1) * P], w, slice(P, 2 * P), t)
            last.then_inc(PROJ.full, 1)
            w = Y.arrived(pe, "kwg", P)
            ps = PROJ.claim(pe, "vwg")
            for t in range(TT):
                last = gemm(ps[:, t * 152:(t + 1) * 152], w, slice(0, 152), t)
            last.then_inc(PROJ.full, 1)

            def rope(i):
                ps = PT.claim(pe, f"rope{i}")
                PROJ.taken(pe, ("q0", "q1", "kskw")[i])
                mm(ps[:, :], K("rot"), nsaT[:, 2 * i:2 * i + 2, :], True, True).then_inc(PT.full, 1)

            rope(0)
            rope(1)
            for i, name in enumerate(("gq", "gk")):
                pair(name, "glqk", i)
            rope(2)
            for i, name in enumerate(("hk", "hv")):
                if i == 0:
                    pe.wait_ge(wk1_in, 16)
                w = wk1_sb if i == 0 else W.arrived(pe, "wv1")
                ps = PROJ.claim(pe, name)
                PROJ.taken(pe, ("kc", "vc")[i])
                thin(ps, blk[:, i], w, CMP_LEN // 2).then_inc(PROJ.full, 1)
            for i, name in enumerate(("hk", "hv")):
                ps = SC.claim(pe, name + "T")
                PROJ.taken(pe, name)
                for m in range(2):
                    last = mm(ps[:, m * 2 * N_CMP:(m + 1) * 2 * N_CMP], hid_p[:, i, m * P:(m + 1) * P],
                              K("sum4")[:, 0:2 * N_CMP], True, True)
                last.then_inc(SC.full, 1)

            gemm_T(PROJ.claim(pe, "ga")[0:GLA_RANK, 0:S], Y.arrived(pe, "glag", 0), slice(0, GLA_RANK)).then_inc(PROJ.full, 1)

            for t in token_major("gg", "glag", GLA_RANK):
                pass

            ps = SC.claim(pe, "kc2")
            pe.wait_ge(small_in, 4 * 16)
            SC.taken(pe, "hkT")
            for g in range(2):
                for m in range(2):
                    last = mm(ps[g * HD:(g + 1) * HD, 0:N_CMP], wk2[:, m, :],
                              hid_c[:, 0, m, g * N_CMP:(g + 1) * N_CMP], m == 0, m == 1)
            last.then_inc(SC.full, 1)
            ps = SC.claim(pe, "la")
            PROJ.taken(pe, "ga")
            for c in range(2):
                last = mm(ps[:, c * S:(c + 1) * S], w_alpha[0:GLA_RANK, c * P:(c + 1) * P], glaT[0:GLA_RANK, :], True, True)
            last.then_inc(SC.full, 1)
            ps = SC.claim(pe, "rope_kc")
            SC.taken(pe, "kc2")
            mm(ps[:, 0:N_CMP], K("rot"), kcT, True, True).then_inc(SC.full, 1)
            for t in token_major("gv", "glv"):
                pass
            ps = SC.claim(pe, "vc2")
            SC.taken(pe, "hvT")
            for g in range(2):
                for m in range(2):
                    last = mm(ps[0:N_CMP, g * HD:(g + 1) * HD], hid_c[:, 1, m, g * N_CMP:(g + 1) * N_CMP],
                              wv2[:, m, :], m == 0, m == 1)
            last.then_inc(SC.full, 1)

            pe.wait_ge(roped, 4)
            for g in range(2):
                ps = SC.claim(pe, f"cmp{g}")
                for c in range(4):
                    for t in range(TT):
                        at = (c * TT + t) * N_CMP
                        last = mm(ps[:, at:at + N_CMP], nsaT[g * HD:(g + 1) * HD, c, t * P:(t + 1) * P],
                                  kcT[g * HD:(g + 1) * HD, :], True, True)
                last.then_inc(SC.full, 1)

            def level(n):
                if LEVELS[n] == 0:
                    PROJ.taken(pe, "gq", "gk")
                else:
                    pe.wait_ge(lv_ready, n + (n == 0))
                at = max(n - 1, 0) % 2
                q = glq if LEVELS[n] == 0 else lv_q[:, at].rearrange("p (c s) -> p c s", c=2)
                k = glk if LEVELS[n] == 0 else lv_k[:, at].rearrange("p (c s) -> p c s", c=2)
                for par in range(2):
                    ps = PT.claim(pe, f"lv{n}_{par}")
                    r = slice(par * HD, (par + 1) * HD)
                    for c in range(2):
                        for t in ([1] if LEVELS[n] == P else range(TT)):
                            at = c * P if LEVELS[n] == P else (t * 2 + c) * P
                            s = 0 if LEVELS[n] == P else t
                            last = mm(ps[:, at:at + P], k[r, c, s * P:(s + 1) * P], q[r, c, t * P:(t + 1) * P], True, True)
                    last.then_inc(PT.full, 1)

            for i in range(2):
                pair(f"sq{i}", "sbq", i)
                level(i)
            for i in range(2):
                pair(f"sk{i}", "sbk", i)
                level(2 + i)
            for t in token_major("sv", "sbv"):
                level(4 + t)
            for i in range(2):
                pair(f"fq{i}", "fxq", i)
                level(6 + i)
            for i in range(2):
                pair(f"fk{i}", "fxk", i)
                if i == 0:
                    level(8)
            for t in token_major("fv", "fxv"):
                pass
            ps = PROJ.claim(pe, "ff")
            w = Y.arrived(pe, "fxv", 256)
            for t in range(TT):
                last = gemm(ps[:, t * 8:(t + 1) * 8], w, slice(256, 264), t)
            last.then_inc(PROJ.full, 1)

            PT.taken(pe, "lv8_0", "lv8_1")
            PROJ.taken(pe, "gv0", "gv1")
            for t in range(TT):
                ps = OT.claim(pe, f"go{t}")
                for h in range(GLA_H):
                    dv = slice(h * GLA_DV, (h + 1) * GLA_DV)
                    last = mm(ps[:, dv], att[:, h % 2, t, h // 2, :], glv[:, t, dv], True, t == 0)
                    if t == 1:
                        last = mm(ps[:, dv], att[:, h % 2, 2, h // 2, :], glv[:, 0, dv], False, True)
                last.then_inc(OT.full, 1)

            ps = PROJ.claim(pe, "fc")
            pe.wait_ge(fox_ready, 1)
            upto = consts[:, T["f32"]["neg_upto"][0]:T["f32"]["neg_upto"][0] + S]
            mm(ps[0:8, 0:S], log_f[:, 0, :], upto, True, False)
            mm(ps[0:8, P:S], log_f[:, 1, :], upto[:, 0:P], False, True).then_inc(PROJ.full, 1)

            def turn_gla(t):
                ps = PROJ.claim(pe, f"gyT{t}")
                OT.taken(pe, f"go{t}")
                for h in range(GLA_H):
                    last = turn(ps[:, h * P:(h + 1) * P], gle[:, t, h * GLA_DV:(h + 1) * GLA_DV])
                last.then_inc(PROJ.full, 1)

            def turn_compressed():
                for g in range(2):
                    pe.wait_ge(cmp_ready, g + 1)
                    for i in range(2):
                        ps = PT.claim(pe, f"pc{g}{i}")
                        for c in range(2):
                            for t in range(TT):
                                at = (c * TT + t) * P
                                last = turn(ps[0:N_CMP, at:at + P], p_cmp[:, g, 2 * i + c, t, :])
                        last.then_inc(PT.full, 1)

            def scores(j):
                kind, c, par = jobs[j]
                r = slice(par * HD, (par + 1) * HD)
                ps = SC.claim(pe, f"s{j}")
                if kind == "sb":
                    mm(ps[:, 0:S], sbk[r, c, 0:P], sbq[r, c, :], True, False)
                    mm(ps[:, S:S + P], sbk[r, c, P:S], sbq[r, c, P:S], False, False)
                    mm(ps[:, 0:P], M("ident"), M("strict"), False, False)
                    mm(ps[:, S:S + P], M("ident"), M("strict"), False, True).then_inc(SC.full, 1)
                    return
                for t in range(TT):
                    n = (t + 1) * P
                    at = t * P
                    if kind == "fox":
                        mm(ps[:, at:at + n], fxq[r, c, t * P:(t + 1) * P], fxk[r, c, 0:n], True, False)
                        mm(ps[:, at:at + n], head_sel[0:8, 2 * c + par, :], fox_row[0:8, 0:n], False, False)
                    else:
                        mm(ps[:, at:at + n], nsaT[r, c, t * P:(t + 1) * P], nsaT[r, 4 + (kind == "win"), 0:n], True, False)
                    last = mm(ps[:, at + n - P:at + n], M("ident"), M("causal"), False, True)
                last.then_inc(SC.full, 1)

            def turned(j):
                kind, c, par = jobs[j]
                if kind == "sb":
                    ps = SC.bank(f"s{j}")
                    pe.wait_ge(sb_soft, j - 23)
                    sp_ = sb_p[:, j % 2]
                    add = lambda out, neg, rhs: nc.tensor.matmul(out, K(neg), rhs, start=False, stop=True, skip_group_check=True)
                    add(ps[:, 0:S], "neg_from", sp_[:, 0:S])
                    add(ps[:, P:S], "neg_ones", sp_[:, S:S + P])
                    add(ps[:, S:S + P], "neg_from", sp_[:, S:S + P]).then_inc(sb_later, 1)
                    return
                ps = PT.claim(pe, f"p{j}")
                pe.wait_ge(prob_ready, j + 1)
                p = prob[:, j % 2]
                turn(ps[:, 0:P], p[:, 0:P])
                turn(ps[:, P:2 * P], p[:, P:2 * P])
                turn(ps[:, 2 * P:3 * P], p[:, 2 * P:3 * P]).then_inc(PT.full, 1)

            def output(j):
                kind, c, par = jobs[j]
                r = slice(par * HD, (par + 1) * HD)
                group = "nsa" if kind in ("slc", "win") else kind
                name = f"o_{group}{c}"
                first, last_of = (kind != "win"), (kind != "slc")
                ps = OT.claim(pe, name) if first and par == 0 else OT.bank(name)
                if kind == "slc":
                    PT.taken(pe, f"pc{par}{c // 2}")
                    mm(ps[r, 0:S], vc[0:N_CMP, par, :], pcT[par][0:N_CMP, c, :], True, False)
                if kind == "sb":
                    SC.taken(pe, f"s{j}")
                    p, v = probT[:, j % 2], sbv[:, :, (2 * c + par) * HD:(2 * c + par + 1) * HD]
                else:
                    PT.taken(pe, f"p{j}")
                    p = probT[:, j % 2]
                    v = {"slc": vs, "win": vw}[kind][:, :, r] if kind != "fox" else \
                        fxv[:, :, (2 * c + par) * HD:(2 * c + par + 1) * HD]
                mm(ps[r, 0:S], v[:, 0, :], p[:, 0:S], kind in ("sb", "fox"), False)
                last = mm(ps[r, P:S], v[:, 1, :], p[:, S:S + P], False, last_of)
                if par == 1 and last_of:
                    last.then_inc(OT.full, 1)

            PROJ.taken(pe, "vs", "vwg")
            SC.taken(pe, "vc2")
            for i in range(NJ + 2):
                if i < 4 * KD:
                    w = W.arrived(pe, f"gate{i // 4}")
                    ps = PROJ.claim(pe, f"g{i}")
                    if i == 0:
                        pe.wait_ge(hT_whole, 1)
                    for k in range(KD):
                        last = mm(ps[:, 0:S], w[:, k, i % 4 * P:(i % 4 + 1) * P], hT[:, k, :], k == 0, k == KD - 1)
                    last.then_inc(PROJ.full, 1)
                if i in (2, 3):
                    turn_gla(i - 2)
                if i - 1 in ada_steps:
                    n = ada_steps.index(i - 1)
                    ps = PROJ.claim(pe, f"adT{n}")
                    PROJ.taken(pe, f"ada{n}")
                    for c in range(4):
                        last = mm(ps[:, 2 * c:2 * c + 2], ada_p[:, c * P:(c + 1) * P], K("sum4")[:, 0:2], True, True)
                    last.then_inc(PROJ.full, 1)
                if i in ada_steps:
                    n = ada_steps.index(i)
                    w = W.arrived(pe, f"ada{n}")
                    thin(PROJ.claim(pe, f"ada{n}"), silu_c, w, KD).then_inc(PROJ.full, 1)
                if i == 15:
                    PROJ.taken(pe, "fc", "fv0", "fv1", "fk0", "fk1")
                if i < NJ:
                    scores(i)
                if i == 0:
                    turn_compressed()
                if 1 <= i <= NJ:
                    turned(i - 1)
                if i >= 2:
                    output(i - 2)

            for n in range(4):
                w = W.arrived(pe, f"branch{n}")
                if n == 0:
                    PROJ.taken(pe, "gyT0", "gyT1")
                    OT.taken(pe, "o_sb2", "o_sb3")
                for f in range(KD // 2):
                    ps = PROJ.claim(pe, f"br{n}_{f}")
                    for k in range(2):
                        for c in range(4):
                            last = mm(ps[:, k * S:(k + 1) * S], w[:, c, (2 * f + k) * P:(2 * f + k + 1) * P],
                                      yT[:, 4 * n + c, :], c == 0, c == 3)
                    last.then_inc(PROJ.full, 1)
            pe.wait_ge(mixed_ready, 3 * KD // 2)
            for h in range(2):
                w = W.arrived(pe, f"out{h}")
                for t in range(TT):
                    ps = PROJ.claim(pe, f"wo{h}{t}")
                    for k in range(KD):
                        last = mm(ps[:, :], mixedT[:, k, t * P:(t + 1) * P], w[:, k, :], k == 0, k == KD - 1)
                    last.then_inc(PROJ.full, 1)

            turn_x("yT", 2 * TT)
            PROJ.taken(pe, "yT2", "yT3")
            pe.wait_ge(hT_cut, KD)
            for i in range(8):
                for b in range(2):
                    w = X.arrived(pe, f"up{i}", b)
                    ps = PROJ.claim(pe, f"up{2 * i + b}")
                    for c in range(2):
                        for k in range(KD):
                            last = product(nc, ps[:, c * S:(c + 1) * S], [part[:, k, c * P:(c + 1) * P] for part in w],
                                           [part[:, k, :] for part in (hT_high[1], hT_low)], k == 0, k == KD - 1)
                    last.then_inc(PROJ.full, 1)
            downs = [SC.claim(pe, "down0"), SC.claim(pe, "down1"), OT.claim(pe, "down2"), OT.claim(pe, "down3")]
            for i in range(8):
                for b in range(2):
                    w = X.arrived(pe, f"down{i}", b)
                    pe.wait_ge(hidden_ready, 2 * i + b + 1)
                    for k in range(2):
                        c = 4 * i + 2 * b + k
                        for t in range(TT):
                            for h in range(2):
                                last = product(nc, downs[2 * t + h][:, :], [part[:, c, t * P:(t + 1) * P] for part in (hidden_high, hidden_low)],
                                               [part[:, k, 512 * h:512 * h + 512] for part in w], c == 0, c == FFK - 1)
                                if c == FFK - 1:
                                    last.then_inc((SC, OT)[t].full, 1)
                    if c < FFK - 1:
                        last.then_inc(down_used, 1)

        @block.scalar
        def _(act):
            link = Chain(act, act_self)

            def f(out, in_, func, **kw):
                return nc.scalar.activation(out, in_, func, **kw)

            def copy(out, in_, **kw):
                return f(out, in_, ACT.Copy, **kw)

            def take(name, out, in_=slice(None), **kw):
                ps = PROJ.arrived(act, name)
                copy(out, ps[:, in_], **kw).then_inc(PROJ.free(name), 1)

            def row_scale(ready):
                link(f(rstd, eps.to_broadcast([P, TT]), ACT.Sqrt))
                for t in range(TT):
                    ready(t)
                    link(f(sq, x[:, t, :], ACT.Square, accum_out=stat[:, t:t + 1]))
                f(rstd, stat, ACT.Sqrt, scale=1.0 / D, bias=eps).then_inc(rstd_ready, 1)

            def take_hT(name, row, high):
                for c in range(4):
                    ps = PROJ.arrived(act, f"{name}{c}")
                    for k in range(2):
                        copy(high[:, 2 * c + k, :], ps[:, k * S:k * S + S], scale=cols[:, row + 2 * c + k:row + 2 * c + k + 1])
                    copy(hT[:, 2 * c, :], ps[:, 0:S], scale=cols[:, row + 2 * c:row + 2 * c + 1])
                    copy(hT[:, 2 * c + 1, :], ps[:, S:2 * S], scale=cols[:, row + 2 * c + 1:row + 2 * c + 2])\
                        .then_inc(PROJ.free(f"{name}{c}"), 1)

            def log1p_exp_neg_abs(out, in_):
                link(f(out, in_, ACT.Abs))
                link(f(out, out, ACT.Exp, scale=-1.0))
                return f(out, out, ACT.Ln, bias=one)

            def level_exp(k):
                act.wait_ge(lv_diff, k + 1)
                link(f(lv_d[:, k % 2], lv_d[:, k % 2], ACT.Abs))
                f(lv_d[:, k % 2], lv_d[:, k % 2], ACT.Exp, scale=-1.0 / GLA_TAU).then_inc(lv_exp, 1)

            act.dma_start(wk2, layer_of("nsa_cmp_wk2").rearrange("l (k p) n -> p (l k) n", p=P)).then_inc(small_in, 16)
            act.dma_start(wv2, layer_of("nsa_cmp_wv2").rearrange("l (k p) n -> p (l k) n", p=P)).then_inc(small_in, 16)
            act.dma_start(w_alpha[0:GLA_RANK, :], layer_of("gla_w_alpha").rearrange("l r n -> (l r) n")).then_inc(small_in, 16)
            act.dma_start(fox_b, layer_of("fox_b_f").partition_broadcast(P).rearrange("p l h -> p (l h)")).then_inc(small_in, 16)

            row_scale(lambda t: None)
            ps = PROJ.arrived(act, "params")
            copy(cols[:, 0:ROW_GATE], ps[:, 0:ROW_GATE])
            copy(cols[:, ROW_GATE:ROW_GLB], ps[:, ROW_GATE:ROW_GLB], scale=-1.0)
            link(copy(cols[:, ROW_GLB:N_ROWS], ps[:, ROW_GLB:N_ROWS]))
            copy(kc_sin, ps[:, 0:N_CMP]).then_inc(PROJ.free("params"), 1)
            act.wait_ge(x_saved, 16)
            Y.make_high(nc, act, 0)
            take_hT("xT", ROW_MIX, hT_high[0])
            Y.make_high(nc, act, 1)

            for i in range(2):
                take(f"q{i}", nsaT[:, 2 * i:2 * i + 2, :].rearrange("p a b -> p (a b)"), scale=HD ** -0.5)
                Y.make_high(nc, act, 2 + i)
            Y.make_high(nc, act, 4, 5)
            take("kskw", nsaT[:, 4:6, :].rearrange("p a b -> p (a b)"))
            Y.make_high(nc, act, 6)
            take("vs", vs.rearrange("p a b -> p (a b)"), slice(0, S))
            Y.make_high(nc, act, 7)
            ps = PROJ.arrived(act, "vwg")[:, 0:TT * 152].rearrange("p (t n) -> p t n", t=TT)
            copy(vw, ps[:, :, 0:P])
            f(g_nsa, ps[:, :, P:152], ACT.Exp, scale=-1.0).then_inc(PROJ.free("vwg"), 1)
            Y.make_high(nc, act, 8)
            take("gq", glq.rearrange("p a b -> p (a b)"), scale=HD ** -0.5)
            Y.make_high(nc, act, 9)
            take("gk", glk.rearrange("p a b -> p (a b)"))
            Y.make_high(nc, act, 10)
            for i, name in enumerate(("hk", "hv")):
                take(name, hid_p[:, i], slice(0, CMP_HID))
            for i, name in enumerate(("hkT", "hvT")):
                ps = SC.arrived(act, name)[:, 0:4 * N_CMP].rearrange("p (m n) -> p m n", m=2)
                f(gelu_t, ps, ACT.Square).then_inc(gelu_x2, 1)
                act.wait_ge(gelu_in, i + 1)
                f(gelu_e, gelu_t, ACT.Exp, scale=-2.0 * GELU_C).then_inc(gelu_exp, 1)
                SC.taken(act, name)

            ps = PROJ.arrived(act, "ga")
            copy(glaT[0:GLA_RANK, :], ps[0:GLA_RANK, 0:S]).then_inc(PROJ.free("ga"), 1)
            Y.make_high(nc, act, 11)
            Y.make_high(nc, act, 12)
            for t in range(TT):
                ps = PROJ.arrived(act, f"gg{t}")
                copy(glg[:, t, :], ps[:, :])
                f(gle[:, t, :], ps[:, :], ACT.Exp, scale=-1.0).then_inc(PROJ.free(f"gg{t}"), 1)
                if t == 0:
                    Y.make_high(nc, act, 13)
            ps = SC.arrived(act, "kc2")
            copy(kcT, ps[:, 0:N_CMP]).then_inc(SC.free("kc2"), 1)
            ps = SC.arrived(act, "la")
            for c in range(2):
                link(f(gla_t[:, c, :], ps[:, c * S:(c + 1) * S], ACT.Abs, bias=cols[:, ROW_GLB + c:ROW_GLB + c + 1]))
            link(f(gla_t, gla_t, ACT.Exp, scale=-1.0))
            f(gla_t, gla_t, ACT.Ln, bias=one).then_inc(la_log, 1)
            for t in range(TT):
                if t == 0:
                    Y.make_high(nc, act, 14)
                take(f"gv{t}", glv[:, t, :])
            ps = SC.arrived(act, "vc2")
            copy(vc[0:N_CMP], ps[0:N_CMP, 0:P].rearrange("p (g d) -> p g d", g=2)).then_inc(SC.free("vc2"), 1)
            Y.make_high(nc, act, 15)

            level_exp(0)
            level_exp(1)
            for i, (name, out, kw) in enumerate((
                    ("sq0", sbq[:, 0:2, :], {"scale": HD ** -0.5}), ("sq1", sbq[:, 2:4, :], {"scale": HD ** -0.5}),
                    ("sk0", sbk[:, 0:2, :], {}), ("sk1", sbk[:, 2:4, :], {}),
                    ("sv0", sbv[:, 0:1, :], {}), ("sv1", sbv[:, 1:2, :], {}),
                    ("fq0", fxq[:, 0:2, :], {"scale": HD ** -0.5}), ("fq1", fxq[:, 2:4, :], {"scale": HD ** -0.5}),
                    ("fk0", fxk[:, 0:2, :], {}), ("fk1", fxk[:, 2:4, :], {}),
                    ("fv0", fxv[:, 0:1, :], {}), ("fv1", fxv[:, 1:2, :], {}))):
                take(name, out.rearrange("p a b -> p (a b)"), **kw)
                Y.make_high(nc, act, 16 + i)
                if 2 <= i + 1 <= len(LEVELS) - 2:
                    level_exp(i + 1)
            PROJ.taken(act, "ff")
            log1p_exp_neg_abs(log_f, fox_t).then_inc(fox_log, 1)

            for t in range(TT):
                ps = OT.arrived(act, f"go{t}")
                for h in range(GLA_H):
                    link(f(gla_t[:, 0, 0:P], ps[:, h * P:(h + 1) * P], ACT.Square, accum_out=gl_stat[:, t, h:h + 1]))
                link(f(gl_stat[:, t], gl_stat[:, t], ACT.Ln, scale=1.0 / GLA_DV, bias=eps))
                f(gl_rstd[:, t], gl_stat[:, t], ACT.Exp, scale=-0.5).then_inc(gl_scale, 1)

            for g in range(2):
                act.wait_ge(cmp_in, g + 1)
                f(p_cmp[:, g], p_cmp[:, g], ACT.Exp).then_inc(cmp_exp, 1)
            for g in range(2):
                for i in range(2):
                    ps = PT.arrived(act, f"pc{g}{i}")
                    copy(pcT[g][0:N_CMP, 2 * i:2 * i + 2, :], ps[0:N_CMP, :].rearrange("p (c s) -> p c s", c=2))\
                        .then_inc(PT.free(f"pc{g}{i}"), 1)
            ps = PROJ.arrived(act, "fc")
            copy(fox_row[0:8, :], ps[0:8, 0:S]).then_inc(PROJ.free("fc"), 1)
            for i in range(NJ + 2):
                if i < 4 * KD:
                    ps = PROJ.arrived(act, f"g{i}")
                    f(gates[:, i, :], ps[:, 0:S], ACT.Exp, scale=-1.0, bias=cols[:, ROW_GATE + i:ROW_GATE + i + 1])\
                        .then_inc(PROJ.free(f"g{i}"), 1)
                if i in (2, 3):
                    t = i - 2
                    ps = PROJ.arrived(act, f"gyT{t}")
                    copy(yT[:, 8:12, t * P:(t + 1) * P], ps[:, :].rearrange("p (h s) -> p h s", h=GLA_H),
                         scale=cols[:, ROW_GLN:ROW_GLN + 1]).then_inc(PROJ.free(f"gyT{t}"), 1)
                if i - 1 in ada_steps:
                    n = ada_steps.index(i - 1)
                    ps = PROJ.arrived(act, f"adT{n}")
                    copy(chip["mod"][:, bass.ds(l * (2 * MODC) + 8 * n, 8)], ps[:, 0:8]).then_inc(PROJ.free(f"adT{n}"), 1)
                if i in ada_steps:
                    take(f"ada{ada_steps.index(i)}", ada_p)
                if i < NJ and jobs[i][0] == "sb":
                    ps = SC.arrived(act, f"s{i}")
                    log1p_exp_neg_abs(sb_u[:, i % 2], ps[:, 0:3 * P]).then_inc(sb_log, 1)
                elif i < NJ:
                    act.wait_ge(max_ready, i + 1)
                    ps = SC.arrived(act, f"s{i}")
                    f(prob[:, i % 2, 0:P], ps[:, 0:P], ACT.Exp, bias=neg_max[:, i % 2, 0:1],
                      accum_out=total[:, i % 2, 0:1])
                    f(prob[:, i % 2, P:3 * P], ps[:, P:3 * P], ACT.Exp, bias=neg_max[:, i % 2, 1:2],
                      accum_out=total[:, i % 2, 1:2]).then_inc(SC.free(f"s{i}"), 1)
                if 1 <= i <= NJ and jobs[i - 1][0] == "sb":
                    act.wait_ge(sb_later, i - 24)
                    ps = SC.arrived(act, f"s{i - 1}")
                    f(probT[:, (i - 1) % 2], ps[:, 0:3 * P], ACT.Exp).then_inc(SC.free(f"s{i - 1}"), 1)
                elif 1 <= i <= NJ:
                    ps = PT.arrived(act, f"p{i - 1}")
                    copy(probT[:, (i - 1) % 2], ps[:, 0:3 * P]).then_inc(PT.free(f"p{i - 1}"), 1)
                if i >= 2:
                    kind, c, par = jobs[i - 2]
                    if kind != "slc" and par == 1:
                        group, at = {"win": ("nsa", 0), "sb": ("sb", 4), "fox": ("fox", 12)}[kind]
                        ps = OT.arrived(act, f"o_{group}{c}")
                        copy(yT[:, at + c, :], ps[:, 0:S]).then_inc(OT.free(f"o_{group}{c}"), 1)

            X.make_high(nc, act, 0, 1)
            row_scale(lambda t: PROJ.taken(act, f"wo0{t}", f"wo1{t}"))
            take_hT("yT", ROW_FF, hT_high[1])
            X.make_high(nc, act, 2, 3)
            for i in range(FFK // 2):
                ps = PROJ.arrived(act, f"up{i}")
                part = hidden[:, 2 * i:2 * i + 2, :].rearrange("p a b -> p (a b)")
                f(part, ps[:, :], ACT.Relu).then_inc(PROJ.free(f"up{i}"), 1)
                PROJ.taken(act, f"up{i}")
                link(f(hidden_high[:, 2 * i:2 * i + 2, :].rearrange("p a b -> p (a b)"), part, ACT.Square))
                f(part, part, ACT.Square).then_inc(hidden_squared, 1)
                X.make_high(nc, act, i + 4)
            X.make_high(nc, act, *range(FFK // 2 + 4, FFK))

        @block.vector
        def _(dve):
            link = Chain(dve, dve_self)
            vec = nc.vector

            def norm(count):
                dve.wait_ge(rstd_ready, count)
                link(vec.reciprocal(rstd, rstd))
                for t in range(TT):
                    vec.tensor_scalar(xn[:, t, :], x[:, t, :], rstd[:, t:t + 1], None, ALU.mult).then_inc(xn_ready, 1)

            def sigmoid(e):
                link(vec.tensor_scalar_add(e, e, 1.0))
                link(vec.reciprocal(e, e))

            def low_bits(high):
                for c in range(KD // 2):
                    part = slice(2 * c, 2 * c + 2)
                    PROJ.taken(dve, f"{'xT' if high is hT_high[0] else 'yT'}{c}")
                    vec.tensor_tensor(hT_low[:, part, :], hT[:, part, :], high[:, part, :].bitcast(F32), ALU.subtract)\
                        .then_inc(hT_cut, 1)

            norm(1)
            Y.make_low(nc, dve, 0)
            low_bits(hT_high[0])
            Y.make_low(nc, dve, 1)
            link(vec.memset(att[:, :, 0:2].rearrange("p a b c d -> p a (b c d)"), 0.0))

            link(vec.memset(blk[:, :, :, 2 * N_CMP:THIN], 0.0))
            for i, name in enumerate(("kc", "vc")):
                if i == 0:
                    PROJ.taken(dve, "params")
                Y.make_low(nc, dve, *(((2, 3), (4,))[i]))
                ps = PROJ.arrived(dve, name)
                row = (ROW_PEK, ROW_PEV)[i]
                for g in range(2):
                    tok = ps[:, g * S:(g + 1) * S].rearrange("p (n b r) -> p r b n", n=16, r=2)
                    for r in range(2):
                        h = slice(r * HD, (r + 1) * HD)
                        for a in range(2):
                            last = vec.tensor_tensor(blk[h, i, 8 * a:8 * a + 8, g * N_CMP:(g + 1) * N_CMP], tok[h, r, :, a:a + N_CMP],
                                                     cols[h, row + 8 * a:row + 8 * a + 8].unsqueeze(2).to_broadcast([HD, 8, N_CMP]),
                                                     ALU.add)
                last.then_inc(PROJ.free(name), 1)
            Y.make_low(nc, dve, 5, 6, 7, 8)

            cos2 = cos.unsqueeze(1).to_broadcast([P, 2, S])
            sin2 = sin.unsqueeze(1).to_broadcast([P, 2, S])
            for i in range(3):
                ps = PT.arrived(dve, f"rope{i}")
                part = nsaT[:, 2 * i:2 * i + 2, :]
                turn = mix_t[:, 0, :].rearrange("p (a b) -> p a b", a=2)
                vec.tensor_tensor(turn, ps[:, :].rearrange("p (a b) -> p a b", a=2), sin2, ALU.mult)\
                    .then_inc(PT.free(f"rope{i}"), 1)
                link(vec.tensor_tensor(part, part, cos2, ALU.mult))
                PT.taken(dve, f"rope{i}")
                vec.tensor_tensor(part, part, turn, ALU.add).then_inc(roped, 1)
                dve.wait_ge(roped, i + 1)

            Y.make_low(nc, dve, 9, 10)
            for i, name in enumerate(("hkT", "hvT")):
                ps = SC.arrived(dve, name)[:, 0:4 * N_CMP].rearrange("p (m n) -> p m n", m=2)
                dve.wait_ge(gelu_x2, i + 1)
                link(vec.tensor_scalar(gelu_t, gelu_t, 0.044715, 1.0, ALU.mult, ALU.add))
                vec.tensor_tensor(gelu_t, gelu_t, ps, ALU.mult).then_inc(gelu_in, 1)
                dve.wait_ge(gelu_exp, i + 1)
                sigmoid(gelu_e)
                vec.tensor_tensor(hid_c[:, i], gelu_e, ps, ALU.mult).then_inc(SC.free(name), 1)
            Y.make_low(nc, dve, 11, 12, 13)
            last_tok = CMP_LEN - 1
            ps = SC.arrived(dve, "rope_kc")
            vec.tensor_tensor(kc_sin, ps[:, 0:N_CMP], sin[:, last_tok:S:CMP_STRIDE], ALU.mult).then_inc(SC.free("rope_kc"), 1)
            link(vec.tensor_tensor(kcT, kcT, cos[:, last_tok:S:CMP_STRIDE], ALU.mult))
            SC.taken(dve, "rope_kc")
            vec.tensor_tensor(kcT, kcT, kc_sin, ALU.add).then_inc(roped, 1)
            PROJ.taken(dve, "vwg")
            sigmoid(g_nsa)
            nsa_gate = g_nsa.rearrange("p t (h k) -> p k h t", k=3)

            dve.wait_ge(la_log, 1)
            ps = SC.arrived(dve, "la")
            vec.tensor_scalar(gla_b[:, 0, :], ps[:, 0:S], cols[:, ROW_GLB:ROW_GLB + 1], 0.0, ALU.add, ALU.min)
            vec.tensor_scalar(gla_b[:, 1, :], ps[:, S:2 * S], cols[:, ROW_GLB + 1:ROW_GLB + 2], 0.0, ALU.add, ALU.min)\
                .then_inc(SC.free("la"), 1)
            SC.taken(dve, "la")
            Y.make_low(nc, dve, 14)
            link(vec.tensor_tensor(gla_t, gla_b, gla_t, ALU.subtract))
            for c in range(2):
                link(vec.tensor_tensor_scan(gla_b[:, c, :], K("ones"), gla_t[:, c, :], 0.0, ALU.mult, ALU.add))

            prepared = [0]

            def prepare(n):
                h, k = LEVELS[n], prepared[0]
                prepared[0] += 1
                b = gla_b.rearrange("p c s -> p (c s)").rearrange("p (n j) -> p n j", j=2 * h)
                d = lv_d[:, k % 2]
                vec.tensor_tensor(d.rearrange("p (n j) -> p n j", j=2 * h), b,
                                  b[:, :, h - 1:h].to_broadcast([P, 512 // (2 * h), 2 * h]), ALU.subtract).then_inc(lv_diff, 1)
                dve.wait_ge(lv_exp, k + 1)
                vec.tensor_tensor(lv_q[:, k % 2], glq.rearrange("p c s -> p (c s)"), d, ALU.mult)
                vec.tensor_tensor(lv_k[:, k % 2], glk.rearrange("p c s -> p (c s)"), d, ALU.mult).then_inc(lv_ready, 1)

            def merge(n):
                for par in range(2):
                    name = f"lv{n}_{par}"
                    ps = PT.arrived(dve, name)
                    if LEVELS[n] == P:
                        vec.tensor_copy(att[:, par, 2].rearrange("p c t -> p (c t)"), ps[:, 0:2 * P])\
                            .then_inc(PT.free(name), 1)
                    else:
                        vec.copy_predicated(att[:, par, 0:2].rearrange("p b c t -> p (b c) t"),
                                            level_mask[:, n - 1:n, :].to_broadcast([P, 4, P]),
                                            ps[:, :].rearrange("p (a t) -> p a t", a=4)).then_inc(PT.free(name), 1)
                PT.taken(dve, f"lv{n}_0", f"lv{n}_1")

            PROJ.taken(dve, "gq", "gk")
            def silu_gate(t):
                PROJ.taken(dve, f"gg{t}")
                sigmoid(gle[:, t, :])
                link(vec.tensor_tensor(gle[:, t, :], gle[:, t, :], glg[:, t, :], ALU.mult))

            prepare(0)
            Y.make_low(nc, dve, 15)
            prepare(2)
            for n in range(2):
                Y.make_low(nc, dve, 16 + n)
                merge(n)
            for n in range(3, len(LEVELS)):
                prepare(n)
                Y.make_low(nc, dve, 15 + n)
                merge(n - 1)
            Y.make_low(nc, dve, 24)
            merge(len(LEVELS) - 1)
            Y.make_low(nc, dve, 25)

            for t in range(TT):
                silu_gate(t)

            dve.wait_ge(small_in, 4 * 16)
            ps = PROJ.arrived(dve, "ff")
            vec.tensor_tensor(fox_t, ps[:, 0:TT * 8].rearrange("p (t h) -> p t h", t=TT),
                              fox_b.unsqueeze(1).to_broadcast([P, TT, 8]), ALU.add).then_inc(PROJ.free("ff"), 1)
            vec.tensor_tensor(hT, hT_low[:, :, :].bitcast(F32), hT_high[0][:, :, :].bitcast(F32), ALU.add).then_inc(hT_whole, 1)
            dve.wait_ge(fox_log, 1)
            vec.scalar_tensor_tensor(log_f, fox_t, 0.0, log_f, ALU.min, ALU.subtract).then_inc(fox_ready, 1)

            for t in range(TT):
                dve.wait_ge(gl_scale, t + 1)
                ps = OT.arrived(dve, f"go{t}")
                for h in range(GLA_H):
                    dv = slice(h * GLA_DV, (h + 1) * GLA_DV)
                    last = vec.scalar_tensor_tensor(gle[:, t, dv], ps[:, dv], gl_rstd[:, t, h:h + 1], gle[:, t, dv],
                                                    ALU.mult, ALU.mult)
                last.then_inc(OT.free(f"go{t}"), 1)

            bias = K("cmp_bias").rearrange("p (t n) -> p t n", t=TT).unsqueeze(1).to_broadcast([P, 4, TT, N_CMP])
            seen = K("cmp_seen").rearrange("p (t n) -> p t n", t=TT).unsqueeze(1).to_broadcast([P, 4, TT, N_CMP])
            for g in range(2):
                ps = SC.arrived(dve, f"cmp{g}")
                pc, st = p_cmp[:, g], stat_cmp[:, g]
                wide = st.unsqueeze(3).to_broadcast([P, 4, TT, N_CMP])
                vec.tensor_tensor(pc, ps[:, 0:4 * TT * N_CMP].rearrange("p (c t n) -> p c t n", c=4, t=TT), bias, ALU.add)\
                    .then_inc(SC.free(f"cmp{g}"), 1)
                SC.taken(dve, f"cmp{g}")
                link(vec.tensor_reduce(st, pc, axis=AX.X, op=ALU.max))
                vec.tensor_tensor(pc, pc, wide, ALU.subtract).then_inc(cmp_in, 1)
                dve.wait_ge(cmp_exp, g + 1)
                link(vec.tensor_tensor(pc, pc, seen, ALU.mult))
                link(vec.tensor_reduce(st, pc, axis=AX.X, op=ALU.add))
                link(vec.tensor_scalar_max(st, st, 1e-30))
                link(vec.reciprocal(st, st))
                link(vec.tensor_tensor(st, st, nsa_gate[:, 0, 4 * g:4 * g + 4, :], ALU.mult))
                vec.tensor_tensor(pc, pc, wide, ALU.mult).then_inc(cmp_ready, 1)

            for i in range(NJ):
                kind, c, par = jobs[i]
                if kind != "sb":
                    ps = SC.arrived(dve, f"s{i}")
                    vec.tensor_reduce(neg_max[:, i % 2, 0:1], ps[:, 0:P], axis=AX.X, op=ALU.max, negate=True)
                    vec.tensor_reduce(neg_max[:, i % 2, 1:2], ps[:, P:3 * P], axis=AX.X, op=ALU.max, negate=True)\
                        .then_inc(max_ready, 1)
                PROJ.taken(dve, f"g{i}")
                sigmoid(gates[:, i, :])
                if kind == "sb":
                    dve.wait_ge(sb_log, i - 23)
                    ps = SC.arrived(dve, f"s{i}")
                    vec.scalar_tensor_tensor(sb_p[:, i % 2], ps[:, 0:3 * P], 0.0, sb_u[:, i % 2], ALU.max, ALU.add)\
                        .then_inc(sb_soft, 1)
                    continue
                SC.taken(dve, f"s{i}")
                link(vec.reciprocal(total[:, i % 2], total[:, i % 2]))
                if kind != "fox":
                    branch_of = 1 if kind == "slc" else 2
                    link(vec.tensor_tensor(total[:, i % 2], total[:, i % 2], nsa_gate[:, branch_of, 4 * par + c, :], ALU.mult))
                vec.tensor_scalar(prob[:, i % 2, 0:P], prob[:, i % 2, 0:P], total[:, i % 2, 0:1], None, ALU.mult)
                vec.tensor_scalar(prob[:, i % 2, P:3 * P], prob[:, i % 2, P:3 * P], total[:, i % 2, 1:2], None, ALU.mult)\
                    .then_inc(prob_ready, 1)

            for n in range(4):
                for fc in range(KD // 2):
                    name = f"br{n}_{fc}"
                    ps = PROJ.arrived(dve, name)[:, :].rearrange("p (a b) -> p a b", a=2)
                    gate = gates[:, n * KD + 2 * fc:n * KD + 2 * fc + 2, :]
                    mixed = mixedT[:, 2 * fc:2 * fc + 2, :]
                    if n == 0:
                        vec.tensor_tensor(mixed, ps, gate, ALU.mult).then_inc(PROJ.free(name), 1)
                        continue
                    part = mix_t[:, fc % 2, :].rearrange("p (a b) -> p a b", a=2)
                    vec.tensor_tensor(part, ps, gate, ALU.mult).then_inc(PROJ.free(name), 1)
                    PROJ.taken(dve, name)
                    vec.tensor_tensor(mixed, mixed, part, ALU.add).then_inc(mixed_ready, 1)
                if n > 0:
                    dve.wait_ge(mixed_ready, 4 * n)
            X.make_low(nc, dve, 0, 1)
            dve.wait_ge(x_back, 16)
            for h in range(2):
                for t in range(TT):
                    ps = PROJ.arrived(dve, f"wo{h}{t}")
                    part = x[:, t, 512 * h:512 * h + 512]
                    vec.tensor_tensor(part, part, ps[:, :], ALU.add).then_inc(PROJ.free(f"wo{h}{t}"), 1)
            norm(2)

            low_bits(hT_high[1])
            X.make_low(nc, dve, 2, 3)
            for i in range(FFK // 2):
                dve.wait_ge(hidden_squared, i + 1)
                part = slice(2 * i, 2 * i + 2)
                vec.tensor_tensor(hidden_low[:, part, :], hidden[:, part, :], hidden_high[:, part, :].bitcast(F32), ALU.subtract)\
                    .then_inc(hidden_ready, 1)
                X.make_low(nc, dve, i + 4)
            X.make_low(nc, dve, *range(FFK // 2 + 4, FFK))
            for t in range(TT):
                for h in range(2):
                    name = f"down{2 * t + h}"
                    bank = (SC, OT)[t]
                    ps = bank.arrived(dve, name)
                    part = x[:, t, 512 * h:512 * h + 512]
                    vec.tensor_tensor(part, part, ps[:, :], ALU.add).then_inc(bank.free(name), 1)


def prologue(nc, T, dram, sem, chip):
    x, consts, masks, cos, sin = (chip[n] for n in ("x", "consts", "masks", "cos", "sin"))
    work = Carver(chip["work"])
    pos, rows = work.take(S), work.take(P)
    cols, silu_c = chip["cols2"], chip["silu_c"]
    silu_t = work.take(2, KD)
    ident = consts[:, T["f32"]["ident"][0]:sum(T["f32"]["ident"])]
    angle, turns, part = work.take(S), work.take(S), work.take(S)
    tables_in, x_in = sem("tables_in"), sem("x_in")
    sin_arg, cos_arg = sem("sin_arg"), sem("cos_arg")
    sin_cos = sem("sin_cos")
    rows_in = sem("rows2_in")
    cols_full = sem("cols2_full")
    silu_exp = sem("silu_exp")
    pro_self, silu_done = sem("pro_self"), sem("silu_done")

    with nc.Block() as block:

        @block.sync
        def _(sp):
            sp.dma_start(pos.bitcast(I32), dram["positions"].partition_broadcast(P).rearrange("p b s -> p (b s)"))\
                .then_inc(tables_in, 16)
            sp.dma_start(consts[:, :], dram["f32_tables"]).then_inc(tables_in, 16)
            sp.dma_start(masks[:, :], dram["bf16_tables"]).then_inc(tables_in, 16)
            sp.dma_start(x, dram["x"].rearrange("b (t p) d -> p (b t) d", p=P)).then_inc(x_in, 16)
            sp.wait_ge(x_in, 16)

        @block.tensor
        def _(pe):
            pe.wait_ge(tables_in, 3 * 16)
            pe.wait_ge(rows_in, 9 * 16)
            nc.tensor.transpose(chip["psum"][0][:, 0:N_ROWS2], rows[0:N_ROWS2, :], ident[0:N_ROWS2, 0:N_ROWS2])\
                .then_inc(cols_full, 1)

        @block.vector
        def _(dve):
            link = Chain(dve, pro_self)
            vec = nc.vector
            link(vec.memset(silu_c, 0.0))
            inv = consts[:, T["f32"]["inv_freq"][0]:T["f32"]["inv_freq"][0] + 1]
            dve.wait_ge(tables_in, 3 * 16)
            link(vec.tensor_copy(angle, pos.bitcast(I32)))
            link(vec.tensor_scalar(angle, angle, inv, None, ALU.mult))
            link(vec.tensor_scalar(turns, angle, float(1 / (2 * np.pi)), None, ALU.mult))
            link(vec.tensor_scalar(turns, turns, MAGIC, None, ALU.add))
            link(vec.tensor_scalar(turns, turns, -MAGIC, None, ALU.add))
            for c in TWO_PI_PARTS:
                link(vec.scalar_tensor_tensor(angle, turns, -c, angle, ALU.mult, ALU.add))
            limit = 3.1415925
            vec.tensor_scalar(part, angle, limit, -limit, ALU.min, ALU.max).then_inc(sin_arg, 1)
            link(vec.tensor_scalar(angle, angle, float(np.pi / 2), None, ALU.add))
            link(vec.tensor_scalar(turns, angle, float(np.pi), float(-2 * np.pi), ALU.is_gt, ALU.mult))
            link(vec.tensor_tensor(angle, angle, turns, ALU.add))
            vec.tensor_scalar(angle, angle, limit, -limit, ALU.min, ALU.max).then_inc(cos_arg, 1)
            dve.wait_ge(silu_exp, 1)
            link(vec.tensor_scalar_add(silu_t, silu_t, 1.0))
            link(vec.reciprocal(silu_t, silu_t))
            vec.tensor_tensor(silu_c[:, :, 0:2].rearrange("p k s -> p s k"), silu_t,
                              cols[:, ROW_C:N_ROWS2].rearrange("p (s k) -> p s k", s=2), ALU.mult)

        @block.scalar
        def _(act):
            def row_load(at, n, src, c0=0, width=P):
                act.dma_start(rows[at:at + n, c0:c0 + width], src).then_inc(rows_in, 16)

            row_load(ROW_ADA, 2 * MODC, dram["b_ada_2"].rearrange("l (r p) -> (l r) p", p=P))
            for half in range(2):
                row_load(ROW_QN, 1, dram["gqa_q_norm_2"], half * HD, HD)
                row_load(ROW_KN, 1, dram["gqa_k_norm_2"], half * HD, HD)
            row_load(ROW_MQN, 3, dram["mla_q_norm_2"].rearrange("l (r p) -> (l r) p", p=P))
            row_load(ROW_MKN, 2, dram["mla_kv_norm_2"].rearrange("l (r p) -> (l r) p", p=P))
            c_rows = dram["c_2"].rearrange("b (r p) -> (b r) p", p=P)
            row_load(ROW_C, KD, c_rows)
            act.dma_start(rows[ROW_C + KD:N_ROWS2, :], dram["c_ctx_2"].rearrange("(r p) -> r p", p=P)).then_inc(rows_in, 16)
            act.wait_ge(cols_full, 1)
            ps = chip["psum"][0]
            nc.scalar.activation(cols, ps[:, 0:N_ROWS2], ACT.Copy)
            nc.scalar.activation(silu_t, ps[:, ROW_C:N_ROWS2].rearrange("p (s k) -> p s k", s=2), ACT.Exp, scale=-1.0)\
                .then_inc(silu_exp, 1)
            act.wait_ge(sin_arg, 1)
            nc.scalar.activation(sin, part, ACT.Sin)
            act.wait_ge(cos_arg, 1)
            nc.scalar.activation(cos, angle, ACT.Sin)


def second_block(nc, T, dram, out, sem, chip):
    x, consts, mod, cols2 = chip["x"], chip["consts"], chip["mod"], chip["cols2"]
    work = Carver(chip["work"])

    xc = work.take(TT, D)
    hT = work.take(KD, 2 * S)
    gate_rows = work.take(2, D)
    ln_rows = work.take(2, D)
    grid = work.take(P + 2 * S)
    z = work.take(2, 512)
    small = Carver(chip["cos"])
    ln_stats, ln_mv, ln_rs = small.take(4, 2, 6), small.take(4, 2), small.take(4)
    neg_max, total = small.take(8, 2), small.take(8, 2)
    nf_stat = small.take(TT)
    late = work.at
    gate_src = z.rearrange("p a b -> p (a b)").rearrange("p (k j) -> p k j", k=KD)
    grid_swap, grid_cos, grid_sin = grid[:, 0:P], grid[:, P:P + S], grid[:, P + S:P + 2 * S]
    g = Carver(chip["work"], late)
    g_qT = g.take(KD, 2 * S)
    g_kT = g.take(KV_HEADS, 2 * S)
    g_k = g.take(2, 2 * S)
    g_v = g.take(4, KV_HEADS * HD)
    g_turn = g.take(4, 6, S)
    g_yT = g.take(KD, 2 * S)
    before = Carver(g_turn.rearrange("p a b c -> p (a b c)"))
    g_sq, g_rs, g_rot = before.take(2, 512), before.take(2, 512), before.take(S)
    g_prob = hT.rearrange("p k s -> p (k s)").rearrange("p (a b) -> p a b", a=8)
    g_turn = [g_turn[:, n] for n in range(4)]
    nf_row, nf_junk = (g_yT.rearrange("p a b -> p (a b)")[:, n * D:(n + 1) * D] for n in range(2))
    m = Carver(chip["work"], late)
    m_kT = m.take(HEADS, 2 * S)
    m_qT = m.take(HEADS, S)
    m_v = m.take(4, HEADS * HD)
    m_cq, m_ckv = m.take(3, S), m.take(2, 2 * S)
    early, spare = Carver(hT.rearrange("p a b -> p (a b)")), Carver(chip["work"], m.at - 7 * S)
    m_prob = early.take(6, 512)
    m_turn = [early.take(4, S), z.rearrange("p a b -> p (a b)").rearrange("p (a b) -> p a b", a=4),
              spare.take(4, S), spare.take(4, S)]
    m_yT = xc.rearrange("p a b -> p (a b)").rearrange("p (c s) -> p c s", c=KD)
    flat_xc = xc.rearrange("p a b -> p (a b)")
    m_sqkv = flat_xc[:, 0:4 * S].rearrange("p (c s) -> p c s", c=2)
    m_sqq = m_qT[:, 0:3, :]
    m_rskv, m_rsq = z[:, 0], z[:, 1, 0:S]
    m_kpe, m_rot = gate_rows[:, 1, 0:512], gate_rows[:, 1, 512:1024]
    rounded = chip["rounded"]
    half_high = [rounded(f"half_high{n}", late + n * SPLIT_HALF, SPLIT_HALF) for n in range(3)]
    at = late + 3 * SPLIT_HALF
    hT_low, hT_high = rounded("hT_low2", TT * D, KD, 2 * S), rounded("hT_high2", at, KD, 2 * S)
    at += KD * 2 * S
    hidden = Carver(chip["work"], at).take(KD, 2 * S)
    hidden_low, hidden_high = rounded("hidden_low2", at, KD, 2 * S), rounded("hidden_high2", at + KD * 2 * S, KD, 2 * S)

    tok = [x[:, 0, :], x[:, 1, :], xc[:, 0, :], xc[:, 1, :]]
    K = lambda name: consts[:, T["f32"][name][0]:sum(T["f32"][name])]
    ident, eps = K("ident"), K("eps")

    def mod_col(i, part, k, s):
        at = ((i * MOD_PARTS + part) * KD + k) * 2 + s
        return mod[:, at:at + 1]

    NT = [4, 2]
    UNITS = [3, 2]
    LAG = [3, 2]
    PAIRS = HEADS // 2
    NORMED = 10
    XT_ORDER = [(0, 1, 2, 3), (0, 1, 2, 3)]
    UP_PER = [1, 2]
    GM_AT = [2, 5]
    QUARTERS = FFK // KD

    def gate_fills(i, kind, s):
        return [f"{i}{kind}{s}{h}" for h in range(2)]

    proj, score, turned, outs = [], [], [], []
    for i in range(DEPTH):
        streams = NT[i] // TT
        if i == 0:
            proj += [f"{i}xT{t}{h}" for t in XT_ORDER[i] for h in range(2)]
            proj += ["0v0"] + gate_fills(0, "ga", 0) + ["0v1"] + gate_fills(0, "ga", 1)
            proj += [f"0a{n}" for n in range(NORMED)]
            score += [f"0ms{n}" for n in range(NORMED)]
            turned += [f"0rt{n}" for n in range(NORMED)]
        else:
            proj += [f"1xT{t}{h}" for t in range(TT) for h in range(2)] + ["1cq0"] + gate_fills(1, "ga", 0) + ["1cq1"]
            proj += [f"1xT{t}{h}" for t in range(TT, 2 * TT) for h in range(2)] + ["1ckv0", "1ckv1", "1kpe"]
            proj += [f"1kn{j}" for j in range(8)] + [f"1v{j}" for j in range(8)] + [f"1qf{j}" for j in range(8)]
            score += ["1mskv", "1msq"]
            turned += ["1rtk"] + [f"1rt{j}" for j in range(8)]
        units = [(2 * c, u) for c in range(PAIRS) for u in range(UNITS[i])]
        score += [f"{i}s{h}_{u}" for h, u in units]
        proj += [f"{i}s{h + 1}_{u}" for h, u in units]
        turned += [f"{i}t{h + e}_{u}" for h, u in units for e in range(2)]
        outs += [f"{i}o{c}" for c in range(PAIRS)] + [f"{i}wo{t}{h}" for t in range(NT[i]) for h in range(2)]
        proj += [f"{i}hT{t}{h}" for t in range(NT[i]) for h in range(2)]
        for q in range(QUARTERS):
            for n in range(KD // UP_PER[i]):
                proj.append(f"{i}up{q}_{n}")
                for s in range(streams):
                    if q == 0 and n == GM_AT[s]:
                        proj += gate_fills(i, "gm", s)
            score += [f"{i}down{q}0{t}" for t in range(2)]
            outs += [f"{i}down{q}0{t}" for t in range(2, NT[i])]
            turned += [f"{i}down{q}1{t}" for t in range(2)]
            proj += [f"{i}down{q}1{t}" for t in range(2, NT[i])]
    PROJ = Banks(sem, "proj2", chip["psum"][0:2], proj)
    SC = Banks(sem, "score2", chip["psum"][2:4], score)
    PT = Banks(sem, "turn2", chip["psum"][4:6], turned)
    OT = Banks(sem, "out2", chip["psum"][6:8], outs)

    SCORE = (SC, PROJ)

    def down_banks(h, t):
        return ((SC, OT), (PT, PROJ))[h][t // 2]

    whole = (slice(None), slice(None), slice(None))
    down_used = sem("down_used2")

    def chunked(a):
        return a.rearrange("(k p) n -> p k n", p=P)

    def done(bank, name):
        return bank.full, bank.order[name] + 1

    def up_done(i, q, j, b):
        return done(PROJ, f"{i}up{q}_{(4 * j + 2 * b + 1) // UP_PER[i]}")

    halves, freed = [], []
    w_qkv, w_in = chunked(dram["gqa_w_qkv_2"][0]), chunked(dram["mla_w_in_2"][0])
    w_uq = chunked(dram["mla_w_uq_2"][0])
    w_ukv = dram["mla_w_ukv_2"][0].rearrange("(k p) (h e d) -> k e p h d", p=P, e=2, d=HD)
    qw, kvw = HEADS * HD, 2 * KV_HEADS * HD
    uq_half = HEADS * MLA_QK // 2
    tiles = [("0kv", KD, kvw, [(whole, w_qkv[:, :, qw:qw + kvw])], done(PROJ, "0a1"))]
    tiles += [(f"0q{j}", KD, 512, [(whole, w_qkv[:, :, 512 * j:512 * j + 512])], done(PROJ, f"0a{4 * j + 5}"))
              for j in range(2)]
    for i in range(DEPTH):
        if i == 1:
            tiles += [("1cq", KD, Q_RANK, [(whole, w_in[:, :, 0:Q_RANK])], done(PROJ, "1cq1")),
                      ("1ckv", KD, KV_RANK + PE_DIM, [(whole, w_in[:, :, Q_RANK:])], done(PROJ, "1kpe")),
                      ("1ukv", 4, HEADS * HD, [((slice(None), 2 * e + k, slice(None)), w_ukv[k, e])
                                               for e in range(2) for k in range(2)], done(PROJ, "1v7"))]
            tiles += [(f"1uq{j}", 3, uq_half, [(whole, w_uq[:, :, uq_half * j:uq_half * (j + 1)])],
                       done(PROJ, f"1qf{4 * j + 3}")) for j in range(2)]
        w_o = chunked(dram[("gqa_w_o_2", "mla_w_o_2")[i]][0])
        w1, w2 = chunked(dram["mlp_w1_2"][i]), chunked(dram["mlp_w2_2"][i])
        last = NT[i] - 1
        tiles += [(f"{i}wo{h}", KD, 512, [(whole, w_o[:, :, 512 * h:512 * h + 512])], done(OT, f"{i}wo{last}{h}"))
                  for h in range(2)]
        for q in range(QUARTERS):
            for j in range(2):
                at = (2 * q + j) * 512
                tiles.append((f"{i}up{q}{j}", KD, 512, [(whole, w1[:, :, at:at + 512])], up_done(i, q, j, 1)))
                halves += [(f"{i}up{q}{j}", b, "n", 2 * P * b, 2 * P) for b in range(2)]
                freed += [up_done(i, q, j, b) for b in range(2)]
            for h in range(2):
                tiles.append((f"{i}down{q}{h}", KD, 512, [(whole, w2[:, KD * q:KD * q + KD, 512 * h:512 * h + 512])],
                              done(down_banks(h, last), f"{i}down{q}{h}{last}")))
                halves += [(f"{i}down{q}{h}", b, "k", 4 * b, 4) for b in range(2)]
                freed += [(down_used, 8 * i + 2 * q + h + 1), done(down_banks(h, last), f"{i}down{q}{h}{last}")]
    W = Weights(sem, "w2", chip["ring"], [n % N_SLOTS for n in range(len(tiles))], tiles)
    X = Split(sem, "mlp", W, chip["ring_low"], half_high, halves, freed)

    ctx_in, gain_in = sem("ctx_in"), sem("gain_in")
    first_in = sem("first_in")
    grid_in = sem("grid_in")
    ln_in = sem("ln_in")
    out_in = sem("out_done")
    nf_scale = sem("nf_scale")
    x_first = sem("x_first")
    mod_ready = sem("mod_ready")
    gate_wide = sem("gate_wide")
    rs_ready = sem("rs_ready")
    normed = sem("normed")
    roped = sem("roped2")
    k_copied = sem("k_copied")
    max_ready = sem("max_ready2")
    prob_ready = sem("prob_ready2")
    var_ready = sem("var_ready")
    ln_scale = sem("ln_scale")
    x_ready = sem("x_ready")
    hT_cut = sem("hT_cut2")
    hidden_squared = sem("hidden_squared2")
    hidden_ready = sem("hidden_ready2")
    kpe_ready = sem("kpe_ready")
    kpe_zero = sem("kpe_zero")
    act_self, dve_self = sem("act_self2"), sem("dve_self2")

    ln_order = [(i, j, t) for i in range(DEPTH) for j in range(2) for t in range(NT[i])]
    ln_count = {key: n + 1 for n, key in enumerate(ln_order)}
    gate_order = [(i, kind, s) for i in range(DEPTH) for kind in ("ga", "gm") for s in range(NT[i] // TT)]
    gate_count = {key: n + 1 for n, key in enumerate(gate_order)}
    unit_base = [0, HEADS * UNITS[0]]
    up_base = [0, FFK // UP_PER[0]]
    cut_base = [0, NT[0]]

    def unit(i, h, u):
        return unit_base[i] + (h // 2 * UNITS[i] + u) * 2 + h % 2

    def prob_slot(i, h, u):
        return (unit(i, h, u) - unit_base[i]) % (2 * (LAG[i] + 1))

    def buffers(i):
        return ((g_prob, g_turn, g_yT, 2 * S), (m_prob, m_turn, m_yT, S))[i]

    def x_arrived(eng, i, t):
        if i == 1:
            eng.wait_ge(x_ready, ln_count[0, 1, t])
        elif t < TT:
            eng.wait_ge(x_first, t + 1)
        else:
            eng.wait_ge(ctx_in, 16)

    with nc.Block() as block:

        @block.sync
        def _(sp):
            sp.dma_start(xc, dram["ctx_2"].rearrange("b (t p) d -> p (b t) d", p=P)).then_inc(ctx_in, 16)
            W.load(sp, 0, 1)
            sp.dma_start(grid, dram["grid_gqa"]).then_inc(first_in, 16)
            for n, name in enumerate(("ln_g_2", "ln_b_2")):
                sp.dma_start(ln_rows[:, n, :], dram[name][0, 0].partition_broadcast(P)).then_inc(first_in, 16)
            W.load(sp, 1)
            for t in range(TT):
                sp.wait_ge(x_ready, ln_count[1, 1, t])
                sp.dma_start(out.rearrange("b (t p) d -> p (b t) d", p=P)[:, t, :], x[:, t, :]).then_inc(out_in, 16)
            sp.wait_ge(out_in, TT * 16)

        @block.tensor
        def _(pe):
            def mm(o, lhsT, rhs, start, stop):
                return nc.tensor.matmul(o, lhsT, rhs, start=start, stop=stop)

            def turn(o, src):
                return nc.tensor.transpose(o, src, ident)

            def turn_tile(names, t):
                for h, name in enumerate(names):
                    ps = PROJ.claim(pe, name)
                    for k in range(4):
                        last = turn(ps[:, k * P:k * P + P], tok[t][:, (4 * h + k) * P:(4 * h + k + 1) * P])
                    last.then_inc(PROJ.full, 1)

            def turn_tiles(i, which):
                for t in which:
                    x_arrived(pe, i, t)
                    turn_tile([f"{i}xT{t}{h}" for h in range(2)], t)
                PROJ.taken(pe, *[f"{i}xT{t}{h}" for t in which for h in range(2)])

            def turn_gate(i, kind, s):
                pe.wait_ge(gate_wide, gate_count[i, kind, s])
                for h, name in enumerate(gate_fills(i, kind, s)):
                    ps = PROJ.claim(pe, name)
                    for k in range(4):
                        last = turn(ps[:, k * P:k * P + P], gate_src[:, 4 * h + k, :])
                    last.then_inc(PROJ.full, 1)

            def gemm_T(o, w, cols, n=2 * S, chunks=KD, src=None):
                src = hT if src is None else src
                for k in range(chunks):
                    last = mm(o, w[:, k, cols], src[:, k, 0:n], k == 0, k == chunks - 1)
                return last

            def gqa_project():
                w = W.arrived(pe, "0kv")
                pe.wait_ge(first_in, 3 * 16)
                kw = KV_HEADS * HD
                for j in range(2):
                    ps = PROJ.claim(pe, f"0v{j}")
                    for b in range(2):
                        for k in range(KD):
                            t = 2 * j + b
                            last = mm(ps[:, b * kw:(b + 1) * kw], hT[:, k, t * P:t * P + P], w[:, k, kw:2 * kw],
                                      k == 0, k == KD - 1)
                    last.then_inc(PROJ.full, 1)
                    turn_gate(0, "ga", j)
                for n in range(NORMED + 2):
                    if n < NORMED:
                        if n >= 2 and n % 4 == 2:
                            w = W.arrived(pe, f"0q{n // 4}")
                        c = n if n < 2 else (n - 2) % 4
                        gemm_T(PROJ.claim(pe, f"0a{n}")[:, :], w, slice(c * P, c * P + P)).then_inc(PROJ.full, 1)
                    if 1 <= n <= NORMED:
                        PROJ.taken(pe, f"0a{n - 1}")
                        mm(SC.claim(pe, f"0ms{n - 1}")[:, :], K("head_mean"), g_sq[:, (n - 1) % 2], True, True)\
                            .then_inc(SC.full, 1)
                    if n >= 2:
                        pe.wait_ge(normed, n - 1)
                        raw = g_k[:, n - 2] if n < 4 else g_qT[:, n - 4]
                        mm(PT.claim(pe, f"0rt{n - 2}")[:, 0:S], grid_swap, raw[:, 0:S], True, True).then_inc(PT.full, 1)

            def mla_project():
                w = W.arrived(pe, "1cq")
                for j in range(2):
                    ps = PROJ.claim(pe, f"1cq{j}")
                    for b in range(2 - j):
                        c = 2 * j + b
                        last = gemm_T(ps[:, b * S:b * S + S], w, slice(c * P, c * P + P), S)
                    last.then_inc(PROJ.full, 1)
                    if j == 0:
                        turn_gate(1, "ga", 0)
                turn_tiles(1, XT_ORDER[1][TT:])
                w = W.arrived(pe, "1ckv")
                for j in range(2):
                    gemm_T(PROJ.claim(pe, f"1ckv{j}")[:, :], w, slice(j * P, j * P + P)).then_inc(PROJ.full, 1)
                gemm_T(PROJ.claim(pe, "1kpe")[HD:MLA_QK, :], w, slice(KV_RANK, KV_RANK + PE_DIM)).then_inc(PROJ.full, 1)
                PROJ.taken(pe, "1ckv0", "1ckv1")
                ps = SC.claim(pe, "1mskv")
                for c in range(2):
                    last = mm(ps[:, :], K("ones")[:, 0:P], m_sqkv[:, c, :], c == 0, c == 1)
                last.then_inc(SC.full, 1)
                PROJ.taken(pe, "1cq0", "1cq1")
                ps = SC.claim(pe, "1msq")
                for c in range(3):
                    last = mm(ps[:, 0:S], K("ones")[:, 0:P], m_sqq[:, c, :], c == 0, c == 2)
                last.then_inc(SC.full, 1)
                PROJ.taken(pe, "1kpe")
                pe.wait_ge(kpe_zero, 1)
                pe.wait_ge(grid_in, 16)
                mm(PT.claim(pe, "1rtk")[0:MLA_QK, 0:S], grid_swap[0:MLA_QK, 0:MLA_QK], m_kpe[0:MLA_QK, 0:S], True, True)\
                    .then_inc(PT.full, 1)
                w = W.arrived(pe, "1ukv")
                pe.wait_ge(normed, NORMED + 1)
                for j in range(8):
                    gemm_T(PROJ.claim(pe, f"1kn{j}")[:, :], w[:, 0:2], slice(j * P, j * P + P), chunks=2, src=m_ckv)\
                        .then_inc(PROJ.full, 1)
                for j in range(8):
                    ps = PROJ.claim(pe, f"1v{j}")
                    for c in range(2):
                        last = mm(ps[:, :], m_ckv[:, c, (j // 2) * P:(j // 2 + 1) * P],
                                  w[:, 2 + c, 512 * (j % 2):512 * (j % 2) + 512], c == 0, c == 1)
                    last.then_inc(PROJ.full, 1)
                pe.wait_ge(normed, NORMED + 2)
                for j in range(9):
                    if j < 8:
                        if j % 4 == 0:
                            w = W.arrived(pe, f"1uq{j // 4}")
                        ps = PROJ.claim(pe, f"1qf{j}")
                        for b in range(2):
                            at = (2 * j + b) % 8 * MLA_QK
                            last = gemm_T(ps[0:MLA_QK, b * S:b * S + S], w, slice(at, at + MLA_QK), S, 3, m_cq)
                        last.then_inc(PROJ.full, 1)
                    if j >= 1:
                        PROJ.taken(pe, f"1qf{j - 1}")
                        mm(PT.claim(pe, f"1rt{j - 1}")[0:MLA_QK, :], grid_swap[0:MLA_QK, 0:MLA_QK],
                           m_qT[0:MLA_QK, 2 * j - 2:2 * j, :].rearrange("p a b -> p (a b)"), True, True).then_inc(PT.full, 1)

            def operands(i, h):
                if i == 0:
                    rows, kv = slice(h % 2 * HD, h % 2 * HD + HD), h // (HEADS // KV_HEADS)
                    return g_qT[rows, h // 2, :], g_kT[rows, kv, :], g_v[:, :, kv * HD:kv * HD + HD]
                return m_qT[0:MLA_QK, h, :], m_kT[0:MLA_QK, h, :], m_v[:, :, h * HD:h * HD + HD]

            def attention(i):
                prob, turned_p = buffers(i)[0:2]
                U = UNITS[i]
                for n in range(PAIRS * U + LAG[i] + 1):
                    if n < PAIRS * U:
                        c, u = n // U, n % U
                        if u == 0:
                            pe.wait_ge(roped, (3 if i == 0 else NORMED + 1) + c)
                        names = [f"{i}s{2 * c + e}_{u}" for e in range(2)]
                        ps = [SCORE[e].claim(pe, names[e]) for e in range(2)]
                        for t in range(1 if u < 2 else TT):
                            for e in range(2):
                                q, k, _ = operands(i, 2 * c + e)
                                if u < 2:
                                    last = mm(ps[e][:, :], q[:, u * P:u * P + P], k, True, True)
                                else:
                                    last = mm(ps[e][:, t * S:t * S + S], q[:, S + t * P:S + t * P + P], k[:, S:2 * S], True, True)
                                if u < 2 or t == TT - 1:
                                    last.then_inc(SCORE[e].full, 1)
                    if LAG[i] <= n < PAIRS * U + LAG[i]:
                        c, u = (n - LAG[i]) // U, (n - LAG[i]) % U
                        for h in (2 * c, 2 * c + 1):
                            src = prob[:, prob_slot(i, h, u)]
                            pe.wait_ge(prob_ready, unit(i, h, u) + 1)
                            ps = PT.claim(pe, f"{i}t{h}_{u}")
                            for b in range(4):
                                at = b if u < 2 else b % 2 * 2 + b // 2
                                last = turn(ps[:, b * P:b * P + P], src[:, at * P:at * P + P])
                            last.then_inc(PT.full, 1)
                    if n > LAG[i] and (n - LAG[i]) % U == 0:
                        c = (n - LAG[i]) // U - 1
                        PT.taken(pe, *[f"{i}t{h}_{u}" for u in range(U) for h in (2 * c, 2 * c + 1)])
                        ps = OT.claim(pe, f"{i}o{c}")
                        for b in range(4 if U == 2 else 6):
                            cols = slice(0, S) if b < 4 else slice(S, 2 * S)
                            for e in range(2):
                                v, keys = operands(i, 2 * c + e)[2], turned_p[2 * (c % 2) + e]
                                last = mm(ps[e * HD:e * HD + HD, cols], v[:, b if b < 4 else b - 2, :], keys[:, b, :],
                                          b in (0, 4), b in (3, 5))
                        last.then_inc(OT.full, 1)

            for i in range(DEPTH):
                yT, n_tok = buffers(i)[2:]
                turn_tiles(i, XT_ORDER[i] if i == 0 else XT_ORDER[i][0:TT])
                if i == 0:
                    gqa_project()
                    pe.wait_ge(k_copied, 8)
                else:
                    mla_project()
                    pe.wait_ge(k_copied, 12)
                attention(i)

                OT.taken(pe, f"{i}o{PAIRS - 2}", f"{i}o{PAIRS - 1}")
                w = [W.arrived(pe, f"{i}wo{h}") for h in range(2)]
                for t in range(NT[i] + 1):
                    if t < NT[i]:
                        for h in range(2):
                            ps = OT.claim(pe, f"{i}wo{t}{h}")
                            for c in range(KD):
                                last = mm(ps[:, :], yT[:, c, t * P:t * P + P], w[h][:, c, :], c == 0, c == KD - 1)
                            last.then_inc(OT.full, 1)
                    if t >= 1:
                        pe.wait_ge(x_ready, ln_count[i, 0, t - 1])
                        turn_tile([f"{i}hT{t - 1}{h}" for h in range(2)], t - 1)

                pe.wait_ge(hT_cut, cut_base[i] + NT[i])
                per = UP_PER[i]
                src = [part[:, :, 0:n_tok] for part in (hT_high, hT_low)]
                for q in range(QUARTERS):
                    for n in range(KD // per):
                        ps = PROJ.claim(pe, f"{i}up{q}_{n}")
                        for b in range(per):
                            c = n * per + b
                            w = X.arrived(pe, f"{i}up{q}{c // 4}", c // 2 % 2)
                            cols = slice(c % 2 * P, c % 2 * P + P)
                            for k in range(KD):
                                last = product(nc, ps[:, b * n_tok:(b + 1) * n_tok], [part[:, k, cols] for part in w],
                                               [part[:, k, :] for part in src], k == 0, k == KD - 1)
                        last.then_inc(PROJ.full, 1)
                        for s in range(NT[i] // TT):
                            if q == 0 and n == GM_AT[s]:
                                turn_gate(i, "gm", s)
                    for h in range(2):
                        order = [(b, t) for b in range(2) for t in range(NT[i])]
                        if q + 1 == QUARTERS and h == 1:
                            order.sort(key=lambda step: step[1])
                        for b, t in order:
                            w = X.arrived(pe, f"{i}down{q}{h}", b)
                            pe.wait_ge(hidden_ready, up_base[i] + (q * KD + 4 * b + 3) // per + 1)
                            banks, name = down_banks(h, t), f"{i}down{q}{h}{t}"
                            ps = banks.claim(pe, name) if b == 0 else banks.bank(name)
                            for k in range(4):
                                last = product(nc, ps[:, :], [part[:, 4 * b + k, t * P:t * P + P] for part in (hidden_high, hidden_low)],
                                               [part[:, k, :] for part in w], b + k == 0, 4 * b + k == KD - 1)
                            if b == 1:
                                last.then_inc(banks.full, 1)
                            elif t == NT[i] - 1:
                                last.then_inc(down_used, 1)

        @block.scalar
        def _(act):
            f = nc.scalar.activation
            link = Chain(act, act_self)

            def copy(o, src, **kw):
                return f(o, src, ACT.Copy, **kw)

            def modulate(i, name, t, part, high=None):
                ps = PROJ.arrived(act, name)
                for k in range(4):
                    if high is not None:
                        f(high[:, k, t * P:t * P + P], ps[:, k * P:k * P + P], ACT.Identity,
                          scale=mod_col(i, part + 1, k, t // TT), bias=mod_col(i, part, k, t // TT))
                    last = f(hT[:, k, t * P:t * P + P], ps[:, k * P:k * P + P], ACT.Identity,
                             scale=mod_col(i, part + 1, k, t // TT), bias=mod_col(i, part, k, t // TT))
                last.then_inc(PROJ.free(name), 1)

            def take_gate(i, kind, s):
                for h, name in enumerate(gate_fills(i, kind, s)):
                    ps = PROJ.arrived(act, name)
                    copy(gate_rows[:, s, 512 * h:512 * h + 512], ps[:, :]).then_inc(PROJ.free(name), 1)

            def scale_of(banks, name, part, o, mean):
                ps = banks.arrived(act, name)
                f(o, ps[:, 0:o.shape[1]], ACT.Ln, scale=mean, bias=eps).then_inc(banks.free(name), 1)
                banks.taken(act, name)
                f(o, o, ACT.Exp, scale=-0.5).then_inc(rs_ready, 1)

            def gqa_project():
                for j in range(2):
                    ps = PROJ.arrived(act, f"0v{j}")
                    copy(g_v[:, 2 * j:2 * j + 2, :].rearrange("p a b -> p (a b)"), ps[:, :]).then_inc(PROJ.free(f"0v{j}"), 1)
                    take_gate(0, "ga", j)
                for n in range(NORMED + 1):
                    if n < NORMED:
                        ps = PROJ.arrived(act, f"0a{n}")
                        copy(g_k[:, n] if n < 2 else g_qT[:, n - 2], ps[:, :])
                        f(g_sq[:, n % 2], ps[:, :], ACT.Square).then_inc(PROJ.free(f"0a{n}"), 1)
                    if n >= 1:
                        if n >= 3:
                            act.wait_ge(normed, n - 2)
                        scale_of(SC, f"0ms{n - 1}", None, g_rs[:, (n - 1) % 2], 1.0)

            def mla_project():
                for j in range(2):
                    ps = PROJ.arrived(act, f"1cq{j}")
                    n = (2 - j) * S
                    copy(m_cq[:, 2 * j:2 * j + 2 - j, :].rearrange("p a b -> p (a b)"), ps[:, 0:n])
                    f(m_sqq[:, 2 * j:2 * j + 2 - j, :].rearrange("p a b -> p (a b)"), ps[:, 0:n], ACT.Square)\
                        .then_inc(PROJ.free(f"1cq{j}"), 1)
                    if j == 0:
                        take_gate(1, "ga", 0)
                for t in XT_ORDER[1][TT:]:
                    modulate(1, f"1xT{t}0", t, 0)
                for j in range(2):
                    ps = PROJ.arrived(act, f"1ckv{j}")
                    copy(m_ckv[:, j, :], ps[:, :])
                    f(m_sqkv[:, j, :], ps[:, :], ACT.Square).then_inc(PROJ.free(f"1ckv{j}"), 1)
                ps = PROJ.arrived(act, "1kpe")
                copy(m_kpe[HD:MLA_QK, :], ps[HD:MLA_QK, :]).then_inc(PROJ.free("1kpe"), 1)
                scale_of(SC, "1mskv", None, m_rskv, 1.0 / KV_RANK)
                scale_of(SC, "1msq", None, m_rsq, 1.0 / Q_RANK)
                for j in range(0, 8, 2):
                    ps = PROJ.arrived(act, f"1kn{j}")
                    copy(m_kT[0:HD, 2 * j, :], ps[0:HD, :])
                    copy(m_kT[0:HD, 2 * j + 1, :], ps[HD:P, :]).then_inc(PROJ.free(f"1kn{j}"), 1)
                for j in range(0, 8, 2):
                    ps = PROJ.arrived(act, f"1v{j}")
                    copy(m_v[:, j // 2, 0:512], ps[:, :]).then_inc(PROJ.free(f"1v{j}"), 1)
                for j in range(8):
                    ps = PROJ.arrived(act, f"1qf{j}")
                    copy(m_qT[0:MLA_QK, 2 * j:2 * j + 2, :].rearrange("p a b -> p (a b)"), ps[0:MLA_QK, :],
                         scale=MLA_QK ** -0.5).then_inc(PROJ.free(f"1qf{j}"), 1)

            def attention(i):
                prob, turned_p, yT = buffers(i)[0:3]
                U = UNITS[i]
                for n in range(PAIRS * U + LAG[i] + 1):
                    if n < PAIRS * U:
                        c, u = n // U, n % U
                        for e in range(2):
                            h, name = 2 * c + e, f"{i}s{2 * c + e}_{u}"
                            slot = prob_slot(i, h, u)
                            act.wait_ge(max_ready, unit(i, h, u) + 1)
                            ps = SCORE[e].arrived(act, name)
                            for t in range(1 if u < 2 else TT):
                                part = slice(0, 512) if u < 2 else slice(t * S, t * S + S)
                                last = f(prob[:, slot, part], ps[:, part], ACT.Exp, bias=neg_max[:, slot, t:t + 1],
                                         accum_out=total[:, slot, t:t + 1])
                            last.then_inc(SCORE[e].free(name), 1)
                    if LAG[i] <= n < PAIRS * U + LAG[i]:
                        c, u = (n - LAG[i]) // U, (n - LAG[i]) % U
                        for e in range(2):
                            name = f"{i}t{2 * c + e}_{u}"
                            ps = PT.arrived(act, name)
                            keys = turned_p[2 * (c % 2) + e]
                            if u < 2:
                                o, src = keys[:, 0:4, u * P:u * P + P], ps[:, :].rearrange("p (b t) -> p b t", b=4)
                            else:
                                o, src = keys[:, 4:6, :].rearrange("p a b -> p (a b)"), ps[:, :]
                            copy(o, src).then_inc(PT.free(name), 1)
                    if n > LAG[i] and (n - LAG[i]) % U == 0:
                        c = (n - LAG[i]) // U - 1
                        ps = OT.arrived(act, f"{i}o{c}")
                        copy(yT[:, c, :], ps[:, 0:yT.shape[2]]).then_inc(OT.free(f"{i}o{c}"), 1)

            def ln_rstd(i, j, t):
                act.wait_ge(var_ready, ln_count[i, j, t])
                f(ln_rs[:, t:t + 1], ln_mv[:, t, 1:2], ACT.Sqrt, bias=eps).then_inc(ln_scale, 1)

            act.dma_start(nf_row, dram["norm_final"].partition_broadcast(P)).then_inc(gain_in, 16)
            for t in range(TT):
                link(f(nf_junk, x[:, t, :], ACT.Square, accum_out=nf_stat[:, t:t + 1]))
            f(nf_stat, nf_stat, ACT.Sqrt, scale=1.0 / D, bias=eps).then_inc(nf_scale, 1)
            act.wait_ge(mod_ready, 1)
            for i in range(DEPTH):
                n_tok = buffers(i)[3]
                for t in XT_ORDER[i] if i == 0 else XT_ORDER[i][0:TT]:
                    modulate(i, f"{i}xT{t}0", t, 0)
                if i == 1:
                    ln_rstd(0, 1, NT[0] - 1)
                (gqa_project, mla_project)[i]()
                attention(i)
                own = len(halves) // DEPTH

                def make(n):
                    if n < own:
                        X.make_high(nc, act, own * i + n)

                for n in range(3):
                    make(n)
                for t in range(NT[i] + 1):
                    if t < NT[i]:
                        ln_rstd(i, 0, t)
                    if t >= 1:
                        modulate(i, f"{i}hT{t - 1}0", t - 1, 3, hT_high)
                per = UP_PER[i]
                for q in range(QUARTERS):
                    for n in range(KD // per):
                        name = f"{i}up{q}_{n}"
                        ps = PROJ.arrived(act, name)
                        part = hidden[:, n * per:(n + 1) * per, 0:n_tok]
                        f(part, ps[:, :].rearrange("p (a b) -> p a b", a=per), ACT.Relu).then_inc(PROJ.free(name), 1)
                        PROJ.taken(act, name)
                        link(f(hidden_high[:, n * per:(n + 1) * per, 0:n_tok], part, ACT.Square))
                        f(part, part, ACT.Square).then_inc(hidden_squared, 1)
                        for s in range(NT[i] // TT):
                            if q == 0 and n == GM_AT[s]:
                                take_gate(i, "gm", s)
                        if (n + 1) * per % 2 == 0:
                            make(8 * q + (n + 1) * per // 2 + 2)
                    for n in range(4):
                        make(8 * q + 4 + n + 3)
                for t in range(NT[i] - 1 if i == 0 else NT[i]):
                    ln_rstd(i, 1, t)

        @block.vector
        def _(dve):
            link = Chain(dve, dve_self)
            vec = nc.vector

            def widen(i, kind, s):
                part = {"ga": 2, "gm": 5}[kind]
                at = (i * MOD_PARTS + part) * KD * 2
                src = mod[:, at:at + 2 * KD].rearrange("p (k s) -> p k s", s=2)[:, :, s:s + 1]
                if gate_count[i, kind, s] > 1:
                    i0, kind0, s0 = gate_order[gate_count[i, kind, s] - 2]
                    PROJ.taken(dve, *gate_fills(i0, kind0, s0))
                vec.tensor_copy(gate_src, src.to_broadcast([P, KD, P])).then_inc(gate_wide, 1)
                dve.wait_ge(gate_wide, gate_count[i, kind, s])

            def modulate(i, name, t, part, high=None):
                ps = PROJ.arrived(dve, name)
                for k in range(4):
                    if high is not None:
                        vec.tensor_scalar(high[:, 4 + k, t * P:t * P + P], ps[:, k * P:k * P + P],
                                          mod_col(i, part + 1, 4 + k, t // TT), mod_col(i, part, 4 + k, t // TT),
                                          ALU.mult, ALU.add)
                    last = vec.tensor_scalar(hT[:, 4 + k, t * P:t * P + P], ps[:, k * P:k * P + P],
                                             mod_col(i, part + 1, 4 + k, t // TT), mod_col(i, part, 4 + k, t // TT),
                                             ALU.mult, ALU.add)
                last.then_inc(PROJ.free(name), 1)

            def residual(t, h, banks, name, keep=ALPHA):
                ps = banks.arrived(dve, name)
                half = slice(512 * h, 512 * h + 512)
                vec.tensor_tensor(z[:, h, :], ps[:, :], gate_rows[:, t // TT, half], ALU.mult).then_inc(banks.free(name), 1)
                banks.taken(dve, name)
                link(vec.scalar_tensor_tensor(tok[t][:, half], tok[t][:, half], keep, z[:, h, :], ALU.mult, ALU.add))

            def layer_norm(i, j, t):
                n, xt = ln_count[i, j, t], tok[t]
                for h in range(2):
                    link(vec.bn_stats(ln_stats[:, t, h, :], xt[:, 512 * h:512 * h + 512]))
                vec.bn_aggr(ln_mv[:, t, :], ln_stats[:, t]).then_inc(var_ready, 1)
                dve.wait_ge(var_ready, n)
                if i + j > 0:
                    dve.wait_ge(ln_in, 32 * (2 * i + j))
                link(vec.scalar_tensor_tensor(xt, xt, ln_mv[:, t, 0:1], ln_rows[:, 0, :], ALU.subtract, ALU.mult))
                dve.wait_ge(ln_scale, n)
                link(vec.reciprocal(ln_rs[:, t:t + 1], ln_rs[:, t:t + 1]))
                vec.scalar_tensor_tensor(xt, xt, ln_rs[:, t:t + 1], ln_rows[:, 1, :], ALU.mult, ALU.add).then_inc(x_ready, 1)

            def rotate(part, name, rows, sin_of, cos_of, tmp, rt):
                ps = PT.arrived(dve, name)
                vec.tensor_tensor(tmp, rt(ps), sin_of, ALU.mult).then_inc(PT.free(name), 1)
                link(vec.tensor_tensor(part, part, cos_of, ALU.mult))
                PT.taken(dve, name)
                return vec.tensor_tensor(part, part, tmp, ALU.add)

            def gqa_project():
                dve.wait_ge(first_in, 3 * 16)
                for n in range(NORMED + 1):
                    if n < NORMED:
                        raw = g_k[:, n] if n < 2 else g_qT[:, n - 2]
                        gain = cols2[:, ROW_KN:ROW_KN + 1] if n < 2 else cols2[:, ROW_QN:ROW_QN + 1]
                        dve.wait_ge(rs_ready, n + 1)
                        vec.scalar_tensor_tensor(raw, raw, gain, g_rs[:, n % 2], ALU.mult, ALU.mult).then_inc(normed, 1)
                    if n >= 1:
                        raw = g_k[:, n - 1] if n < 3 else g_qT[:, n - 3]
                        dve.wait_ge(normed, n)
                        if n >= 2:
                            dve.wait_ge(roped, n - 1)
                        rotate(raw[:, 0:S], f"0rt{n - 1}", None, grid_sin, grid_cos, g_rot, lambda ps: ps[:, 0:S])\
                            .then_inc(roped, 1)

            def mla_project():
                vec.memset(m_kpe[0:HD, :], 0.0).then_inc(kpe_zero, 1)
                pe_rows = slice(HD, MLA_QK)
                dve.wait_ge(rs_ready, NORMED + 1)
                for c in range(2):
                    last = vec.scalar_tensor_tensor(m_ckv[:, c, :], m_ckv[:, c, :], cols2[:, ROW_MKN + c:ROW_MKN + c + 1],
                                                    m_rskv, ALU.mult, ALU.mult)
                last.then_inc(normed, 1)
                dve.wait_ge(rs_ready, NORMED + 2)
                for c in range(3):
                    last = vec.scalar_tensor_tensor(m_cq[:, c, :], m_cq[:, c, :], cols2[:, ROW_MQN + c:ROW_MQN + c + 1],
                                                    m_rsq, ALU.mult, ALU.mult)
                last.then_inc(normed, 1)
                dve.wait_ge(grid_in, 16)
                rotate(m_kpe[pe_rows, 0:S], "1rtk", None, grid_sin[pe_rows, :], grid_cos[pe_rows, :], m_rot[pe_rows, 0:S],
                       lambda ps: ps[pe_rows, 0:S]).then_inc(kpe_ready, 1)
                dve.wait_ge(kpe_ready, 1)
                for j in range(1, 8, 2):
                    ps = PROJ.arrived(dve, f"1kn{j}")
                    vec.tensor_copy(m_kT[0:HD, 2 * j, :], ps[0:HD, :])
                    vec.tensor_copy(m_kT[0:HD, 2 * j + 1, :], ps[HD:P, :]).then_inc(PROJ.free(f"1kn{j}"), 1)
                for j in range(1, 8, 2):
                    ps = PROJ.arrived(dve, f"1v{j}")
                    vec.tensor_copy(m_v[:, j // 2, 512:1024], ps[:, :]).then_inc(PROJ.free(f"1v{j}"), 1)
                wide = lambda a: a[pe_rows, :].unsqueeze(1).to_broadcast([PE_DIM, 2, S])
                for j in range(8):
                    if j >= 1:
                        dve.wait_ge(roped, NORMED + j)
                    rotate(m_qT[pe_rows, 2 * j:2 * j + 2, :], f"1rt{j}", None, wide(grid_sin), wide(grid_cos),
                           m_rot[pe_rows, :].rearrange("p (a b) -> p a b", a=2),
                           lambda ps: ps[pe_rows, :].rearrange("p (a b) -> p a b", a=2)).then_inc(roped, 1)

            def attention(i):
                prob, U = buffers(i)[0], UNITS[i]
                order = [(2 * c + e, u) for c in range(PAIRS) for u in range(U) for e in range(2)]
                for n in range(len(order) + 1):
                    if n < len(order):
                        h, u = order[n]
                        slot = prob_slot(i, h, u)
                        ps = SCORE[h % 2].arrived(dve, f"{i}s{h}_{u}")
                        if u < 2:
                            last = vec.tensor_reduce(neg_max[:, slot, 0:1], ps[:, :], axis=AX.X, op=ALU.max, negate=True)
                        else:
                            last = vec.tensor_reduce(neg_max[:, slot, :], ps[:, :].rearrange("p (t k) -> p t k", t=TT),
                                                     axis=AX.X, op=ALU.max, negate=True)
                        last.then_inc(max_ready, 1)
                    if n >= 1:
                        h, u = order[n - 1]
                        slot = prob_slot(i, h, u)
                        tiles_of = 1 if u < 2 else TT
                        SCORE[h % 2].taken(dve, f"{i}s{h}_{u}")
                        link(vec.reciprocal(total[:, slot, 0:tiles_of], total[:, slot, 0:tiles_of]))
                        for t in range(tiles_of):
                            part = slice(0, 512) if u < 2 else slice(t * S, t * S + S)
                            last = vec.tensor_scalar(prob[:, slot, part], prob[:, slot, part], total[:, slot, t:t + 1],
                                                     None, ALU.mult)
                        last.then_inc(prob_ready, 1)

            every = mod[:, :].rearrange("p (n s) -> p n s", s=2)
            link(vec.tensor_tensor(every, every, cols2[:, ROW_ADA:ROW_ADA + DEPTH * MODC].unsqueeze(2)
                                   .to_broadcast([P, DEPTH * MODC, 2]), ALU.add))
            scales = mod[:, :].rearrange("p (l m n) -> p l m n", l=2 * DEPTH, m=3)[:, :, 1, :]
            vec.tensor_scalar_add(scales, scales, 1.0).then_inc(mod_ready, 1)
            dve.wait_ge(mod_ready, 1)
            link(vec.tensor_scalar(cols2[:, ROW_QN:ROW_QN + 1], cols2[:, ROW_QN:ROW_QN + 1], HD ** -0.5, None, ALU.mult))
            widen(0, "ga", 0)
            dve.wait_ge(gain_in, 16)
            dve.wait_ge(nf_scale, 1)
            link(vec.reciprocal(nf_stat, nf_stat))
            for t in range(TT):
                vec.scalar_tensor_tensor(x[:, t, :], x[:, t, :], nf_stat[:, t:t + 1], nf_row, ALU.mult, ALU.mult)\
                    .then_inc(x_first, 1)
            for i in range(DEPTH):
                n_tok = buffers(i)[3]
                if i == 1:
                    widen(1, "ga", 0)
                for t in XT_ORDER[i]:
                    if i == 1 and t == TT:
                        layer_norm(0, 1, NT[0] - 1)
                    modulate(i, f"{i}xT{t}1", t, 0)
                if i == 0:
                    widen(0, "ga", 1)
                (gqa_project, mla_project)[i]()
                attention(i)
                own = len(halves) // DEPTH

                def make(n):
                    if n < own:
                        X.make_low(nc, dve, own * i + n)

                for n in range(3):
                    make(n)
                PROJ.taken(dve, *gate_fills(i, "ga", NT[i] // TT - 1))
                for t in range(NT[i] + 1):
                    if t < NT[i]:
                        for h in range(2):
                            residual(t, h, OT, f"{i}wo{t}{h}")
                        layer_norm(i, 0, t)
                    if t >= 1:
                        modulate(i, f"{i}hT{t - 1}1", t - 1, 3, hT_high)
                        PROJ.taken(dve, f"{i}hT{t - 1}0", f"{i}hT{t - 1}1")
                        part = slice((t - 1) * P, t * P)
                        vec.tensor_tensor(hT_low[:, :, part], hT[:, :, part], hT_high[:, :, part].bitcast(F32), ALU.subtract)\
                            .then_inc(hT_cut, 1)
                widen(i, "gm", 0)
                per = UP_PER[i]
                for q in range(QUARTERS):
                    for n in range(KD // per):
                        dve.wait_ge(hidden_squared, up_base[i] + (q * KD) // per + n + 1)
                        part = slice(n * per, (n + 1) * per)
                        vec.tensor_tensor(hidden_low[:, part, 0:n_tok], hidden[:, part, 0:n_tok],
                                          hidden_high[:, part, 0:n_tok].bitcast(F32), ALU.subtract).then_inc(hidden_ready, 1)
                        if q == 0 and n == GM_AT[0] and NT[i] > TT:
                            widen(i, "gm", 1)
                        if (n + 1) * per % 2 == 0:
                            make(8 * q + (n + 1) * per // 2 + 2)
                    if q == 0:
                        PROJ.taken(dve, *gate_fills(i, "gm", NT[i] // TT - 1))
                    for h in range(2):
                        make(8 * q + 4 + 2 * h + 3)
                        for t in range(NT[i]):
                            residual(t, h, down_banks(h, t), f"{i}down{q}{h}{t}", ALPHA if q == 0 else 1.0)
                            if q == QUARTERS - 1 and h == 1 and (i, t) != (0, NT[0] - 1):
                                layer_norm(i, 1, t)
                        make(8 * q + 5 + 2 * h + 3)

        @block.gpsimd
        def _(pool):
            for n in range(2):
                pool.wait_ge(roped, n + 1)
                for a in range(2):
                    for half in range(2):
                        nc.gpsimd.tensor_copy(g_kT[half * HD:half * HD + HD, 2 * n + a, :], g_k[a * HD:a * HD + HD, n, :])\
                            .then_inc(k_copied, 1)
            pool.wait_ge(roped, NORMED)
            pool.dma_start(grid, dram["grid_mla"]).then_inc(grid_in, 16)

            def norm_rows(i, j, after):
                pool.wait_ge(x_ready, after)
                for n, name in enumerate(("ln_g_2", "ln_b_2")):
                    pool.dma_start(ln_rows[:, n, :], dram[name][i, j].partition_broadcast(P)).then_inc(ln_in, 16)

            norm_rows(0, 1, ln_count[0, 0, NT[0] - 1])
            norm_rows(1, 0, ln_count[0, 1, NT[0] - 1])
            pool.wait_ge(kpe_ready, 1)
            for n in range(4):
                nc.gpsimd.tensor_copy(m_kT[HD:MLA_QK, 4 * n:4 * n + 4, :],
                                      m_kpe[HD:MLA_QK, :].unsqueeze(1).to_broadcast([PE_DIM, 4, 2 * S])).then_inc(k_copied, 1)
            norm_rows(1, 1, ln_count[1, 0, NT[1] - 1])


def build(nc, T, dram, out):
    with ExitStack() as ctx:
        def sb(name, shape, dt=F32):
            return ctx.enter_context(nc.sbuf_tensor(name, shape, dt))

        names = []

        def sem(name):
            names.append(name)
            return ctx.enter_context(nc.semaphore(f"{name}_{len(names)}"))

        n_f32 = dram["f32_tables"].shape[1]
        n_bf16 = dram["bf16_tables"].shape[1]
        chip = {"consts": sb("consts", [P, n_f32]), "masks": sb("masks", [P, n_bf16], BF16),
                }
        at = nc.sbuf_base
        chip["ring"] = sb("ring", [P, N_SLOTS, SLOT])
        chip["ring_low"] = [nc.alloc_sbuf_tensor_at(f"ring_low{n}", [P, SLOT], F32R, offset=at + 4 * n * SLOT)
                            for n in range(N_SLOTS)]
        chip["ring_high"] = [nc.alloc_sbuf_tensor_at(f"ring_high{n}", [P, SLOT // 2], F32R,
                                                     offset=at + 4 * (N_SLOTS - 1) * SLOT + 2 * n * SLOT) for n in range(2)]
        at = nc.sbuf_base
        x = sb("x_sb", [P, TT, D])
        chip["hT_high"] = nc.alloc_sbuf_tensor_at("hT_high", [P, KD, S], F32R, offset=at)
        cos, sin = sb("cos", [P, S]), sb("sin", [P, S])
        chip.update(x=x[:, :, :], cos=cos[:, :], sin=sin[:, :])
        chip["mod"] = sb("mod", [P, DEPTH * 2 * MODC])
        chip["cols2"] = sb("cols2", [P, N_ROWS2])[:, :]
        chip["silu_c"] = sb("silu_c", [P, KD, THIN])[:, :, :]
        work_base = nc.sbuf_base
        chip["work"] = sb("work", [P, WORK])

        def rounded(name, at, *dims):
            n = int(np.prod(dims))
            assert at + n <= WORK, (name, at, n)
            return nc.alloc_sbuf_tensor_at(name, [P, *dims], F32R, offset=work_base + 4 * at)

        chip["rounded"] = rounded
        chip["psum"] = [ctx.enter_context(nc.psum_tensor(f"bank{i}", [P, 512], F32)) for i in range(8)]

        prologue(nc, T, dram, sem, chip)
        layer_sems = []

        def layer_sem(name):
            layer_sems.append(sem(name))
            return layer_sems[-1]

        with nc.Fori(0, DEPTH) as l:
            first_layer(nc, l, T, dram, out, layer_sem, chip)
            for s in layer_sems:
                nc.gpsimd.sem_clear(s)
            nc.all_engine_barrier()

        second_block(nc, T, dram, out, sem, chip)


_INS = ["x", "positions", "norm_mix", "w_in", "b_gate", "nsa_cmp_pos_k", "nsa_cmp_pos_v", "nsa_cmp_wk1",
        "nsa_cmp_wk2", "nsa_cmp_wv1", "nsa_cmp_wv2", "gla_w_alpha", "gla_b_alpha", "gla_norm", "fox_b_f",
        "w_branch", "w_out", "norm_ff", "w_ff1", "w_ff2", "norm_final",
        "c_2", "ctx_2", "c_ctx_2", "w_ada_2", "b_ada_2", "ln_g_2", "ln_b_2", "mlp_w1_2", "mlp_w2_2",
        "gqa_w_qkv_2", "gqa_q_norm_2", "gqa_k_norm_2", "gqa_w_o_2", "mla_w_in_2", "mla_q_norm_2",
        "mla_kv_norm_2", "mla_w_uq_2", "mla_w_ukv_2", "mla_w_o_2"]


def kernel(**inputs):
    import concourse.bacc as _bacc
    import ml_dtypes
    from concourse.bass_utils import run_bass_kernel_spmd as _run

    nc = _bacc.Bacc("TRN2", target_bir_lowering=False, num_devices=1)
    f32, bf16 = constants()
    T, arrays, dram = {}, {}, {}
    T["f32"], arrays["f32_tables"] = packed(f32, np.float32)
    T["bf16"], arrays["bf16_tables"] = packed(bf16, ml_dtypes.bfloat16)
    arrays["grid_gqa"] = grid_tables(HD, 0, HD)
    arrays["grid_mla"] = grid_tables(PE_DIM, HD, HD)
    for name in _INS:
        arrays[name] = np.ascontiguousarray(inputs[name])
    for name, a in arrays.items():
        dram[name] = nc.dram_tensor(name, a.shape, mybir.dt.from_np(a.dtype), kind="ExternalInput").ap()
    out = nc.dram_tensor("out", (1, S, D), F32, kind="ExternalOutput").ap()
    build(nc, T, dram, out)
    r = _run(nc, [arrays], core_ids=[0])
    return r.results[0]["out"]
```
